# Optimizing a Trainium2 kernel written in Bass

```python
import jax, jax.numpy as jnp
from jax import lax
import numpy as np
import math

D_MODEL = 1024
BATCH = 1
SEQ = 512
DEPTH = 2

N_EVEN = (DEPTH + 1) // 2
N_ODD = DEPTH // 2

GLA_HEADS = 4
GLA_DK = 64
GLA_DV = 128
GLA_GATE_RANK = 16
GLA_GATE_TAU = 16.0
GLA_CHUNK = 64

DSA_HEADS = 4
DSA_HEAD_DIM = 128
IDX_HEADS = 8
IDX_DIM = 64
DSA_TOPK = 256

POOL_WINDOWS = (2, 4, 8, 16)
POOL_GROUPS = 4
POOL_CH = 128

SB_HEADS = 4
SB_HEAD_DIM = 128

BLOCK_Q = 128
ROPE_THETA = 10000.0
NORM_EPS = 1e-6
D_FF = ((8 * D_MODEL + 3 * 256 - 1) // (3 * 256)) * 256

AB_SPLITS = (GLA_HEADS * GLA_DK, GLA_HEADS * GLA_DK, GLA_HEADS * GLA_DV, GLA_GATE_RANK,
             GLA_HEADS * GLA_DV,
             DSA_HEADS * DSA_HEAD_DIM, DSA_HEADS * DSA_HEAD_DIM, DSA_HEADS * DSA_HEAD_DIM,
             IDX_HEADS * IDX_DIM, IDX_DIM, IDX_HEADS)
AB_IN = sum(AB_SPLITS)
D_MIX_AB = GLA_HEADS * GLA_DV + DSA_HEADS * DSA_HEAD_DIM
CD_SPLITS = (POOL_GROUPS * POOL_CH, SB_HEADS * SB_HEAD_DIM, SB_HEADS * SB_HEAD_DIM,
             SB_HEADS * SB_HEAD_DIM)
CD_IN = sum(CD_SPLITS)
D_MIX_CD = POOL_GROUPS * POOL_CH + SB_HEADS * SB_HEAD_DIM


def split_cols(t, sizes):
    offsets = np.cumsum(sizes)[:-1].tolist()
    return jnp.split(t, offsets, axis=-1)

def rms_norm(t, w):
    tf = t.astype(jnp.float32)
    y = tf * lax.rsqrt(jnp.mean(tf * tf, axis=-1, keepdims=True) + NORM_EPS)
    return (y * w.astype(jnp.float32)).astype(t.dtype)

def modulate(h, shift, scale):
    return h * (1.0 + scale[:, None, :]) + shift[:, None, :]

def rope(t, positions):
    half = t.shape[-1] // 2
    inv_freq = ROPE_THETA ** (-jnp.arange(half, dtype=jnp.float32) / half)
    ang = positions.astype(jnp.float32)[:, :, None, None] * inv_freq
    cos, sin = jnp.cos(ang), jnp.sin(ang)
    tf = t.astype(jnp.float32)
    t1, t2 = tf[..., :half], tf[..., half:]
    return jnp.concatenate([t1 * cos - t2 * sin, t2 * cos + t1 * sin], axis=-1).astype(t.dtype)

def swiglu(h, w1, w2):
    gate, up = jnp.split(h @ w1, 2, axis=-1)
    return (jax.nn.silu(gate) * up) @ w2

def gla_chunked(q, k, v, log_a):
    B, S, H, DK = q.shape
    DV = v.shape[-1]
    C = GLA_CHUNK
    N = S // C

    def chunks(t):
        return t.astype(jnp.float32).reshape(B, N, C, H, t.shape[-1]).transpose(0, 3, 1, 2, 4)

    q, k, v, g = chunks(q), chunks(k), chunks(v), chunks(log_a)
    q = q * (DK ** -0.5)
    b = jnp.cumsum(g, axis=3)
    b_mid = b[:, :, :, C // 2 - 1:C // 2, :]
    att = jnp.einsum('bhnid,bhnjd->bhnij', q * jnp.exp(b - b_mid), k * jnp.exp(b_mid - b))
    causal = jnp.tril(jnp.ones((C, C), dtype=bool))
    att = jnp.where(causal, att, 0.0)
    o_intra = jnp.einsum('bhnij,bhnjv->bhniv', att, v)
    b_last = b[:, :, :, -1:, :]
    k_dec = k * jnp.exp(b_last - b)
    q_dec = q * jnp.exp(b)
    decay = jnp.exp(b_last[:, :, :, 0, :])
    kv = jnp.einsum('bhncd,bhncv->bhndv', k_dec, v)

    def step(state, inp):
        dec, kv_n = inp
        return dec[..., None] * state + kv_n, state

    init = jnp.zeros((B, H, DK, DV), jnp.float32)
    _, prev = lax.scan(step, init, (jnp.moveaxis(decay, 2, 0), jnp.moveaxis(kv, 2, 0)))
    prev = jnp.moveaxis(prev, 0, 2)
    o_inter = jnp.einsum('bhncd,bhndv->bhncv', q_dec, prev)
    o = o_intra + o_inter
    return o.transpose(0, 2, 3, 1, 4).reshape(B, S, H, DV)

def dsa_attention(q, k, v, iq, ik, iw, n_sel):
    B, S, H, Dh = q.shape
    bidx = jnp.arange(B)[:, None, None]
    key_pos = jnp.arange(S)
    idx_scale = (IDX_HEADS ** -0.5) * (IDX_DIM ** -0.5)
    att_scale = Dh ** -0.5

    def block(i):
        t0 = i * BLOCK_Q
        tpos = t0 + jnp.arange(BLOCK_Q)
        qb = lax.dynamic_slice_in_dim(q, t0, BLOCK_Q, axis=1)
        iqb = lax.dynamic_slice_in_dim(iq, t0, BLOCK_Q, axis=1)
        iwb = lax.dynamic_slice_in_dim(iw, t0, BLOCK_Q, axis=1)
        rel = jax.nn.relu(jnp.einsum('bqhd,bsd->bqhs', iqb, ik).astype(jnp.float32))
        score = jnp.einsum('bqhs,bqh->bqs', rel, iwb.astype(jnp.float32)) * idx_scale
        causal = key_pos[None, :] <= tpos[:, None]
        score = jnp.where(causal[None], score, -jnp.inf)
        _, sel = lax.top_k(score, n_sel)
        kg = k[bidx, sel]
        vg = v[bidx, sel]
        logits = jnp.einsum('bqhd,bqkhd->bhqk', qb, kg).astype(jnp.float32) * att_scale
        valid = (sel <= tpos[None, :, None])[:, None]
        logits = jnp.where(valid, logits, -jnp.inf)
        p = jax.nn.softmax(logits, axis=-1).astype(v.dtype)
        return jnp.einsum('bhqk,bqkhd->bqhd', p, vg)

    out = lax.map(block, jnp.arange(S // BLOCK_Q))
    return jnp.moveaxis(out, 0, 1).reshape(B, S, H, Dh)

def stick_breaking_attention(q, k, v):
    B, S, H, Dh = q.shape
    key_pos = jnp.arange(S)
    scale = Dh ** -0.5

    def block(i):
        t0 = i * BLOCK_Q
        tpos = t0 + jnp.arange(BLOCK_Q)
        qb = lax.dynamic_slice_in_dim(q, t0, BLOCK_Q, axis=1)
        z = jnp.einsum('bqhd,bshd->bhqs', qb, k).astype(jnp.float32) * scale
        strict = (key_pos[None, :] < tpos[:, None])[None, None]
        log_beta = jax.nn.log_sigmoid(z)
        log_1m = jnp.where(strict, jax.nn.log_sigmoid(-z), 0.0)
        after = lax.cumsum(log_1m, axis=3, reverse=True) - log_1m
        w = jnp.where(strict, jnp.exp(log_beta + after), 0.0)
        return jnp.einsum('bhqs,bshd->bqhd', w.astype(v.dtype), v)

    out = lax.map(block, jnp.arange(S // BLOCK_Q))
    return jnp.moveaxis(out, 0, 1).reshape(B, S, H, Dh)

def multiscale_pool(u, pool_w, pool_scale):
    B, S, _ = u.shape
    ug = u.astype(jnp.float32).reshape(B, S, POOL_GROUPS, POOL_CH)
    cs = jnp.cumsum(ug, axis=1)
    cs0 = jnp.concatenate([jnp.zeros((B, 1, POOL_GROUPS, POOL_CH), jnp.float32), cs], axis=1)
    t = jnp.arange(S, dtype=jnp.float32)
    pooled = []
    for g, w in enumerate(POOL_WINDOWS):
        lo = jnp.pad(cs0[:, :S + 1 - w, g], ((0, 0), (w - 1, 0), (0, 0)))
        count = jnp.minimum(t + 1.0, float(w))[None, :, None]
        pooled.append((cs[:, :, g] - lo) / count - ug[:, :, g])
    pooled = jnp.stack(pooled, axis=2)
    y = jnp.einsum('bsgc,gcd->bsgd', pooled, pool_w.astype(jnp.float32))
    y = y * pool_scale.astype(jnp.float32).reshape(POOL_GROUPS, POOL_CH)
    return y.reshape(B, S, POOL_GROUPS * POOL_CH).astype(u.dtype)

def ab_mixer(h, positions, w_in, gate_up, gate_b, out_norm, q_norm, k_norm, w_out):
    B, S, _ = h.shape
    (gq, gk, gv, glow, gr, dq, dk, dv, iq, ik, iw) = split_cols(h @ w_in, AB_SPLITS)
    log_a = jax.nn.log_sigmoid((glow @ gate_up + gate_b).astype(jnp.float32)) / GLA_GATE_TAU
    o_gla = gla_chunked(gq.reshape(B, S, GLA_HEADS, GLA_DK), gk.reshape(B, S, GLA_HEADS, GLA_DK),
                        gv.reshape(B, S, GLA_HEADS, GLA_DV), log_a.reshape(B, S, GLA_HEADS, GLA_DK))
    o_gla = rms_norm(o_gla.astype(h.dtype), out_norm) * jax.nn.silu(gr.reshape(B, S, GLA_HEADS, GLA_DV))
    q = rope(rms_norm(dq.reshape(B, S, DSA_HEADS, DSA_HEAD_DIM), q_norm), positions)
    k = rope(rms_norm(dk.reshape(B, S, DSA_HEADS, DSA_HEAD_DIM), k_norm), positions)
    v = dv.reshape(B, S, DSA_HEADS, DSA_HEAD_DIM)
    iq = rope(iq.reshape(B, S, IDX_HEADS, IDX_DIM), positions)
    ik = rope(ik[:, :, None, :], positions)[:, :, 0, :]
    n_sel = min(DSA_TOPK, S // 4)
    o_dsa = dsa_attention(q, k, v, iq, ik, iw, n_sel)
    mix = jnp.concatenate([o_gla.reshape(B, S, -1), o_dsa.reshape(B, S, -1)], axis=-1)
    return mix @ w_out

def cd_mixer(h, w_in, pool_w, pool_scale, q_norm, k_norm, w_out):
    B, S, _ = h.shape
    u, sq, sk, sv = split_cols(h @ w_in, CD_SPLITS)
    o_pool = multiscale_pool(u, pool_w, pool_scale)
    q = rms_norm(sq.reshape(B, S, SB_HEADS, SB_HEAD_DIM), q_norm)
    k = rms_norm(sk.reshape(B, S, SB_HEADS, SB_HEAD_DIM), k_norm)
    v = sv.reshape(B, S, SB_HEADS, SB_HEAD_DIM)
    o_sb = stick_breaking_attention(q, k, v)
    mix = jnp.concatenate([o_pool, o_sb.reshape(B, S, -1)], axis=-1)
    return mix @ w_out

def first_inputs(seed: int = 0) -> dict:
    key = jax.random.key(seed)
    ks = jax.random.split(key, 24)
    f32 = jnp.float32

    def nrm(k, shape, scale):
        return jax.random.normal(k, shape, f32) * scale

    def gain(k, shape):
        return 1.0 + 0.1 * jax.random.normal(k, shape, f32)

    x = nrm(ks[0], (BATCH, SEQ, D_MODEL), 1.0)
    c = nrm(ks[1], (BATCH, D_MODEL), 1.0)
    positions = (jnp.arange(SEQ, dtype=jnp.int32)[None, :]
                 + jax.random.randint(ks[2], (BATCH, 1), 0, 4096, dtype=jnp.int32))
    return {
        "x": x,
        "c": c,
        "positions": positions,
        "ada_w": nrm(ks[3], (DEPTH, D_MODEL, 6 * D_MODEL), 0.5 * D_MODEL ** -0.5),
        "ada_b": nrm(ks[4], (DEPTH, 6 * D_MODEL), 0.01),
        "mix_norm": gain(ks[5], (DEPTH, D_MODEL)),
        "ffn_norm": gain(ks[6], (DEPTH, D_MODEL)),
        "ffn_w1": nrm(ks[7], (DEPTH, D_MODEL, 2 * D_FF), D_MODEL ** -0.5),
        "ffn_w2": nrm(ks[8], (DEPTH, D_FF, D_MODEL), D_FF ** -0.5),
        "ab_w_in": nrm(ks[9], (N_EVEN, D_MODEL, AB_IN), D_MODEL ** -0.5),
        "gla_gate_up": nrm(ks[10], (N_EVEN, GLA_GATE_RANK, GLA_HEADS * GLA_DK), GLA_GATE_RANK ** -0.5),
        "gla_gate_b": nrm(ks[11], (N_EVEN, GLA_HEADS * GLA_DK), 0.01),
        "gla_out_norm": gain(ks[12], (N_EVEN, GLA_DV)),
        "dsa_q_norm": gain(ks[13], (N_EVEN, DSA_HEAD_DIM)),
        "dsa_k_norm": gain(ks[14], (N_EVEN, DSA_HEAD_DIM)),
        "ab_w_out": nrm(ks[15], (N_EVEN, D_MIX_AB, D_MODEL), D_MIX_AB ** -0.5),
        "cd_w_in": nrm(ks[16], (N_ODD, D_MODEL, CD_IN), D_MODEL ** -0.5),
        "pool_w": nrm(ks[17], (N_ODD, POOL_GROUPS, POOL_CH, POOL_CH), POOL_CH ** -0.5),
        "pool_scale": gain(ks[18], (N_ODD, POOL_GROUPS * POOL_CH)),
        "sb_q_norm": gain(ks[19], (N_ODD, SB_HEAD_DIM)),
        "sb_k_norm": gain(ks[20], (N_ODD, SB_HEAD_DIM)),
        "cd_w_out": nrm(ks[21], (N_ODD, D_MIX_CD, D_MODEL), D_MIX_CD ** -0.5),
    }

def first_block(x, c, positions, ada_w, ada_b, mix_norm, ffn_norm, ffn_w1, ffn_w2,
              ab_w_in, gla_gate_up, gla_gate_b, gla_out_norm, dsa_q_norm, dsa_k_norm, ab_w_out,
              cd_w_in, pool_w, pool_scale, sb_q_norm, sb_k_norm, cd_w_out):
    cond = jax.nn.silu(c)
    for layer in range(DEPTH):
        mod = cond @ ada_w[layer] + ada_b[layer]
        sh1, sc1, g1, sh2, sc2, g2 = jnp.split(mod, 6, axis=-1)
        h = modulate(rms_norm(x, mix_norm[layer]), sh1, sc1)
        if layer % 2 == 0:
            i = layer // 2
            y = ab_mixer(h, positions, ab_w_in[i], gla_gate_up[i], gla_gate_b[i], gla_out_norm[i],
                         dsa_q_norm[i], dsa_k_norm[i], ab_w_out[i])
        else:
            i = layer // 2
            y = cd_mixer(h, cd_w_in[i], pool_w[i], pool_scale[i], sb_q_norm[i], sb_k_norm[i],
                         cd_w_out[i])
        x = x + g1[:, None, :] * y
        h = modulate(rms_norm(x, ffn_norm[layer]), sh2, sc2)
        x = x + g2[:, None, :] * swiglu(h, ffn_w1[layer], ffn_w2[layer])
    return x


N_MIXERS = 2
N_MLSTM_LAYERS = (DEPTH + 1) // 2
N_CONV_LAYERS = DEPTH // 2

M_HEADS = 4
M_DV = D_MODEL // M_HEADS
M_DQK = M_DV // 2
M_QK_WIDTH = 2 * M_HEADS * M_DQK
M_V_WIDTH = M_HEADS * M_DV
M_IN_WIDTH = M_QK_WIDTH + M_V_WIDTH + M_V_WIDTH + 2 * M_HEADS
M_CONV_K = 4
M_CHUNK = 64
FGATE_BIAS = 3.0

C_KERNEL = 31

D_FF_2 = 2816
F_CONV_K = 3

EPS = 1e-6


def rmsnorm(x, g):
    xf = x.astype(jnp.float32)
    y = xf * lax.rsqrt(jnp.mean(xf * xf, axis=-1, keepdims=True) + EPS)
    return (y * g.astype(jnp.float32)).astype(x.dtype)

def layernorm(x, g, b):
    xf = x.astype(jnp.float32)
    mu = jnp.mean(xf, axis=-1, keepdims=True)
    var = jnp.mean(jnp.square(xf - mu), axis=-1, keepdims=True)
    y = (xf - mu) * lax.rsqrt(var + EPS)
    return (y * g.astype(jnp.float32) + b.astype(jnp.float32)).astype(x.dtype)

def causal_dwconv(x, w, b):
    k, c = w.shape
    y = lax.conv_general_dilated(
        x, w[:, None, :].astype(x.dtype), window_strides=(1,), padding=[(k - 1, 0)],
        dimension_numbers=("NWC", "WIO", "NWC"), feature_group_count=c)
    return y + b.astype(x.dtype)

def mlstm_chunkwise(q, k, v, logi, logf):
    bsz, nh, t, dk = q.shape
    dv = v.shape[-1]
    nc = t // M_CHUNK

    def chunks(a):
        a = a.reshape(a.shape[:2] + (nc, M_CHUNK) + a.shape[3:])
        return jnp.moveaxis(a, 2, 0)

    qc, kc, vc = chunks(q), chunks(k), chunks(v)
    lic = chunks(logi)
    bc = jnp.cumsum(chunks(logf), axis=-1)
    causal = jnp.tril(jnp.ones((M_CHUNK, M_CHUNK), dtype=bool))

    def step(carry, inp):
        c_st, n_st, m_st = carry
        qb, kb, vb, li, bb = inp
        d = bb[..., :, None] - bb[..., None, :] + li[..., None, :]
        d = jnp.where(causal, d, -jnp.inf)
        inter = bb + m_st[..., None]
        m_t = jnp.maximum(inter, jnp.max(d, axis=-1))
        s = jnp.einsum("bhtd,bhsd->bhts", qb, kb) * jnp.exp(d - m_t[..., None])
        sc = jnp.exp(inter - m_t)
        num = jnp.einsum("bhts,bhsv->bhtv", s, vb) + sc[..., None] * jnp.einsum("bhvd,bhtd->bhtv", c_st, qb)
        den = jnp.sum(s, axis=-1) + sc * jnp.einsum("bhd,bhtd->bht", n_st, qb)
        h = num / jnp.maximum(jnp.abs(den), jnp.exp(-m_t))[..., None]
        b_last = bb[..., -1]
        w_log = b_last[..., None] - bb + li
        m_new = jnp.maximum(b_last + m_st, jnp.max(w_log, axis=-1))
        decay = jnp.exp(b_last + m_st - m_new)
        ws = jnp.exp(w_log - m_new[..., None])
        c_new = decay[..., None, None] * c_st + jnp.einsum("bhs,bhsv,bhsd->bhvd", ws, vb, kb)
        n_new = decay[..., None] * n_st + jnp.einsum("bhs,bhsd->bhd", ws, kb)
        return (c_new, n_new, m_new), h

    init = (jnp.zeros((bsz, nh, dv, dk), jnp.float32),
            jnp.zeros((bsz, nh, dk), jnp.float32),
            jnp.zeros((bsz, nh), jnp.float32))
    _, hs = lax.scan(step, init, (qc, kc, vc, lic, bc))
    return jnp.moveaxis(hs, 0, 2).reshape(bsz, nh, t, dv)

def mlstm_mixer(x, w_in, conv_w, conv_b, b_gates, head_norm, w_out):
    bsz, t, _ = x.shape
    proj = x @ w_in
    qk = jax.nn.silu(causal_dwconv(proj[..., :M_QK_WIDTH], conv_w, conv_b))
    v = proj[..., M_QK_WIDTH:M_QK_WIDTH + M_V_WIDTH]
    o = proj[..., M_QK_WIDTH + M_V_WIDTH:M_QK_WIDTH + 2 * M_V_WIDTH]
    gates = (proj[..., M_QK_WIDTH + 2 * M_V_WIDTH:] + b_gates).astype(jnp.float32)
    logi = jnp.transpose(gates[..., :M_HEADS], (0, 2, 1))
    logf = jnp.transpose(jax.nn.log_sigmoid(gates[..., M_HEADS:]), (0, 2, 1))

    def heads(a, d):
        return jnp.transpose(a.reshape(bsz, t, M_HEADS, d), (0, 2, 1, 3)).astype(jnp.float32)

    q = heads(qk[..., :M_HEADS * M_DQK], M_DQK) * (M_DQK ** -0.5)
    k = heads(qk[..., M_HEADS * M_DQK:], M_DQK)
    h = mlstm_chunkwise(q, k, heads(v, M_DV), logi, logf)
    h = jnp.transpose(h, (0, 2, 1, 3))
    h = h * lax.rsqrt(jnp.mean(h * h, axis=-1, keepdims=True) + EPS)
    h = h.reshape(bsz, t, M_V_WIDTH) * head_norm.astype(jnp.float32)
    h = h.astype(x.dtype) * jax.nn.sigmoid(o)
    return h @ w_out

def conformer_conv_mixer(x, w_in, b_in, dw_w, dw_b, ln_g, ln_b, w_out, b_out):
    a = x @ w_in + b_in
    u = a[..., :D_MODEL] * jax.nn.sigmoid(a[..., D_MODEL:])
    u = causal_dwconv(u, dw_w, dw_b)
    u = jax.nn.silu(layernorm(u, ln_g, ln_b))
    return u @ w_out + b_out

def conv_ffn(x, w_up, conv_w, conv_b, w_down):
    hdn = causal_dwconv(x @ w_up, conv_w, conv_b)
    return (jax.nn.silu(hdn[..., :D_FF_2]) * hdn[..., D_FF_2:]) @ w_down

def second_inputs(seed: int = 0) -> dict:
    key = jax.random.key(seed)
    ks = iter(jax.random.split(key, 32))
    f32 = jnp.float32
    nrm = lambda shape, s: jax.random.normal(next(ks), shape, f32) * s
    out_scale = 1.0 / math.sqrt(2 * DEPTH)
    nm, ncv = N_MLSTM_LAYERS, N_CONV_LAYERS
    gate_bias = jnp.concatenate([jnp.zeros((nm, M_HEADS), f32), jnp.full((nm, M_HEADS), FGATE_BIAS, f32)], axis=-1)
    return {
        "x": nrm((BATCH, SEQ, D_MODEL), 1.0),
        "norm_mix": 1.0 + nrm((DEPTH, D_MODEL), 0.02),
        "norm_ffn": 1.0 + nrm((DEPTH, D_MODEL), 0.02),
        "norm_final": 1.0 + nrm((D_MODEL,), 0.02),
        "m_w_in": nrm((nm, D_MODEL, M_IN_WIDTH), D_MODEL ** -0.5),
        "m_conv_w": nrm((nm, M_CONV_K, M_QK_WIDTH), M_CONV_K ** -0.5),
        "m_conv_b": nrm((nm, M_QK_WIDTH), 0.02),
        "m_b_gates": gate_bias + nrm((nm, 2 * M_HEADS), 0.1),
        "m_head_norm": 1.0 + nrm((nm, M_V_WIDTH), 0.02),
        "m_w_out": nrm((nm, M_V_WIDTH, D_MODEL), M_V_WIDTH ** -0.5 * out_scale),
        "c_w_in": nrm((ncv, D_MODEL, 2 * D_MODEL), D_MODEL ** -0.5),
        "c_b_in": nrm((ncv, 2 * D_MODEL), 0.02),
        "c_dw_w": nrm((ncv, C_KERNEL, D_MODEL), C_KERNEL ** -0.5),
        "c_dw_b": nrm((ncv, D_MODEL), 0.02),
        "c_ln_g": 1.0 + nrm((ncv, D_MODEL), 0.02),
        "c_ln_b": nrm((ncv, D_MODEL), 0.02),
        "c_w_out": nrm((ncv, D_MODEL, D_MODEL), D_MODEL ** -0.5 * out_scale),
        "c_b_out": nrm((ncv, D_MODEL), 0.02),
        "f_w_up": nrm((DEPTH, D_MODEL, 2 * D_FF_2), D_MODEL ** -0.5),
        "f_conv_w": nrm((DEPTH, F_CONV_K, 2 * D_FF_2), F_CONV_K ** -0.5),
        "f_conv_b": nrm((DEPTH, 2 * D_FF_2), 0.02),
        "f_w_down": nrm((DEPTH, D_FF_2, D_MODEL), D_FF_2 ** -0.5 * out_scale),
    }

def second_block(x, norm_mix, norm_ffn, norm_final,
              m_w_in, m_conv_w, m_conv_b, m_b_gates, m_head_norm, m_w_out,
              c_w_in, c_b_in, c_dw_w, c_dw_b, c_ln_g, c_ln_b, c_w_out, c_b_out,
              f_w_up, f_conv_w, f_conv_b, f_w_down):
    for i in range(DEPTH):
        h = rmsnorm(x, norm_mix[i])
        j = i // N_MIXERS
        if i % N_MIXERS == 0:
            x = x + mlstm_mixer(h, m_w_in[j], m_conv_w[j], m_conv_b[j], m_b_gates[j],
                                m_head_norm[j], m_w_out[j])
        else:
            x = x + conformer_conv_mixer(h, c_w_in[j], c_b_in[j], c_dw_w[j], c_dw_b[j],
                                         c_ln_g[j], c_ln_b[j], c_w_out[j], c_b_out[j])
        x = x + conv_ffn(rmsnorm(x, norm_ffn[i]), f_w_up[i], f_conv_w[i], f_conv_b[i], f_w_down[i])
    return rmsnorm(x, norm_final)


_first_inputs = second_inputs


def second_inputs(seed=0):
    import zlib

    import numpy as np

    out = dict(_first_inputs(seed))
    spreads = {}
    factors = {'norm_mix': 4.259,
     'norm_ffn': 4.908,
     'norm_final': 9.04,
     'm_conv_b': 38.824,
     'm_head_norm': 8.0,
     'c_b_in': 25.464,
     'c_dw_b': 16.733,
     'c_ln_g': 61.73,
     'c_ln_b': 60.931,
     'c_b_out': 22.049,
     'f_conv_b': 5.086}
    for name, (base, spread) in spreads.items():
        noise = np.random.default_rng([zlib.crc32(name.encode()), seed]).standard_normal(out[name].shape)
        drawn = base * np.exp(spread * noise) if base else spread * noise
        out[name] = __import__('jax').numpy.asarray(drawn.astype(out[name].dtype))
    for name, factor in factors.items():
        out[name] = (out[name] * factor).astype(out[name].dtype)
    return out


_narrow_inputs = second_inputs


def second_inputs(seed=0):

    out = dict(_narrow_inputs(seed))
    wider = {'norm_final': 3.41, 'c_ln_g': 3.31, 'c_ln_b': 3.31, 'c_b_out': 3.25}
    for name, times in wider.items():
        mean = out[name].mean()
        out[name] = (mean + times * (out[name] - mean)).astype(out[name].dtype)
    return out


DEPTH_3 = 1

GRID_W = 64
CTX_LEN = 256

RET_W = D_MODEL // 2
RET_HEADS = 4
RET_HEAD_DIM = RET_W // RET_HEADS
RET_CHUNK = 128
ROPE_BASE = 10000.0
ROPE_FREQS = RET_HEAD_DIM // 4
FNET_W = D_MODEL // 4
FNET_GROUPS = 4
FNET_GROUP_DIM = FNET_W // FNET_GROUPS
GMLP_W = D_MODEL // 4
GMLP_GROUPS = 4
GMLP_GROUP_DIM = GMLP_W // GMLP_GROUPS
GMLP_CHUNK = 128
N_BRANCH = 3
D_FF_3 = 4 * D_MODEL
IN_W = 4 * RET_W + FNET_W + 2 * GMLP_W + N_BRANCH * D_MODEL
IN_SPLITS = (RET_W, 2 * RET_W, 3 * RET_W, 4 * RET_W, 4 * RET_W + FNET_W,
             4 * RET_W + FNET_W + GMLP_W, 4 * RET_W + FNET_W + 2 * GMLP_W)


def rms_norm_3(x, gain=None):
    xf = x.astype(jnp.float32)
    y = xf * lax.rsqrt(jnp.mean(xf * xf, axis=-1, keepdims=True) + EPS)
    if gain is not None:
        y = y * gain.astype(jnp.float32)
    return y.astype(x.dtype)

def modulate_3(h, shift, scale):
    return h * (1.0 + scale) + shift

def grid_rope_angles(n_tokens):
    rows = n_tokens // GRID_W
    row = jnp.repeat(jnp.arange(rows, dtype=jnp.float32), GRID_W)
    col = jnp.tile(jnp.arange(GRID_W, dtype=jnp.float32), rows)
    freqs = ROPE_BASE ** (-jnp.arange(ROPE_FREQS, dtype=jnp.float32) / ROPE_FREQS)
    return jnp.concatenate([row[:, None] * freqs, col[:, None] * freqs], axis=-1)

def apply_grid_rope(a, angles):
    cos = jnp.cos(angles)[None, :, None, :]
    sin = jnp.sin(angles)[None, :, None, :]
    a1, a2 = jnp.split(a, 2, axis=-1)
    return jnp.concatenate([a1 * cos - a2 * sin, a1 * sin + a2 * cos], axis=-1)

def ret_scan_states(k, v, log_g, s0):
    B, L, H, dk = k.shape
    n = L // RET_CHUNK
    kc = k.reshape(B, n, RET_CHUNK, H, dk)
    vc = v.reshape(B, n, RET_CHUNK, H, -1)
    pos = jnp.arange(RET_CHUNK, dtype=jnp.float32)
    w_state = jnp.exp(log_g[:, None] * (RET_CHUNK - 1.0 - pos)[None, :])
    u = jnp.einsum('bnshd,hs,bnshe->nbhde', kc, w_state, vc)
    decay = jnp.exp(log_g * RET_CHUNK)[None, :, None, None]

    def step(s, u_i):
        return decay * s + u_i, s

    s_final, s_starts = lax.scan(step, s0, u)
    return s_starts, s_final

def ret_chunk_out(q, k, v, log_g, s_starts, inclusive):
    B, L, H, dk = q.shape
    n = L // RET_CHUNK
    qc = q.reshape(B, n, RET_CHUNK, H, dk)
    kc = k.reshape(B, n, RET_CHUNK, H, dk)
    vc = v.reshape(B, n, RET_CHUNK, H, -1)
    pos = jnp.arange(RET_CHUNK, dtype=jnp.float32)
    diff = pos[:, None] - pos[None, :]
    keep = (diff >= 0) if inclusive else (diff > 0)
    dmask = jnp.where(keep[None], jnp.exp(log_g[:, None, None] * jnp.maximum(diff, 0.0)[None]), 0.0)
    scores = jnp.einsum('bnchd,bnshd->bnhcs', qc, kc) * dmask[None, None]
    inner = jnp.einsum('bnhcs,bnshe->bnche', scores, vc)
    q_decay = jnp.exp(log_g[:, None] * (pos + 1.0)[None, :])
    cross = jnp.einsum('bnchd,hc,nbhde->bnche', qc, q_decay, s_starts)
    return (inner + cross).reshape(B, L, H, -1)

def retention_bidir(q, k, v, log_g_f, log_g_b, s0_f, s0_b):
    st_f, sf = ret_scan_states(k, v, log_g_f, s0_f)
    o_f = ret_chunk_out(q, k, v, log_g_f, st_f, True)
    qr, kr, vr = jnp.flip(q, axis=1), jnp.flip(k, axis=1), jnp.flip(v, axis=1)
    st_b, sb = ret_scan_states(kr, vr, log_g_b, s0_b)
    o_b = jnp.flip(ret_chunk_out(qr, kr, vr, log_g_b, st_b, False), axis=1)
    return o_f + o_b, sf, sb

def fourier_mix(f):
    B, L, _ = f.shape
    fg = f.reshape(B, L, FNET_GROUPS, FNET_GROUP_DIM).astype(jnp.float32)
    y = jnp.fft.fft2(fg, axes=(1, 3), norm='ortho').real
    return y.reshape(B, L, FNET_W).astype(f.dtype)

def sgu_mix(u, v, w_s, b_s, g_norm):
    B, L, _ = v.shape
    u = jax.nn.gelu(u)
    v = jax.nn.gelu(v).reshape(B, L, GMLP_GROUPS, GMLP_GROUP_DIM)
    v = rms_norm_3(v, g_norm.reshape(GMLP_GROUPS, GMLP_GROUP_DIM))
    v = v.reshape(B, L // GMLP_CHUNK, GMLP_CHUNK, GMLP_GROUPS, GMLP_GROUP_DIM)
    s = jnp.einsum('gts,bnsgc->bntgc', w_s, v) + jnp.transpose(b_s)[None, None, :, :, None]
    return u * s.reshape(B, L, GMLP_W)

def token_mixer(h, w_in, log_g, w_s, b_s, g_norm, w_a, w_b, w_c, w_o, s0_f, s0_b, angles):
    B, L, _ = h.shape
    z = h @ w_in
    q, k, v, g, f, u, vs, gates = jnp.split(z, IN_SPLITS, axis=-1)
    q = q.reshape(B, L, RET_HEADS, RET_HEAD_DIM).astype(jnp.float32)
    k = k.reshape(B, L, RET_HEADS, RET_HEAD_DIM).astype(jnp.float32) * (RET_HEAD_DIM ** -0.5)
    v = v.reshape(B, L, RET_HEADS, RET_HEAD_DIM).astype(jnp.float32)
    if angles is not None:
        q = apply_grid_rope(q, angles)
        k = apply_grid_rope(k, angles)
    o, sf, sb = retention_bidir(q, k, v, log_g[0], log_g[1], s0_f, s0_b)
    ret = rms_norm_3(o).reshape(B, L, RET_W).astype(h.dtype) * jax.nn.silu(g)
    four = fourier_mix(f)
    sgu = sgu_mix(u, vs, w_s, b_s, g_norm)
    ga, gb, gc = jnp.split(jax.nn.sigmoid(gates), N_BRANCH, axis=-1)
    merged = ga * (ret @ w_a) + gb * (four @ w_b) + gc * (sgu @ w_c)
    return merged @ w_o, sf, sb

def sq_relu_mlp(h, w_up, w_down):
    a = jax.nn.relu(h @ w_up)
    return (a * a) @ w_down

def third_inputs(seed: int = 0) -> dict:
    key = jax.random.key(seed)
    ks = jax.random.split(key, 24)
    f32 = jnp.float32
    nrm = lambda k, shape, s: jax.random.normal(k, shape, f32) * s
    base_logit = jnp.log(2.0 ** (5.0 + jnp.arange(RET_HEADS, dtype=f32)) - 1.0)
    return {
        'x': nrm(ks[0], (BATCH, SEQ, D_MODEL), 1.0),
        'c': nrm(ks[1], (BATCH, D_MODEL), 1.0),
        'ctx': nrm(ks[2], (BATCH, CTX_LEN, D_MODEL), 1.0),
        'c_ctx': nrm(ks[3], (D_MODEL,), 1.0),
        'w_mod': nrm(ks[4], (DEPTH_3, D_MODEL, 6 * D_MODEL), 0.5 * D_MODEL ** -0.5),
        'b_mod': nrm(ks[5], (DEPTH_3, 6 * D_MODEL), 0.02),
        'g_pre_mix': 1.0 + nrm(ks[6], (DEPTH_3, D_MODEL), 0.02),
        'g_post_mix': 1.0 + nrm(ks[7], (DEPTH_3, D_MODEL), 0.02),
        'g_pre_mlp': 1.0 + nrm(ks[8], (DEPTH_3, D_MODEL), 0.02),
        'g_post_mlp': 1.0 + nrm(ks[9], (DEPTH_3, D_MODEL), 0.02),
        'w_in': nrm(ks[10], (DEPTH_3, D_MODEL, IN_W), D_MODEL ** -0.5),
        'ret_decay_logit': base_logit[None, None, :] + nrm(ks[11], (DEPTH_3, 2, RET_HEADS), 0.1),
        'sgu_w_s': nrm(ks[12], (DEPTH_3, GMLP_GROUPS, GMLP_CHUNK, GMLP_CHUNK), GMLP_CHUNK ** -0.5),
        'sgu_b_s': 1.0 + nrm(ks[13], (DEPTH_3, GMLP_GROUPS, GMLP_CHUNK), 0.02),
        'sgu_norm': 1.0 + nrm(ks[14], (DEPTH_3, GMLP_W), 0.02),
        'w_branch_a': nrm(ks[15], (DEPTH_3, RET_W, D_MODEL), RET_W ** -0.5),
        'w_branch_b': nrm(ks[16], (DEPTH_3, FNET_W, D_MODEL), FNET_W ** -0.5),
        'w_branch_c': nrm(ks[17], (DEPTH_3, GMLP_W, D_MODEL), GMLP_W ** -0.5),
        'w_out': nrm(ks[18], (DEPTH_3, D_MODEL, D_MODEL), D_MODEL ** -0.5),
        'w_up': nrm(ks[19], (DEPTH_3, D_MODEL, D_FF_3), D_MODEL ** -0.5),
        'w_down': nrm(ks[20], (DEPTH_3, D_FF_3, D_MODEL), D_FF_3 ** -0.5),
    }

def third_block(x, c, ctx, c_ctx, w_mod, b_mod, g_pre_mix, g_post_mix, g_pre_mlp, g_post_mlp,
              w_in, ret_decay_logit, sgu_w_s, sgu_b_s, sgu_norm, w_branch_a, w_branch_b,
              w_branch_c, w_out, w_up, w_down):
    B, L, _ = x.shape
    angles = grid_rope_angles(L)
    silu_c = jax.nn.silu(c)
    silu_cc = jax.nn.silu(c_ctx)
    s0 = jnp.zeros((B, RET_HEADS, RET_HEAD_DIM, RET_HEAD_DIM), jnp.float32)
    for l in range(DEPTH_3):
        last = l == DEPTH_3 - 1
        mod = (silu_c @ w_mod[l] + b_mod[l])[:, None, :]
        sh1, sc1, gt1, sh2, sc2, gt2 = jnp.split(mod, 6, axis=-1)
        mod_c = silu_cc @ w_mod[l] + b_mod[l]
        csh1, csc1, cgt1, csh2, csc2, cgt2 = jnp.split(mod_c, 6, axis=-1)
        log_g = jax.nn.log_sigmoid(ret_decay_logit[l].astype(jnp.float32))

        hc = modulate_3(rms_norm_3(ctx, g_pre_mix[l]), csh1, csc1)
        if last:
            kc_, vc_ = jnp.split(hc @ w_in[l][:, RET_W:3 * RET_W], 2, axis=-1)
            kc_ = kc_.reshape(B, CTX_LEN, RET_HEADS, RET_HEAD_DIM).astype(jnp.float32) * (RET_HEAD_DIM ** -0.5)
            vc_ = vc_.reshape(B, CTX_LEN, RET_HEADS, RET_HEAD_DIM).astype(jnp.float32)
            _, sf = ret_scan_states(kc_, vc_, log_g[0], s0)
            _, sb = ret_scan_states(jnp.flip(kc_, axis=1), jnp.flip(vc_, axis=1), log_g[1], s0)
        else:
            yc, sf, sb = token_mixer(hc, w_in[l], log_g, sgu_w_s[l], sgu_b_s[l], sgu_norm[l],
                                     w_branch_a[l], w_branch_b[l], w_branch_c[l], w_out[l],
                                     s0, s0, None)
            ctx_mid = ctx + cgt1 * rms_norm_3(yc, g_post_mix[l])
            hc2 = modulate_3(rms_norm_3(ctx_mid, g_pre_mlp[l]), csh2, csc2)
            ctx_next = ctx_mid + cgt2 * rms_norm_3(sq_relu_mlp(hc2, w_up[l], w_down[l]), g_post_mlp[l])

        h = modulate_3(rms_norm_3(x, g_pre_mix[l]), sh1, sc1)
        y, _, _ = token_mixer(h, w_in[l], log_g, sgu_w_s[l], sgu_b_s[l], sgu_norm[l],
                              w_branch_a[l], w_branch_b[l], w_branch_c[l], w_out[l],
                              sf, sb, angles)
        x = x + gt1 * rms_norm_3(y, g_post_mix[l])
        h2 = modulate_3(rms_norm_3(x, g_pre_mlp[l]), sh2, sc2)
        x = x + gt2 * rms_norm_3(sq_relu_mlp(h2, w_up[l], w_down[l]), g_post_mlp[l])

        if not last:
            ctx = ctx_next
    return x


_first_inputs_3 = third_inputs


def third_inputs(seed=0):
    import zlib

    import numpy as np

    out = dict(_first_inputs_3(seed))
    spreads = {}
    factors = {}
    for name, (base, spread) in spreads.items():
        noise = np.random.default_rng([zlib.crc32(name.encode()), seed]).standard_normal(out[name].shape)
        drawn = base * np.exp(spread * noise) if base else spread * noise
        out[name] = __import__('jax').numpy.asarray(drawn.astype(out[name].dtype))
    for name, factor in factors.items():
        out[name] = (out[name] * factor).astype(out[name].dtype)
    return out


_narrow_inputs_3 = third_inputs


def third_inputs(seed=0):

    out = dict(_narrow_inputs_3(seed))
    wider = {'g_pre_mix': 7.31,
     'g_post_mix': 10.8,
     'g_pre_mlp': 10.47,
     'g_post_mlp': 10.43,
     'sgu_b_s': 12.0,
     'sgu_norm': 12.0}
    for name, times in wider.items():
        mean = out[name].mean()
        out[name] = (mean + times * (out[name] - mean)).astype(out[name].dtype)
    return out


def setup_inputs(seed=0):
    out = dict(first_inputs(seed))
    for name, value in second_inputs(seed + 1).items():
        if name != "x":
            out[name + "_2"] = value
    for name, value in third_inputs(seed + 2).items():
        if name != "x":
            out[name + "_3"] = value
    return out


def reference(
    x, c, positions, ada_w, ada_b, mix_norm, ffn_norm, ffn_w1, ffn_w2, ab_w_in, gla_gate_up,
    gla_gate_b, gla_out_norm, dsa_q_norm, dsa_k_norm, ab_w_out, cd_w_in, pool_w, pool_scale,
    sb_q_norm, sb_k_norm, cd_w_out, norm_mix_2, norm_ffn_2, norm_final_2, m_w_in_2, m_conv_w_2,
    m_conv_b_2, m_b_gates_2, m_head_norm_2, m_w_out_2, c_w_in_2, c_b_in_2, c_dw_w_2, c_dw_b_2,
    c_ln_g_2, c_ln_b_2, c_w_out_2, c_b_out_2, f_w_up_2, f_conv_w_2, f_conv_b_2, f_w_down_2, c_3,
    ctx_3, c_ctx_3, w_mod_3, b_mod_3, g_pre_mix_3, g_post_mix_3, g_pre_mlp_3, g_post_mlp_3,
    w_in_3, ret_decay_logit_3, sgu_w_s_3, sgu_b_s_3, sgu_norm_3, w_branch_a_3, w_branch_b_3,
    w_branch_c_3, w_out_3, w_up_3, w_down_3,
):
    x = first_block(
        x, c, positions, ada_w, ada_b, mix_norm, ffn_norm, ffn_w1, ffn_w2, ab_w_in, gla_gate_up,
        gla_gate_b, gla_out_norm, dsa_q_norm, dsa_k_norm, ab_w_out, cd_w_in, pool_w, pool_scale,
        sb_q_norm, sb_k_norm, cd_w_out,
    )
    x = second_block(
        x, norm_mix_2, norm_ffn_2, norm_final_2, m_w_in_2, m_conv_w_2, m_conv_b_2, m_b_gates_2,
        m_head_norm_2, m_w_out_2, c_w_in_2, c_b_in_2, c_dw_w_2, c_dw_b_2, c_ln_g_2, c_ln_b_2,
        c_w_out_2, c_b_out_2, f_w_up_2, f_conv_w_2, f_conv_b_2, f_w_down_2,
    )
    return third_block(
        x, c_3, ctx_3, c_ctx_3, w_mod_3, b_mod_3, g_pre_mix_3, g_post_mix_3, g_pre_mlp_3,
        g_post_mlp_3, w_in_3, ret_decay_logit_3, sgu_w_s_3, sgu_b_s_3, sgu_norm_3, w_branch_a_3,
        w_branch_b_3, w_branch_c_3, w_out_3, w_up_3, w_down_3,
    )


_drawn_inputs = setup_inputs


def setup_inputs(seed=0):
    import zlib

    import numpy as np

    out = dict(_drawn_inputs(seed))
    spreads = {}
    factors = {'gla_gate_b': 8.0,
     'dsa_q_norm': 3.217,
     'dsa_k_norm': 3.867,
     'ctx_3': 8.0,
     'c_ctx_3': 8.0,
     'b_mod_3': 8.0,
     'g_pre_mix_3': 7.602,
     'g_post_mix_3': 7.729,
     'g_pre_mlp_3': 7.663,
     'g_post_mlp_3': 8.0,
     'ret_decay_logit_3': 8.0,
     'sgu_w_s_3': 3.231,
     'sgu_b_s_3': 8.0,
     'sgu_norm_3': 8.0,
     'w_branch_a_3': 3.412,
     'w_branch_b_3': 3.709}
    for name, (base, spread) in spreads.items():
        noise = np.random.default_rng([zlib.crc32(name.encode()), seed]).standard_normal(out[name].shape)
        drawn = base * np.exp(spread * noise) if base else spread * noise
        out[name] = __import__('jax').numpy.asarray(drawn.astype(out[name].dtype))
    for name, factor in factors.items():
        out[name] = (out[name] * factor).astype(out[name].dtype)
    return out
```

```python
from contextlib import ExitStack, contextmanager

import numpy as np

import concourse.bass as bass
from concourse import mybir

F32 = mybir.dt.float32
I32 = mybir.dt.int32
ALU = mybir.AluOpType
ACT = mybir.ActivationFunctionType
AX = mybir.AxisListType

P = 128
S = 512
D = 1024
KD = D // P
NB = S // P
FF = 2816
FT = FF // P
F3 = 4096
F3T = F3 // P
EPS = 1e-6
NEG = -1e30
TAKEN = -3e38
TOPK = 128
CTX = 256
RING = 4
SLOT = 11 * P
ADA_RING = 2
POOL = 64
CHUNK = 64
NCH = S // CHUNK
CONV = 31



def square_constants():
    p = np.arange(P)[:, None]
    c = np.arange(P)[None, :]
    a64 = 2 * np.pi * (np.arange(64)[:, None] * np.arange(64)[None, :] % 64) / 64
    cb, sb = np.zeros((P, P)), np.zeros((P, P))
    for g in range(2):
        s = slice(64 * g, 64 * g + 64)
        cb[s, s] = np.cos(a64)
        sb[s, s] = -np.sin(a64)
    norm = 1.0 / np.sqrt(S * 64.0)
    out = {
        "ones": np.ones((P, P)),
        "ident": (p == c),
        "swap64": (p == (c + 64) % P),
        "swap32": (p == (c ^ 32)),
        "later": (p > c),
        "causal_neg": np.where(c <= p, 0.0, NEG),
        "before": (p <= c),
        "strict": (p < c),
        "strict_neg": np.where(p < c, 0.0, NEG),
        "gla": (p <= c) & (p // CHUNK == c // CHUNK),
        "dft_cos": cb * norm,
        "dft_sin": sb * norm,
    }
    return {k: np.asarray(v, np.float32) for k, v in out.items()}


SQUARES = list(square_constants())


def other_constants():
    p = np.arange(P)
    inv = lambda half: (10000.0 ** (-np.arange(half) / half)).astype(np.float32)
    sel = np.zeros((P, 4, P))
    for h in range(4):
        sel[h, h] = 1
    t = np.arange(16)
    return {
        "reset": np.tile((np.arange(S) % CHUNK != 0).astype(np.float32), (P, 1)),
        "count": np.tile(np.stack([1.0 / np.minimum(t + 1, 2 ** (g + 1)) for g in range(4)]).reshape(1, 64), (P, 1)),
        "sel": sel.reshape(P, 4 * P),
        "freq_q": inv(64)[p % 64][:, None],
        "freq_i": inv(32)[p % 32][:, None],
        "sign_q": np.where(p < 64, -1.0, 1.0)[:, None],
        "sign_i": np.where(p % 64 < 32, -1.0, 1.0)[:, None],
        "eps": np.full((P, 1), EPS),
        "one": np.ones((P, 1)),
    }


SELF_W, CTX_W = 896, 640


def late_constants():
    p = np.arange(P)[:, None]
    x = np.arange(SELF_W)[None, :]
    d = x - 384 - p
    y = np.arange(CTX_W)[None, :]
    rows = np.repeat(np.arange(S // 64, dtype=np.float32), 64)
    cols = np.tile(np.arange(64, dtype=np.float32), S // 64)
    freqs = (np.float32(10000.0) ** (-np.arange(32, dtype=np.float32) / 32)).astype(np.float32)
    ang = np.concatenate([rows[:, None] * freqs, cols[:, None] * freqs], axis=-1).astype(np.float64).T
    aL = 2 * np.pi * (np.arange(S)[:, None] * np.arange(S)[None, :] % S) / S
    tok = lambda m: m.reshape(NB, P, S).transpose(1, 0, 2).reshape(P, NB * S)
    dist = np.zeros((P, 6 * S))
    dist[:, 0:SELF_W] = np.maximum(d, 0)
    dist[:, SELF_W:2 * SELF_W] = np.maximum(-d, 0)
    dist[:, 2 * SELF_W:2 * SELF_W + CTX_W] = y + P - p
    dist[:, 2 * SELF_W + CTX_W:] = CTX_W - y + p
    return {
        "grid": np.concatenate([np.tile(np.cos(ang), (2, 1)),
                                np.concatenate([-np.sin(ang), np.sin(ang)])], axis=1),
        "dist": dist,
        "dft": np.concatenate([tok(np.cos(aL)), tok(np.sin(aL))], axis=1),
    }


VECTORS = [
    ("mix_norm", 2 * D), ("ffn_norm", 2 * D), ("ada_b", 2 * 6 * D), ("gla_gate_b", 256), ("gla_out_norm", P),
    ("dsa_q_norm", P), ("dsa_k_norm", P), ("pool_scale", 4 * P), ("sb_q_norm", P), ("sb_k_norm", P),
    ("norm_mix_2", 2 * D), ("norm_ffn_2", 2 * D), ("norm_final_2", D), ("m_conv_w_2", 4 * D), ("m_conv_b_2", D),
    ("m_head_norm_2", D), ("c_b_in_2", 2 * D), ("c_dw_w_2", CONV * D), ("c_dw_b_2", D), ("c_ln_g_2", D),
    ("c_ln_b_2", D), ("c_b_out_2", D), ("f_conv_w_2", 2 * 3 * 2 * FF), ("f_conv_b_2", 2 * 2 * FF),
    ("b_mod_3", 6 * D), ("g_pre_mix_3", D), ("g_post_mix_3", D), ("g_pre_mlp_3", D), ("g_post_mlp_3", D),
]
VCOL = {}
NV = 0
for _name, _n in VECTORS:
    VCOL[_name] = NV
    NV += _n // P

STAGES = [
    ("iq", "feat", 4, 8), ("ik", "feat", 1, 8), ("gr", "feat", 4, 8), ("gq", "feat", 2, 8), ("gk", "feat", 2, 8),
    ("gv", "tok", 4, 8), ("dv", "tok", 4, 8), ("dq", "feat", 4, 8), ("dk", "feat", 4, 8), ("abo", "loop", 8, 8),
    ("up0", "loop", 2 * FT, 8), ("dn0", "loop", 8, FT),
    ("cu", "feat", 4, 8), ("sq", "feat", 4, 8), ("sk", "feat", 4, 8), ("sv", "tok", 4, 8), ("cdo", "loop", 8, 8),
    ("up1", "loop", 2 * FT, 8), ("dn1", "loop", 8, FT),
    ("mqk", "feat", 8, 8), ("mv", "tok", 8, 8), ("mo", "loop", 8, 8), ("mout", "loop", 8, 8),
    ("up2", "loop", 2 * FT, 8), ("dn2", "loop", 8, FT),
    ("ca", "loop", 16, 8), ("cout", "loop", 8, 8),
    ("up3", "loop", 2 * FT, 8), ("dn3", "loop", 8, FT),
    ("ck", "feat", 4, 8), ("cv", "tok", 2, 8),
    ("rk", "feat", 4, 8), ("rq", "feat", 4, 8), ("rv", "tok", 4, 8), ("fv", "tok", 4, 8), ("ru", "feat", 2, 8),
    ("rg", "feat", 4, 8), ("br", "branch", 48, 8), ("ro", "loop", 8, 8), ("upr", "loop", F3T, 8), ("dnr", "loop", 8, F3T),
]
STAGE = {s[0]: s for s in STAGES}


def pieces(k_tiles):
    return {8: [8], 22: [11, 11], 32: [8, 8, 8, 8]}[k_tiles]


def chunks_of(stage):
    name, kind, tiles, kt = stage
    if kind == "tok":
        return 4 * ((tiles + 3) // 4)
    if kind == "branch":
        return 32
    return tiles * len(pieces(kt))


def chunk_width(stage):
    return max(pieces(stage[3])) * P


def projection_keys():
    keys = []
    for name, kind, tiles, _ in STAGES:
        keys += [(name, t) for t in range(tiles)]
        if name == "ik":
            keys += [("iw", t) for t in range(NB)] + [("glow", 0)]
        if name == "mo":
            keys += [("mi", 0), ("mf", 0)]
    return keys


def mixing_keys():
    k = [("ss", 0)]
    k += [("rot_i", t) for t in range(5)]
    k += [("idx", b, h) for b in range(1, NB) for h in range(8)]
    k += [("gate", t) for t in range(2)]
    for t in range(9):
        k += [("stat_d", t)] if t < 8 else []
        k += [("rot_d", t - 1)] if t >= 1 else []
    k += [("kdt", t) for t in range(2)] + [("att", h) for h in range(4)]
    k += [("kv", t, e) for t in range(2) for e in range(2)]
    for h in range(5):
        k += [("o", h)] if h < 4 else []
        k += [("stat_o", h - 1)] if h >= 1 else []
    units = [(b, h) for b in range(NB) for h in range(4)]
    for n in range(len(units) + 2):
        k += [("qk", *units[n])] if n < 16 else []
        k += [("pT", *units[n - 1])] if 1 <= n <= 16 else []
        k += [("av", *units[n - 2])] if n >= 2 else []
    k += [("ss", 1), ("ss", 2)]
    k += [("stat_s", t) for t in range(8)] + [("pool", g) for g in range(4)]
    for h in range(6):
        k += [("z", h, j) for j in range(NB)] if h < 4 else []
        k += [("cum", h - 1, j) for j in range(NB)] if 1 <= h <= 4 else []
        k += [("sb", h - 2)] if h >= 2 else []
    k += [("ss", 3), ("ss", 4)]
    k += [("acol", 0)]
    for h in range(4):
        k += [("mbc", h, 0), ("mbc", h, 1)] + [("ms", h, j) for j in range(NB)]
        k += [("mn", h, 0), ("mn", h, 1), ("md", h), ("stat_m", h)]
    k += [("ss", 5), ("ss", 6), ("lnm", 0), ("lnv", 0), ("ss", 7), ("ss", 8), ("ssc", 0), ("ss", 9)]
    k += [("rot_r", t) for t in range(8)]
    for h in range(4):
        k += [("rs", h, j) for j in range(6)] + [("rout", h), ("stat_r", h)]
    k += [("dftl", t, c) for t in range(2) for c in range(2)] + [("four", t) for t in range(2)]
    k += [("sgu", t) for t in range(2)]
    k += [("ssy", 0), ("ss", 10), ("ssy", 1)]
    return k


class Ring:

    def __init__(self, banks, full, empty, keys):
        self.banks, self.full_sem, self.empty_sem = banks, full, empty
        self.number = {key: n for n, key in enumerate(keys)}
        assert len(self.number) == len(keys)

    def bank(self, key):
        return self.banks[:, self.number[key] % RING, :]

    def may_fill(self, key):
        n = self.number[key]
        return self.empty_sem[n % RING], n // RING

    def filled(self, key):
        return self.full_sem, self.number[key] + 1

    def emptied(self, key):
        n = self.number[key]
        return self.empty_sem[n % RING], n // RING + 1


class Chip:

    def __init__(self, nc, ctx, dram):
        self.dram = dram

        def sb(name, shape, dt=F32):
            return ctx.enter_context(nc.sbuf_tensor(name, shape, dt))

        def sem(name):
            return ctx.enter_context(nc.semaphore(name))

        self.x = sb("x_tiles", [P, KD * S])
        self.h = sb("h_tiles", [P, KD * S])
        self.pool = sb("scratch", [P, POOL * S])
        self.w = sb("weight_ring", [P, RING * SLOT])
        self.ada = sb("ada_ring", [P, ADA_RING * D])
        self.cond = sb("cond", [P, 2 * D])
        self.sq_const = sb("squares", [P, len(SQUARES) * P])
        self.other = sb("others", [P, sum(v.shape[1] for v in other_constants().values())])
        self.vec = sb("vectors", [P, NV])
        self.wsmall = sb("small_weights", [P, KD * 32])
        self.gate_up = sb("gate_up", [16, 256])
        self.pool_w = self.T(46)
        self.sgu_w = sb("sgu_w", [P, 4 * P])
        self.sgu_norm = sb("sgu_norm", [P, 256])
        self.sgu_b = self.T(63)
        self.m_bias = sb("m_bias", [4, 2])
        self.mod = sb("mod", [P, 4 * 48])
        self.gain = sb("gain", [P, 9 * 8])
        self.acc = sb("ada_acc", [P, 8])
        self.small = sb("small", [P, 160])

        banks = [ctx.enter_context(nc.psum_tensor(n, [P, RING, S], F32)) for n in ("proj_banks", "mix_banks")]
        self.proj = Ring(banks[0], sem("proj_full"), [sem(f"proj_empty{i}") for i in range(RING)], projection_keys())
        self.mix = Ring(banks[1], sem("mix_full"), [sem(f"mix_empty{i}") for i in range(RING)], mixing_keys())
        self.landed = [sem(f"w_landed{i}") for i in range(RING)]
        self.ada_landed = [sem(f"ada_landed{i}") for i in range(ADA_RING)]
        self.sem = {n: sem(n) for n in (
            "x_loaded", "setup", "late", "pool_loaded", "dft_loaded", "cond_loaded", "ctx_loaded", "act_chain", "dve_chain",
            "cond_ready", "pos_ready", "trig_ready", "ada_used", "ada_copied", "ada_first", "mod_ready", "sq_ready", "xn_ready", "h_ready",
            "iq_ready", "idx_used", "gate_ready", "span_ready", "decay_ready", "gla_ready", "head_normed", "head_roped",
            "state_ready", "mixed", "max_ready", "p_ready", "pn_ready",
            "pooled", "z_ready", "sp_ready", "lw_ready", "w_ready", "wneg_ready",
            "convolved", "conv_init", "conv_act", "mid_ready", "m_gate", "m_rows", "m_guard", "e_arg", "e_ready",
            "p_head", "hm_ready", "hsq_ready", "den_abs", "u_ready", "u_centred", "u_sq", "u_normed", "u_act",
            "x_ready", "hc_ready", "vs_var", "vs_std", "vs_ready", "lg_abs", "lg_ready", "table_arg", "table_ready",
            "pr_ready", "sgu_ready", "merged", "relu_ready", "mlp_mid", "y_ready", "out_ready", "out_stored",
        )}
        self.first_chunk, n = {}, 0
        for s in STAGES:
            self.first_chunk[s[0]] = n
            n += chunks_of(s)

    def T(self, i, n=1):
        return self.pool[:, i * S:(i + n) * S]

    def X(self, k):
        return self.x[:, k * S:(k + 1) * S]

    def H(self, k):
        return self.h[:, k * S:(k + 1) * S]

    def square(self, name):
        i = SQUARES.index(name)
        return self.sq_const[:, i * P:(i + 1) * P]

    def const(self, name):
        at = 0
        for k, v in other_constants().items():
            if k == name:
                return self.other[:, at:at + v.shape[1]]
            at += v.shape[1]
        raise KeyError(name)

    def v(self, name, k=0, n=1):
        return self.vec[:, VCOL[name] + k:VCOL[name] + k + n]

    def m(self, layer, part, k=0, n=1):
        at = 48 * layer + 8 * part + k
        return self.mod[:, at:at + n]

    def g(self, use, k=0, n=1):
        return self.gain[:, 8 * use + k:8 * use + k + n]

    def slot(self, chunk):
        i = chunk % RING
        return self.w[:, i * SLOT:(i + 1) * SLOT]

    def chunk_landed(self, chunk):
        return self.landed[chunk % RING], 16 * (chunk // RING + 1)


class Steps:

    def __init__(self, eng, chain):
        self.eng, self.chain, self.count = eng, chain, {}

    def next(self, sem):
        self.count[id(sem)] = self.count.get(id(sem), 0) + 1
        return self.count[id(sem)]

    def link(self, ins):
        self.done(ins, self.chain)

    def done(self, ins, sem):
        ins.then_inc(sem, 1)
        self.eng.wait_ge(sem, self.next(sem))

    def last(self, ins, emptied):
        sem, n = emptied
        ins.then_inc(sem, 1)
        self.eng.wait_ge(sem, n)

NORM_AFTER = {1: "abo", 2: "dn0", 3: "cdo", 4: "dn1", 5: "mout", 6: "dn2", 7: "cout", 8: "dn3"}
MODULATED = {0: (0, 0, 0, 1), 1: (1, 0, 3, 2), 2: (2, 1, 0, 3), 3: (3, 1, 3, 4), 9: (4, 2, 0, 6), 10: (5, 2, 3, 7)}
PLAIN = {4: ("norm_mix_2", 0), 5: ("norm_ffn_2", 0), 6: ("norm_mix_2", 8), 7: ("norm_ffn_2", 8), 8: ("norm_final_2", 0)}
SQ0, RSTD = 56, 54


def h_count(norm, k):
    return 8 * (norm if norm < 8 else norm - 1) + k + 1



def sync_program(nc, sp, c):
    d, s = c.dram, c.sem
    sp.dma_start(c.x[:, :].rearrange("p (k t) -> p k t", k=KD), d["x"].rearrange("(k p) t -> p k t", p=P)).then_inc(s["x_loaded"], 16)

    proj = c.proj

    def load(stage, n, chunk, width):
        sp.dma_start(c.slot(chunk)[:, 0:width], d["w_" + stage][n]).then_inc(c.landed[chunk % RING], 16)

    for stage in STAGES:
        name, kind, tiles, kt = stage
        first, width, total = c.first_chunk[name], chunk_width(stage), chunks_of(stage)
        looped = kind in ("loop", "branch")
        for n in range(RING if looped else total):
            if first + n >= RING:
                sp.wait_ge(proj.full_sem, chunk_use(c, first + n - RING))
            load(name, n, first + n, width)
        if looped:
            per = len(pieces(kt))
            use0 = proj.number[(name, 0)]
            with sp.Fori(1, total // RING) as i:
                for q in range(RING):
                    if kind == "branch":
                        sp.wait_ge(proj.full_sem, use0 + 6 * (i - 1) + (q + 1 if q < 3 else 6))
                    else:
                        sp.wait_ge(proj.full_sem, use0 + (RING // per) * (i - 1) + q // per + 1)
                    slot = c.slot(first + q)[:, 0:width]
                    sp.dma_start(slot, d["w_" + name][bass.ds(i * RING + q, 1)].rearrange("o p f -> p (o f)")) \
                        .then_inc(c.landed[(first + q) % RING], 16)
    for k in range(KD):
        sp.wait_ge(s["out_ready"], k + 1)
        sp.dma_start(d["out"][k * P:(k + 1) * P, :], c.X(k)).then_inc(s["out_stored"], 16)
    sp.wait_ge(s["out_stored"], 16 * KD)


def chunk_use(c, chunk):
    name = [s[0] for s in STAGES if c.first_chunk[s[0]] <= chunk][-1]
    _, kind, tiles, kt = STAGE[name]
    n = chunk - c.first_chunk[name]
    if kind == "tok":
        toks = min(tiles, 4)
        t = toks * (n // 4) + (toks - 1 if n % 4 == 3 else 0)
    elif kind == "branch":
        t = 6 * (n // 4) + (n % 4 if n % 4 < 3 else 5)
    else:
        t = n // len(pieces(kt))
    return c.proj.filled((name, t))[1]


def gpsimd_program(nc, pool, c):
    d, s = c.dram, c.sem
    row = lambda ap: ap.partition_broadcast(P)
    for dst, src in (
        (c.cond[:, 0:D], row(d["c"])), (c.T(60).bitcast(I32), row(d["positions"])),
        (c.sq_const[:, :], d["squares"]), (c.other[:, :], d["others"]), (c.vec[:, :], d["vectors"]),
        (c.wsmall[:, :], d["w_small"]), (c.gate_up[:, :], d["gla_gate_up"]), (c.m_bias[:, :], d["m_bias"]),
    ):
        pool.dma_start(dst, src).then_inc(s["setup"], 16)

    def modulation(n, first):
        used = 48 * n
        for q in range(ADA_RING):
            if used + q >= ADA_RING:
                pool.wait_ge(s["ada_used"], used + q - ADA_RING + 1)
            pool.dma_start(c.ada[:, q * D:(q + 1) * D], d["ada"][used + q]).then_inc(c.ada_landed[q], 16)
        with pool.Fori(1, 48 // ADA_RING) as i:
            for q in range(ADA_RING):
                pool.wait_ge(s["ada_used"], i * ADA_RING + used + q - ADA_RING + 1)
                pool.dma_start(c.ada[:, q * D:(q + 1) * D],
                               d["ada"][bass.ds(i * ADA_RING + used + q, 1)].rearrange("o p f -> p (o f)")) \
                    .then_inc(c.ada_landed[q], 16)

    modulation(0, True)
    for dst, src in (
        (c.sgu_w[:, :], d["sgu_w"]), (c.sgu_norm[:, :], row(d["sgu_norm"])), (c.small[:, 0:8], row(d["decay"])),
    ):
        pool.dma_start(dst, src).then_inc(s["late"], 16)
    modulation(1, False)
    pool.wait_ge(*c.proj.filled(("up0", 2 * FT - 1)))
    pool.dma_start(c.pool_w, d["pool_w"]).then_inc(s["pool_loaded"], 16)
    pool.wait_ge(s["ada_used"], 96)
    pool.dma_start(c.cond[:, 0:D], row(d["c_3"])).then_inc(s["cond_loaded"], 16)
    pool.dma_start(c.cond[:, D:2 * D], row(d["c_ctx_3"])).then_inc(s["cond_loaded"], 16)
    modulation(2, False)
    pool.wait_ge(*c.proj.filled(("dn3", 7)))
    pool.dma_start(c.T(0, 4).rearrange("p (k t) -> p k t", k=KD), d["ctx"].rearrange("(k p) t -> p k t", p=P)).then_inc(s["ctx_loaded"], 16)
    pool.dma_start(c.T(41, 2), d["grid"]).then_inc(s["ctx_loaded"], 16)
    pool.dma_start(c.T(47, 6), d["dist"]).then_inc(s["ctx_loaded"], 16)
    pool.wait_ge(*c.proj.filled(("cv", 1)))
    pool.dma_start(c.T(0, 8), d["dft"]).then_inc(s["dft_loaded"], 16)
    pool.dma_start(c.sgu_b, row(d["sgu_b"])).then_inc(s["dft_loaded"], 16)



def tensor_program(nc, pe, c):
    s, proj, mix, T, H = c.sem, c.proj, c.mix, c.T, c.H
    mm = nc.tensor.matmul

    def open_bank(ring, key):
        pe.wait_ge(*ring.may_fill(key))
        return ring.bank(key)

    def feature_tile(name, t, rhs, n=S, ready=None):
        bank = open_bank(proj, (name, t))
        per = pieces(STAGE[name][3])
        k = 0
        for q, size in enumerate(per):
            chunk = c.first_chunk[name] + t * len(per) + q
            pe.wait_ge(*c.chunk_landed(chunk))
            for i in range(size):
                if ready is not None:
                    pe.wait_ge(*ready(k))
                last = mm(bank[:, 0:n], c.slot(chunk)[:, i * P:(i + 1) * P], rhs(k), start=k == 0, stop=k == sum(per) - 1)
                k += 1
        last.then_inc(proj.full_sem, 1)

    def feature_loop(name, rhs, ready, body=RING):
        _, _, tiles, kt = STAGE[name]
        per = pieces(kt)
        use0, chunk0 = proj.number[(name, 0)], c.first_chunk[name]
        with pe.Fori(0, tiles // body) as i:
            for j in range(body):
                u = use0 + j
                pe.wait_ge(proj.empty_sem[u % RING], i * (body // RING) + u // RING)
                k = 0
                for q, size in enumerate(per):
                    ch = chunk0 + j * len(per) + q
                    pe.wait_ge(c.landed[ch % RING], i * (16 * body * len(per) // RING) + 16 * (ch // RING + 1))
                    for n in range(size):
                        if j == 0 and ready(k) is not None:
                            pe.wait_ge(*ready(k))
                        last = mm(proj.banks[:, u % RING, :], c.slot(ch)[:, n * P:(n + 1) * P], rhs(k),
                                  start=k == 0, stop=k == kt - 1)
                        k += 1
                last.then_inc(proj.full_sem, 1)

    def token_tiles(name, part, lhs, toks=4):
        for q in range(4):
            chunk = c.first_chunk[name] + 4 * part + q
            pe.wait_ge(*c.chunk_landed(chunk))
            for t in range(toks):
                key = (name, toks * part + t)
                bank = open_bank(proj, key) if q == 0 else proj.bank(key)
                for i in range(2):
                    k = 2 * q + i
                    last = mm(bank, lhs(k, t), c.slot(chunk)[:, i * S:(i + 1) * S], start=k == 0, stop=k == 7)
                if q == 3:
                    last.then_inc(proj.full_sem, 1)

    def sum_squares(key, ready, tile, count, n=S):
        bank = open_bank(mix, key)
        for k in range(count):
            pe.wait_ge(*ready(k))
            last = mm(bank[:, 0:n], c.square("ones"), tile(k), start=k == 0, stop=k == count - 1)
        last.then_inc(mix.full_sem, 1)

    def norm(r):
        sum_squares(("ss", r), lambda k: (s["sq_ready"], 8 * r + k + 1), lambda k: T(SQ0 + k), KD)

    def swap(key, name, src):
        mm(open_bank(mix, key), c.square(name), src, start=True, stop=True).then_inc(mix.full_sem, 1)

    def h_ready(r):
        return lambda k: (s["h_ready"], h_count(r, k))

    def h_tok(k, t):
        return c.h[:, k * S + t * P:k * S + (t + 1) * P]

    def mixed(n, more=()):
        def ready(k):
            if k > 0:
                return None
            for w in more:
                pe.wait_ge(*w)
            return s["mixed"], n
        return ready

    pe.wait_ge(s["setup"], 16 * 8)
    norm(0)
    for t in range(6):
        if t < 5:
            feature_tile(*(("iq", t) if t < 4 else ("ik", 0)), H, ready=h_ready(0))
        if t >= 1:
            pe.wait_ge(*proj.emptied(("iq", t - 1) if t < 5 else ("ik", 0)))
            swap(("rot_i", t - 1), "swap32", T(5 + t - 1))
        if t == 4:
            for n in range(NB):
                bank = open_bank(proj, ("iw", n))
                for k in range(KD):
                    last = mm(bank[:, 0:8], h_tok(k, n), c.wsmall[:, 32 * k + 16:32 * k + 24], start=k == 0, stop=k == 7)
                last.then_inc(proj.full_sem, 1)
            bank = open_bank(proj, ("glow", 0))
            for k in range(KD):
                last = mm(bank[0:16, :], c.wsmall[:, 32 * k:32 * k + 16], H(k), start=k == 0, stop=k == 7)
            last.then_inc(proj.full_sem, 1)
    pe.wait_ge(s["iq_ready"], 5)
    for b in range(1, NB):
        for h in range(8):
            r, n = 64 * (h % 2), P * (b + 1)
            q = T(h // 2)[r:r + 64, b * P:(b + 1) * P]
            mm(open_bank(mix, ("idx", b, h))[:, 0:n], q, T(4)[r:r + 64, 0:n], start=True, stop=True).then_inc(mix.full_sem, 1)
    pe.wait_ge(*proj.emptied(("glow", 0)))
    for t in range(2):
        mm(open_bank(mix, ("gate", t)), c.gate_up[0:16, t * P:(t + 1) * P], T(53)[0:16, :], start=True, stop=True) \
            .then_inc(mix.full_sem, 1)
    for name in ("gr", "gq", "gk"):
        for t in range(STAGE[name][2]):
            feature_tile(name, t, H)
    token_tiles("gv", 0, h_tok)
    token_tiles("dv", 0, h_tok)
    for t in range(10):
        if t < 8:
            feature_tile("dq" if t < 4 else "dk", t % 4, H)
        if 1 <= t <= 8:
            pe.wait_ge(*proj.emptied(("dq" if t <= 4 else "dk", (t - 1) % 4)))
            mm(open_bank(mix, ("stat_d", t - 1)), c.square("ones"), T(48 + (t - 1) % 2), start=True, stop=True).then_inc(mix.full_sem, 1)
        if t >= 2:
            pe.wait_ge(s["head_normed"], t - 1)
            swap(("rot_d", t - 2), "swap64", T(38 + t - 2))
    pe.wait_ge(s["gla_ready"], 2)
    for t in range(2):
        bank = open_bank(mix, ("kdt", t))
        for n in range(NB):
            last = nc.tensor.transpose(bank[:, n * P:(n + 1) * P], T(28 + t)[:, n * P:(n + 1) * P], c.square("ident"))
        last.then_inc(mix.full_sem, 1)
    for h in range(4):
        bank, r = open_bank(mix, ("att", h)), 64 * (h % 2)
        for n in range(NB):
            w = slice(n * P, (n + 1) * P)
            last = mm(bank[:, w], T(54 + h // 2)[r:r + 64, w], T(58 + h // 2)[r:r + 64, w], start=True, stop=True)
        last.then_inc(mix.full_sem, 1)
    for t in range(2):
        pe.wait_ge(*mix.emptied(("kdt", t)))
        for e in range(2):
            bank = open_bank(mix, ("kv", t, e))
            for n in range(NB - e):
                for hh in range(2):
                    last = mm(bank[64 * hh:64 * hh + 64, n * P:(n + 1) * P],
                              T(14 + t)[64 * e:64 * e + 64, n * P + 64 * hh:n * P + 64 * hh + 64],
                              T(30 + n)[64 * e:64 * e + 64, (2 * t + hh) * P:(2 * t + hh + 1) * P], start=True, stop=True)
            last.then_inc(mix.full_sem, 1)
    for h in range(5):
        if h < 4:
            t, r = h // 2, 64 * (h % 2)
            pe.wait_ge(*mix.emptied(("att", h)))
            pe.wait_ge(s["state_ready"], 7 * (t + 1))
            bank = open_bank(mix, ("o", h))
            for n in range(NB):
                w = slice(n * P, (n + 1) * P)
                mm(bank[:, w], T(30 + n)[:, h * P:(h + 1) * P], T(ATT[h])[:, w], start=n == 0, stop=False, skip_group_check=True)
                for ch in (2 * n, 2 * n + 1):
                    if ch > 0:
                        w = slice(ch * CHUNK, (ch + 1) * CHUNK)
                        last = mm(bank[:, w], T(5 + 2 * t, 2)[r:r + 64, ch * P:(ch + 1) * P], T(26 + t)[r:r + 64, w],
                                  start=False, stop=ch == NCH - 1, skip_group_check=True)
            last.then_inc(mix.full_sem, 1)
        if h >= 1:
            pe.wait_ge(*mix.emptied(("o", h - 1)))
            mm(open_bank(mix, ("stat_o", h - 1)), c.square("ones"), T(48 + (h - 1) % 2), start=True, stop=True).then_inc(mix.full_sem, 1)
    units = [(b, h) for b in range(NB) for h in range(4)]
    pe.wait_ge(s["head_roped"], 8)
    for n in range(len(units) + 2):
        if n < 16:
            b, h = units[n]
            mm(open_bank(mix, ("qk", b, h))[:, 0:P * (b + 1)], T(38 + h)[:, b * P:(b + 1) * P], T(42 + h)[:, 0:P * (b + 1)],
               start=True, stop=True).then_inc(mix.full_sem, 1)
        if 1 <= n <= 16:
            b, h = units[n - 1]
            pe.wait_ge(s["pn_ready"], n)
            bank = open_bank(mix, ("pT", b, h))
            for j in range(b + 1):
                last = nc.tensor.transpose(bank[:, j * P:(j + 1) * P], T((n - 1) % 2)[:, j * P:(j + 1) * P], c.square("ident"))
            last.then_inc(mix.full_sem, 1)
        if n >= 2:
            b, h = units[n - 2]
            pe.wait_ge(*mix.emptied(("pT", b, h)))
            bank = open_bank(mix, ("av", b, h))
            for j in range(b + 1):
                last = mm(bank[:, 0:P], T(34 + j)[:, h * P:(h + 1) * P], T(2 + n % 2)[:, j * P:(j + 1) * P], start=j == 0, stop=j == b)
            last.then_inc(mix.full_sem, 1)
    feature_loop("abo", H, mixed(4, [mix.emptied(("av", NB - 1, 3))]))

    def feed_forward(r, up, down, mid_count=None):
        norm(r)
        feature_loop(up, H, h_ready(r))
        use0 = proj.number[(up, 0)]

        def mid(k):
            if k not in (0, 18, 20, 21):
                return None
            k = 17 if k == 0 else 19 if k == 18 else k
            if mid_count is not None:
                return s["mid_ready"], 2 + mid_count + k + 1
            return proj.emptied((up, 2 * k + 1))
        feature_loop(down, T, mid)

    feed_forward(1, "up0", "dn0")
    norm(2)
    for t in range(4):
        feature_tile("cu", t, H, ready=h_ready(2))
    for t in range(9):
        if t < 8:
            feature_tile("sq" if t < 4 else "sk", t % 4, H)
        if t >= 1:
            pe.wait_ge(*proj.emptied(("sq" if t <= 4 else "sk", (t - 1) % 4)))
            mm(open_bank(mix, ("stat_s", t - 1)), c.square("ones"), T(20 + (t - 1) % 2), start=True, stop=True).then_inc(mix.full_sem, 1)
    token_tiles("sv", 0, h_tok)
    for g in range(4):
        pe.wait_ge(s["pooled"], g + 1)
        if g == 0:
            pe.wait_ge(s["pool_loaded"], 16)
        mm(open_bank(mix, ("pool", g)), c.pool_w[:, g * P:(g + 1) * P], T(6 + g), start=True, stop=True).then_inc(mix.full_sem, 1)
    pe.wait_ge(s["head_normed"], 8 + 4 + 8)
    pe.wait_ge(*proj.emptied(("sv", 3)))
    for h in range(6):
        if h < 4:
            for j in range(NB):
                mm(open_bank(mix, ("z", h, j))[:, 0:S - P * j], T(14 + h)[:, j * P:(j + 1) * P], T(10 + h)[:, j * P:S],
                   start=True, stop=True).then_inc(mix.full_sem, 1)
        if 1 <= h <= 4:
            pe.wait_ge(s["sp_ready"], h)
            sp = T(34 + 3 * ((h - 1) % 2), 3)
            for j in range(NB):
                bank = open_bank(mix, ("cum", h - 1, j))
                last = mm(bank[:, 0:S - P * j], c.square("later"), sp[:, TRI[j]:TRI[j + 1]], start=True, stop=j == NB - 1, skip_group_check=True)
                for i in range(j + 1, NB):
                    last = mm(bank[:, P * (i - j):S - P * j], c.square("ones"), sp[:, TRI[i]:TRI[i + 1]], start=False,
                              stop=i == NB - 1, skip_group_check=True)
                last.then_inc(mix.full_sem, 1)
        if h >= 2:
            pe.wait_ge(s["w_ready"], h - 1)
            w = T(40 + 3 * (h % 2), 3)
            bank = open_bank(mix, ("sb", h - 2))
            for j in range(NB):
                last = mm(bank[:, P * j:S], T(24 + j)[:, (h - 2) * P:(h - 1) * P], w[:, TRI[j]:TRI[j + 1]], start=j == 0,
                          stop=j == NB - 1, skip_group_check=True)
            last.then_inc(mix.full_sem, 1)
    feature_loop("cdo", H, lambda k: mix.emptied(("sb", 3)) if k == 0 else None)
    feed_forward(3, "up1", "dn1")
    norm(4)
    for t in range(8):
        feature_tile("mqk", t, H, ready=h_ready(4))
    for part in range(2):
        token_tiles("mv", part, h_tok)
    feature_loop("mo", H, lambda k: None)
    for n, key in enumerate((("mi", 0), ("mf", 0))):
        bank = open_bank(proj, key)
        for k in range(KD):
            last = mm(bank[0:4, :], c.wsmall[:, 32 * k + 24 + 4 * n:32 * k + 28 + 4 * n], H(k), start=k == 0, stop=k == 7)
        last.then_inc(proj.full_sem, 1)
    pe.wait_ge(s["m_rows"], 1)
    bank = open_bank(mix, ("acol", 0))
    for j in range(NB):
        last = nc.tensor.transpose(bank[:, 4 * j:4 * j + 4], T(29)[0:4, j * P:(j + 1) * P], c.square("ident")[0:4, 0:4])
    last.then_inc(mix.full_sem, 1)
    pe.wait_ge(s["m_guard"], 1)
    for h in range(4):
        for n, row in enumerate((T(31), T(28))):
            mm(open_bank(mix, ("mbc", h, n)), c.const("sel")[0:4, h * P:(h + 1) * P], row[0:4, :], start=True, stop=True) \
                .then_inc(mix.full_sem, 1)
        if h == 0:
            pe.wait_ge(s["conv_act"], 8)
        for j in range(NB):
            mm(open_bank(mix, ("ms", h, j))[:, 0:S - P * j], T(4 + h)[:, j * P:(j + 1) * P], T(h)[:, P * j:S],
               start=True, stop=True).then_inc(mix.full_sem, 1)
        p = T(38 + 3 * (h % 2), 3)
        for n in range(3):
            bank = open_bank(mix, ("mn", h, n) if n < 2 else ("md", h))
            for j in range(NB):
                if n == 0:
                    pe.wait_ge(*mix.emptied(("ms", h, j)))
                v = T(8 + 2 * j, 2)[:, (2 * h + n) * P:(2 * h + n + 1) * P] if n < 2 else c.square("ones")
                last = mm(bank[:, P * j:S], v, p[:, TRI[j]:TRI[j + 1]], start=j == 0, stop=j == NB - 1, skip_group_check=True)
            last.then_inc(mix.full_sem, 1)
        sum_squares(("stat_m", h), lambda k: (s["hsq_ready"], 2 * h + k + 1), lambda k: T(56 + k), 2)
    feature_loop("mout", H, mixed(MIXED_M))
    feed_forward(5, "up2", "dn2", 0)
    norm(6)
    feature_loop("ca", H, h_ready(6))
    sum_squares(("lnm", 0), lambda k: (s["u_ready"], k + 1), lambda k: T(11 + k), KD)
    sum_squares(("lnv", 0), lambda k: (s["u_sq"], k + 1), lambda k: T(SQ0 + k), KD)
    feature_loop("cout", H, lambda k: (s["u_act"], k + 1))
    feed_forward(7, "up3", "dn3", FT)
    norm(8)
    sum_squares(("ssc", 0), lambda k: (s["u_sq"], 8 + k + 1), lambda k: T(8, 4)[:, k * CTX:(k + 1) * CTX], KD, n=CTX)
    norm(9)
    hc = lambda k: T(4, 4)[:, k * CTX:(k + 1) * CTX]
    for t in range(4):
        feature_tile("ck", t, hc, n=CTX, ready=lambda k: (s["hc_ready"], k + 1))
    token_tiles("cv", 0, lambda k, t: hc(k)[:, t * P:(t + 1) * P], toks=2)
    for t in range(9):
        if t < 8:
            feature_tile("rk" if t < 4 else "rq", t % 4, H, ready=h_ready(9))
        if t >= 1:
            pe.wait_ge(*proj.emptied(("rk" if t <= 4 else "rq", (t - 1) % 4)))
            swap(("rot_r", t - 1), "swap64", T(24 + (t - 1) % 2))
    token_tiles("rv", 0, h_tok)
    token_tiles("fv", 0, h_tok)
    for name in ("ru", "rg"):
        for t in range(STAGE[name][2]):
            feature_tile(name, t, H)
    pe.wait_ge(s["head_roped"], 16)
    for h in range(4):
        for j in range(6):
            keys = T(16 + h)[:, j * P:(j + 1) * P] if j < 4 else T(12, 2)[:, h * CTX + (j - 4) * P:h * CTX + (j - 3) * P]
            mm(open_bank(mix, ("rs", h, j)), keys, T(20 + h), start=True, stop=True).then_inc(mix.full_sem, 1)
        bank = open_bank(mix, ("rout", h))
        for j in range(6):
            pe.wait_ge(*mix.emptied(("rs", h, j)))
            v = T(27 + j) if j < 4 else T(14 + j - 4)
            last = mm(bank, v[:, h * P:(h + 1) * P], T(RP[j]), start=j == 0, stop=j == 5)
        last.then_inc(mix.full_sem, 1)
        pe.wait_ge(*mix.emptied(("rout", h)))
        mm(open_bank(mix, ("stat_r", h)), c.square("ones"), T(58), start=True, stop=True).then_inc(mix.full_sem, 1)
    pe.wait_ge(s["dft_loaded"], 32)
    for t in range(2):
        for n in range(2):
            bank = open_bank(mix, ("dftl", t, n))
            for j in range(NB):
                last = mm(bank, T(31, 2)[:, j * 256 + t * P:j * 256 + (t + 1) * P], T(4 * n + j), start=j == 0, stop=j == NB - 1)
            last.then_inc(mix.full_sem, 1)
    for t in range(2):
        pe.wait_ge(*mix.emptied(("dftl", t, 1)))
        bank = open_bank(mix, ("four", t))
        mm(bank, c.square("dft_cos"), T(53 + t), start=True, stop=False)
        mm(bank, c.square("dft_sin"), T(55 + t), start=False, stop=True).then_inc(mix.full_sem, 1)
    pe.wait_ge(s["vs_ready"], 1)
    pe.wait_ge(s["late"], 16 * 3)
    for t in range(2):
        bank = open_bank(mix, ("sgu", t))
        for n in range(NB):
            for g in range(2):
                last = mm(bank[64 * g:64 * g + 64, n * P:(n + 1) * P],
                          T(33, 2)[:, n * 256 + (2 * t + g) * 64:n * 256 + (2 * t + g) * 64 + 64],
                          c.sgu_w[:, (2 * t + g) * P:(2 * t + g + 1) * P], start=True, stop=True)
        last.then_inc(mix.full_sem, 1)
    use0, chunk0 = proj.number[("br", 0)], c.first_chunk["br"]
    pe.wait_ge(s["mixed"], MIXED_M + 4)
    pe.wait_ge(*mix.emptied(("four", 1)))
    pe.wait_ge(s["sgu_ready"], 2)
    with pe.Fori(0, 4) as i:
        for j in range(12):
            u, n, g = use0 + j, j // 6, j % 6
            pe.wait_ge(proj.empty_sem[u % RING], i * 3 + u // RING)
            ch = chunk0 + 4 * n + min(g, 3)
            pe.wait_ge(c.landed[ch % RING], i * 32 + 16 * (ch // RING + 1))
            srcs = [H(k) for k in range(8)] if g < 3 else [[T(8 + k) for k in range(4)], [T(57), T(58)], [T(59), T(60)]][g - 3]
            at = 0 if g < 3 else (0, 4, 6)[g - 3]
            for k, src in enumerate(srcs):
                last = mm(proj.banks[:, u % RING, :], c.slot(ch)[:, (at + k) * P:(at + k + 1) * P], src,
                          start=k == 0, stop=k == len(srcs) - 1)
            last.then_inc(proj.full_sem, 1)
    feature_loop("ro", lambda k: T(16 + k), lambda k: (s["merged"], k + 1))
    sum_squares(("ssy", 0), lambda k: proj.emptied(("ro", k)), lambda k: T(SQ0 + k), KD)
    norm(10)
    feature_loop("upr", H, h_ready(10))
    feature_loop("dnr", T, lambda k: (s["mlp_mid"], 4 + (28 if k == 0 else k + 1)) if k == 0 or k >= 28 else None)
    sum_squares(("ssy", 1), lambda k: proj.emptied(("dnr", k)), lambda k: T(SQ0 + k), KD)


ATT = (16, 20, 21, 9)
TRI = (0, 512, 896, 1152, 1280)
RP = (24, 25, 26, 53, 54, 55)
MIXED_M = 12



def scalar_program(nc, act, c):
    s, proj, mix, T, H, X = c.sem, c.proj, c.mix, c.T, c.H, c.X
    st = Steps(act, s["act_chain"])

    def f(out, in_, func, **kw):
        return nc.scalar.activation(out, in_, func, **kw)

    def copy_out(ring, key, dst, func=ACT.Copy, rows=P, n=S, **kw):
        act.wait_ge(*ring.filled(key))
        st.last(f(dst, ring.bank(key)[0:rows, 0:n], func, **kw), ring.emptied(key))

    eps = c.const("eps")

    def root(key, dst, count, n=S):
        copy_out(mix, key, dst, ACT.Sqrt, n=n, scale=1.0 / count, bias=eps)

    def norm(r, h_out=True):
        for k in range(KD):
            if r == 0:
                act.wait_ge(s["x_loaded"], 16)
            elif r in NORM_AFTER:
                act.wait_ge(*proj.emptied((NORM_AFTER[r], k)))
            else:
                act.wait_ge(s["x_ready"], 8 * (r - 9) + k + 1)
            st.done(f(T(SQ0 + k), X(k), ACT.Square), s["sq_ready"])
        root(("ss", r), T(RSTD), D)
        if r in MODULATED:
            use, layer, part, ready = MODULATED[r]
            act.wait_ge(s["mod_ready"], ready)
            for k in range(KD):
                act.wait_ge(s["xn_ready"], 8 * list(MODULATED).index(r) + k + 1)
                f(H(k), H(k), ACT.Identity, scale=c.g(use, k), bias=c.m(layer, part, k)).then_inc(s["h_ready"], 1)

    def head_stat(ring, key, raw, sq):
        act.wait_ge(*ring.filled(key))
        f(raw, ring.bank(key), ACT.Copy)
        st.last(f(sq, ring.bank(key), ACT.Square), ring.emptied(key))

    act.wait_ge(s["setup"], 16 * 8)
    st.done(f(c.cond[:, 0:D], c.cond[:, 0:D], ACT.Silu), s["cond_ready"])
    for n in range(4):
        act.wait_ge(s["pos_ready"], n + 1)
        st.done(f(T(10 + n), T(10 + n), ACT.Sin), s["trig_ready"])
    norm(0)
    for t in range(5):
        key = ("iq", t) if t < 4 else ("ik", 0)
        copy_out(proj, key, T(5 + t))
    for n in range(NB):
        copy_out(proj, ("iw", n), c.small[:, 8 + 8 * n:16 + 8 * n], n=8, scale=(8 ** -0.5) * (64 ** -0.5))
    copy_out(proj, ("glow", 0), T(53)[0:16, :], rows=16)
    n = 0
    for b in range(1, NB):
        for h in range(8):
            if n >= 2:
                act.wait_ge(s["idx_used"], n - 1)
            copy_out(mix, ("idx", b, h), T(20 + n % 2)[:, 0:P * (b + 1)], ACT.Relu, n=P * (b + 1))
            n += 1
    for t in range(2):
        act.wait_ge(*mix.filled(("gate", t)))
        f(T(54 + t), mix.bank(("gate", t)), ACT.Identity, bias=c.v("gla_gate_b", t))
        st.last(f(T(56 + t), mix.bank(("gate", t)), ACT.Abs, bias=c.v("gla_gate_b", t)), mix.emptied(("gate", t)))
    st.link(f(T(56, 2), T(56, 2), ACT.Exp, scale=-1.0))
    st.done(f(T(56, 2), T(56, 2), ACT.Ln, bias=c.const("one")), s["gate_ready"])
    for t in range(4):
        copy_out(proj, ("gr", t), T(22 + t), ACT.Silu)
    for t in range(2):
        copy_out(proj, ("gq", t), T(26 + t), scale=64 ** -0.5)
    for t in range(2):
        copy_out(proj, ("gk", t), T(28 + t))
    for t in range(4):
        copy_out(proj, ("gv", t), T(30 + t))
    for t in range(4):
        copy_out(proj, ("dv", t), T(34 + t))
    for t in range(2):
        act.wait_ge(s["span_ready"], t + 1)
        f(T(E_GLA[t][0]), T(58 + t), ACT.Exp, scale=1 / 16)
        f(T(E_GLA[t][1]), T(58 + t), ACT.Exp, scale=-1 / 16)
        f(T(E_GLA[t][2]), T(54 + t), ACT.Exp, scale=1 / 16)
        f(T(E_GLA[t][3]), T(56 + t), ACT.Exp, scale=1 / 16)
        last = T(56 + t).rearrange("p (n c) -> p n c", c=CHUNK)[:, :, CHUNK - 1:CHUNK]
        st.done(f(c.small[:, 40 + 8 * t:48 + 8 * t].unsqueeze(2), last, ACT.Exp, scale=1 / 16), s["decay_ready"])

    def d_key(t):
        return ("dq" if t < 4 else "dk", t % 4)

    for t in range(9):
        if t < 8:
            if t >= 2:
                act.wait_ge(s["head_normed"], t - 1)
            head_stat(proj, d_key(t), T(46 + t % 2), T(48 + t % 2))
        if t >= 1:
            root(("stat_d", t - 1), T(50 + (t - 1) % 2), P)
    for t in range(2):
        copy_out(mix, ("kdt", t), T(14 + t))
    for h in range(5):
        if h < 4:
            if h >= 2:
                act.wait_ge(s["head_normed"], 8 + h - 1)
            head_stat(mix, ("o", h), T(46 + h % 2), T(48 + h % 2))
        if h >= 1:
            root(("stat_o", h - 1), T(50 + (h - 1) % 2), P)
    units = [(b, h) for b in range(NB) for h in range(4)]
    for n in range(len(units) + 2):
        if n < 16:
            b, h = units[n]
            act.wait_ge(s["max_ready"], n + 1)
            z = T(n % 2)[:, 0:P * (b + 1)]
            st.done(f(z, z, ACT.Exp, scale=P ** -0.5, bias=c.small[:, 56 + n % 2:57 + n % 2],
                      accum_out=c.small[:, 58 + n % 2:59 + n % 2]), s["p_ready"])
        if 1 <= n <= 16:
            b, h = units[n - 1]
            if n >= 3:
                act.wait_ge(*mix.filled(("av", *units[n - 3])))
            copy_out(mix, ("pT", b, h), T(2 + (n - 1) % 2)[:, 0:P * (b + 1)], n=P * (b + 1))
        if n >= 2:
            b, h = units[n - 2]
            copy_out(mix, ("av", b, h), H(4 + h)[:, b * P:(b + 1) * P], n=P)

    def swiglu(up):
        u0 = proj.number[(up, 0)]
        with act.Fori(0, 2 * FT // 4) as i:
            for p in range(2):
                u = u0 + 2 * p
                act.wait_ge(proj.full_sem, i * 4 + u + 1)
                act.wait_ge(proj.empty_sem[(u + 1) % RING], i + (u + 1) // RING)
                f(T(22 + p), proj.banks[:, u % RING, :], ACT.Silu).then_inc(proj.empty_sem[u % RING], 1)

    norm(1)
    swiglu("up0")
    norm(2)
    for t in range(4):
        copy_out(proj, ("cu", t), T(t))

    def s_key(t):
        return ("sq" if t < 4 else "sk", t % 4)

    for t in range(9):
        if t < 8:
            if t >= 2:
                act.wait_ge(s["head_normed"], 12 + t - 1)
            head_stat(proj, s_key(t), T(18 + t % 2), T(20 + t % 2))
        if t >= 1:
            root(("stat_s", t - 1), T(22 + (t - 1) % 2), P)
    for t in range(4):
        copy_out(proj, ("sv", t), T(24 + t))
    for g in range(4):
        copy_out(mix, ("pool", g), H(g), scale=c.v("pool_scale", g))
    for h in range(6):
        if h < 4:
            z, l = T(28 + 3 * (h % 2), 3), T(34 + 3 * (h % 2), 3)
            for j in range(NB):
                act.wait_ge(*mix.filled(("z", h, j)))
                bank = mix.bank(("z", h, j))[:, 0:S - P * j]
                f(z[:, TRI[j]:TRI[j + 1]], bank, ACT.Copy, scale=P ** -0.5)
                st.last(f(l[:, TRI[j]:TRI[j + 1]], bank, ACT.Abs, scale=P ** -0.5), mix.emptied(("z", h, j)))
            l = l[:, 0:TRI[4]]
            st.link(f(l, l, ACT.Exp, scale=-1.0))
            st.done(f(l, l, ACT.Ln, bias=c.const("one")), s["z_ready"])
        if 1 <= h <= 4:
            act.wait_ge(*mix.emptied(("cum", h - 1, 3)))
            z, w = T(28 + 3 * ((h - 1) % 2), 3)[:, 0:TRI[4]], T(40 + 3 * ((h - 1) % 2), 3)[:, 0:TRI[4]]
            st.done(f(w, z, ACT.Exp), s["w_ready"])
        if h >= 2:
            copy_out(mix, ("sb", h - 2), H(4 + h - 2))
    norm(3)
    act.wait_ge(s["cond_loaded"], 32)
    st.done(f(c.cond[:, :], c.cond[:, :], ACT.Silu), s["cond_ready"])
    swiglu("up1")
    norm(4)
    for t in range(9):
        if t < 8:
            act.wait_ge(*proj.filled(("mqk", t)))
            st.done(f(T(t), proj.bank(("mqk", t)), ACT.Identity, scale=c.v("m_conv_w_2", 24 + t), bias=c.v("m_conv_b_2", t)), s["conv_init"])
        if t >= 1:
            act.wait_ge(*proj.emptied(("mqk", t - 1)))
            st.done(f(T(t - 1), T(t - 1), ACT.Silu), s["conv_act"])
    for t in range(8):
        copy_out(proj, ("mv", t), T(8 + 2 * (t % 4) + t // 4))
    for t in range(8):
        copy_out(proj, ("mo", t), T(16 + t), ACT.Sigmoid)
    copy_out(proj, ("mi", 0), T(24)[0:4, :], ACT.Identity, rows=4, bias=c.m_bias[0:4, 0:1])
    act.wait_ge(*proj.filled(("mf", 0)))
    f(T(25)[0:4, :], proj.bank(("mf", 0))[0:4, :], ACT.Identity, bias=c.m_bias[0:4, 1:2])
    st.last(f(T(26)[0:4, :], proj.bank(("mf", 0))[0:4, :], ACT.Abs, bias=c.m_bias[0:4, 1:2]), proj.emptied(("mf", 0)))
    st.link(f(T(26)[0:4, :], T(26)[0:4, :], ACT.Exp, scale=-1.0))
    st.done(f(T(26)[0:4, :], T(26)[0:4, :], ACT.Ln, bias=c.const("one")[0:4, :]), s["m_gate"])
    act.wait_ge(s["m_rows"], 1)
    st.done(f(T(28)[0:4, :], T(28)[0:4, :], ACT.Exp, scale=-1.0), s["m_guard"])
    copy_out(mix, ("acol", 0), c.small[:, 64:80], n=16)
    for h in range(4):
        copy_out(mix, ("mbc", h, 0), T(32 + h % 2))
        copy_out(mix, ("mbc", h, 1), T(34 + h % 2))
        e = T(EH[h % 2], 3)[:, 0:TRI[4]]
        act.wait_ge(s["e_arg"], h + 1)
        st.done(f(e, e, ACT.Exp), s["e_ready"])
        copy_out(mix, ("md", h), T(47), ACT.Abs)
        for k in range(2):
            act.wait_ge(s["hm_ready"], 2 * h + k + 1)
            st.done(f(T(56 + k), T(48 + 2 * (h % 2) + k), ACT.Square), s["hsq_ready"])
        root(("stat_m", h), T(58), 2 * P)

    def conv_ffn(up, layer, base):
        u0 = proj.number[(up, 0)]
        w0 = VCOL["f_conv_w_2"] + 3 * 2 * FT * layer + 2 * 2 * FT
        b0 = VCOL["f_conv_b_2"] + 2 * FT * layer
        with act.Fori(0, 2 * FT // 4) as i:
            for p in range(2):
                act.wait_ge(s["mid_ready"], i * 2 + base + p + 1)
                for g in range(2):
                    u = u0 + 2 * p + g
                    act.wait_ge(proj.full_sem, i * 4 + u + 1)
                    col = FT * g + p
                    f(T(22 + 2 * p + g), proj.banks[:, u % RING, :], ACT.Identity,
                      scale=c.vec[:, bass.ds(i * 2 + (w0 + col), 1)], bias=c.vec[:, bass.ds(i * 2 + (b0 + col), 1)]) \
                        .then_inc(s["conv_init"], 1)
                u = u0 + 2 * p
                act.wait_ge(proj.empty_sem[u % RING], i + u // RING + 1)
                f(T(22 + 2 * p), T(22 + 2 * p), ACT.Silu).then_inc(s["conv_act"], 1)

    norm(5)
    conv_ffn("up2", 0, 0)
    norm(6)
    for t in range(8):
        if t >= 2:
            act.wait_ge(*proj.emptied(("ca", 2 * t - 4)))
        copy_out(proj, ("ca", 2 * t + 1), T(9 + t % 2), ACT.Sigmoid, bias=c.v("c_b_in_2", 8 + t))
    for k in range(KD):
        act.wait_ge(s["u_centred"], k + 1)
        st.done(f(T(SQ0 + k), T(11 + k), ACT.Square), s["u_sq"])
    root(("lnv", 0), T(RSTD), D)
    for k in range(KD):
        act.wait_ge(s["u_normed"], k + 1)
        st.done(f(H(k), T(11 + k), ACT.Silu, scale=c.v("c_ln_g_2", k), bias=c.v("c_ln_b_2", k)), s["u_act"])
    norm(7)
    conv_ffn("up3", 1, FT)
    norm(8)
    act.wait_ge(s["ctx_loaded"], 48)
    for k in range(KD):
        st.done(f(T(8, 4)[:, k * CTX:(k + 1) * CTX], T(0, 4)[:, k * CTX:(k + 1) * CTX], ACT.Square), s["u_sq"])
    root(("ssc", 0), T(12)[:, 0:CTX], D, n=CTX)
    act.wait_ge(s["mod_ready"], 5)
    for k in range(KD):
        act.wait_ge(s["u_centred"], 8 + k + 1)
        hc = T(4, 4)[:, k * CTX:(k + 1) * CTX]
        st.done(f(hc, hc, ACT.Identity, scale=c.g(6, k), bias=c.m(3, 0, k)), s["hc_ready"])
    act.wait_ge(s["late"], 16 * 3)
    st.link(f(c.small[:, 80:88], c.small[:, 0:8], ACT.Abs))
    st.link(f(c.small[:, 80:88], c.small[:, 80:88], ACT.Exp, scale=-1.0))
    st.done(f(c.small[:, 88:96], c.small[:, 80:88], ACT.Ln, bias=c.const("one")), s["lg_abs"])
    norm(9)
    for t in range(4):
        copy_out(proj, ("ck", t), T(12, 2)[:, t * CTX:(t + 1) * CTX], n=CTX, scale=P ** -0.5)
    for t in range(2):
        copy_out(proj, ("cv", t), T(14 + t))
    for t in range(8):
        if t >= 2:
            act.wait_ge(s["head_roped"], 8 + t - 1)
        copy_out(proj, ("rk" if t < 4 else "rq", t % 4), T(24 + t % 2), scale=P ** -0.5 if t < 4 else 1.0)
    for t in range(4):
        copy_out(proj, ("rv", t), T(27 + t))
    for t in range(4):
        act.wait_ge(*proj.filled(("fv", t)))
        f(T(31, 2)[:, t * 256:(t + 1) * 256], proj.bank(("fv", t))[:, 0:256], ACT.Copy)
        st.last(f(T(33, 2)[:, t * 256:(t + 1) * 256], proj.bank(("fv", t))[:, 256:512], ACT.Gelu_apprx_tanh), proj.emptied(("fv", t)))
    for t in range(2):
        copy_out(proj, ("ru", t), T(35 + t), ACT.Gelu_apprx_tanh)
    for t in range(4):
        copy_out(proj, ("rg", t), T(37 + t), ACT.Silu)
    act.wait_ge(s["vs_var"], 1)
    st.done(f(c.small[:, 96:112], c.small[:, 96:112], ACT.Sqrt, scale=1 / 64, bias=eps), s["vs_std"])
    for h in range(4):
        for n, (at, width) in enumerate(TABLES):
            act.wait_ge(s["table_arg"], 3 * h + n + 1)
            st.done(f(T(at, 2)[:, 0:width], T(at, 2)[:, 0:width], ACT.Exp), s["table_ready"])
        if h >= 1:
            act.wait_ge(s["mixed"], MIXED_M + h)
        head_stat(mix, ("rout", h), T(57), T(58))
        root(("stat_r", h), T(59), P)
    for t in range(2):
        for n in range(2):
            copy_out(mix, ("dftl", t, n), T(53 + 2 * n + t))
    act.wait_ge(s["mixed"], MIXED_M + 4)
    for t in range(2):
        copy_out(mix, ("four", t), T(57 + t))
    u0 = proj.number[("br", 0)]
    with act.Fori(0, 4) as i:
        for n in range(2):
            for g in range(3):
                u = u0 + 6 * n + g
                act.wait_ge(proj.full_sem, i * 12 + u + 1)
                act.wait_ge(proj.empty_sem[(u + 3) % RING], i * 3 + ((u + 3) // RING - 2))
                f(T(3 * n + g), proj.banks[:, u % RING, :], ACT.Sigmoid).then_inc(proj.empty_sem[u % RING], 1)

    def post_norm(stage, r, y):
        for k in range(KD):
            act.wait_ge(*proj.filled((stage, k)))
            st.link(f(T(y + k), proj.bank((stage, k)), ACT.Copy))
            st.last(f(T(SQ0 + k), T(y + k), ACT.Square), proj.emptied((stage, k)))
        root(("ssy", r), T(RSTD), D)

    post_norm("ro", 0, 27)
    norm(10)
    u0 = proj.number[("upr", 0)]
    with act.Fori(0, F3T // 4) as i:
        for j in range(4):
            u = u0 + j
            act.wait_ge(proj.full_sem, i * 4 + u + 1)
            act.wait_ge(s["mlp_mid"], i * 4 + j + 1)
            f(T(32 + j), proj.banks[:, u % RING, :], ACT.Relu).then_inc(proj.empty_sem[u % RING], 1)
    post_norm("dnr", 1, 32)


EH = (59, 44)
E_GLA = ((60, 61, 62, 63), (0, 1, 2, 3))
TABLES = ((43, SELF_W), (45, CTX_W), (61, CTX_W))



def vector_program(nc, dve, c):
    s, proj, mix, T, H, X, small = c.sem, c.proj, c.mix, c.T, c.H, c.X, c.small
    st = Steps(dve, s["dve_chain"])
    v = nc.vector

    def tt(out, a, b, op):
        return v.tensor_tensor(out, a, b, op)

    def ts(out, a, x, op0, y=None, op1=None):
        if op1 is None:
            return v.tensor_scalar(out, a, x, None, op0)
        return v.tensor_scalar(out, a, x, y, op0, op1)

    def stt(out, a, x, b, op0, op1):
        return v.scalar_tensor_tensor(out=out, in0=a, scalar=x, in1=b, op0=op0, op1=op1)

    def ada_row(chunk, cond, column):
        dve.wait_ge(c.ada_landed[chunk % ADA_RING], 16 * (chunk // ADA_RING + 1))
        w = c.ada[:, (chunk % ADA_RING) * D:(chunk % ADA_RING + 1) * D]
        v.tensor_tensor_reduce(w, w, cond, 1.0, 0.0, ALU.mult, ALU.add, column).then_inc(s["ada_used"], 1)
        dve.wait_ge(s["ada_used"], chunk + 1)

    def ada_rows(layer, first, n):
        for j in range(first, first + n):
            ada_row(48 * layer + j, c.cond[:, 0:D], c.mod[:, 48 * layer + j:48 * layer + j + 1])
        add_bias(layer, first, n, "ada_b", 48 * layer)

    def add_bias(layer, first, n, bias, at):
        cols = c.mod[:, 48 * layer + first:48 * layer + first + n]
        st.link(tt(cols, cols, c.v(bias, at + first, n), ALU.add))

    def gains(use, layer, part, w, at):
        st.done(stt(c.g(use, 0, 8), c.m(layer, part, 0, 8), 1.0, c.v(w, at, 8), ALU.add, ALU.mult), s["mod_ready"])

    def inverse(key, rt):
        dve.wait_ge(*mix.emptied(key))
        st.link(v.reciprocal(rt, rt))

    def norm(r):
        inverse(("ss", r), T(RSTD))
        for k in range(KD):
            if r in MODULATED:
                st.done(tt(H(k), X(k), T(RSTD), ALU.mult), s["xn_ready"])
            else:
                name, at = PLAIN[r]
                out = X(k) if r == 8 else H(k)
                ins = stt(out, X(k), c.v(name, at + k), T(RSTD), ALU.mult, ALU.mult)
                if r == 8:
                    st.done(ins, s["x_ready"])
                else:
                    ins.then_inc(s["h_ready"], 1)
                    dve.wait_ge(s["h_ready"], h_count(r, k))

    def residual(stage, gate=None, bias=None):
        for k in range(KD):
            key = (stage, k)
            dve.wait_ge(*proj.filled(key))
            if gate is not None:
                ins = stt(X(k), proj.bank(key), gate(k), X(k), ALU.mult, ALU.add)
            elif bias is not None:
                ins = stt(X(k), proj.bank(key), bias(k), X(k), ALU.add, ALU.add)
            else:
                ins = tt(X(k), proj.bank(key), X(k), ALU.add)
            st.last(ins, proj.emptied(key))

    dve.wait_ge(s["setup"], 16 * 8)
    st.link(v.tensor_copy(T(59), T(60).bitcast(I32)))
    for n in range(4):
        name, phase, out = ("q", "q", "i", "i")[n], (np.pi / 2, 0.0)[n % 2], T(10 + n)
        if n % 2 == 0:
            st.link(ts(T(61), T(59), c.const("freq_" + name), ALU.mult))
        st.link(ts(T(62), T(61), 1 / (2 * np.pi), ALU.mult, phase / (2 * np.pi), ALU.add))
        st.link(ts(T(62), T(62), ROUND, ALU.add, ROUND, ALU.subtract))
        st.link(stt(out, T(62), -TURN[0], T(61), ALU.mult, ALU.add))
        st.link(stt(out, T(62), -TURN[1], out, ALU.mult, ALU.add))
        st.link(stt(out, T(62), -TURN[2], out, ALU.mult, ALU.add))
        if phase:
            st.link(ts(out, out, phase, ALU.add))
        st.done(ts(out, out, 3.1415925, ALU.min, -3.1415925, ALU.max), s["pos_ready"])
    dve.wait_ge(s["cond_ready"], 1)
    ada_rows(0, 0, 16)
    gains(0, 0, 1, "mix_norm", 0)
    norm(0)
    dve.wait_ge(s["trig_ready"], 4)
    for n, name in ((1, "q"), (3, "i")):
        st.link(ts(T(10 + n), T(10 + n), c.const("sign_" + name), ALU.mult))

    def rotate(key, dst, src, cos, sin, tmp, sem):
        dve.wait_ge(*mix.filled(key))
        st.last(tt(tmp, mix.bank(key), sin, ALU.mult), mix.emptied(key))
        st.link(tt(dst, src, cos, ALU.mult))
        st.done(tt(dst, dst, tmp, ALU.add), sem)

    for t in range(5):
        rotate(("rot_i", t), T(t), T(5 + t), T(12), T(13), T(60), s["iq_ready"])
    n = 0
    for b in range(1, NB):
        score, width = T(13 + b), P * (b + 1)
        if b == 1:
            dve.wait_ge(*proj.emptied(("iw", 3)))
        for h in range(8):
            rel, w = T(20 + n % 2), small[:, 8 + 8 * b + h:9 + 8 * b + h]
            dve.wait_ge(*mix.emptied(("idx", b, h)))
            if h == 0:
                st.link(ts(score[:, 0:P * b], rel[:, 0:P * b], w, ALU.mult))
                st.done(stt(score[:, P * b:width], rel[:, P * b:width], w, c.square("causal_neg"), ALU.mult, ALU.add), s["idx_used"])
            else:
                st.done(stt(score[:, 0:width], rel[:, 0:width], w, score[:, 0:width], ALU.mult, ALU.add), s["idx_used"])
            n += 1
    top8 = small[:, 120:128]
    for b in range(1, NB):
        score, width = T(13 + b)[:, 0:P * (b + 1)], P * (b + 1)
        for _ in range(TOPK // 8):
            st.link(v.max(top8, score))
            st.link(v.match_replace(score, top8, score, TAKEN))
        st.link(ts(T(16 + b)[:, 0:width], score, -2e38, ALU.is_gt, NEG, ALU.mult))
    ada_rows(0, 16, 32)
    gains(1, 0, 4, "ffn_norm", 0)
    dve.wait_ge(s["gate_ready"], 1)
    for t in range(2):
        g, b, mid = T(54 + t), T(56 + t), T(58 + t)
        st.link(stt(g, g, 0.0, b, ALU.min, ALU.subtract))
        st.link(v.tensor_tensor_scan(b, c.const("reset"), g, 0.0, ALU.mult, ALU.add))
        bn = b.rearrange("p (n c) -> p n c", c=CHUNK)
        st.link(tt(mid.rearrange("p (n c) -> p n c", c=CHUNK), bn,
                   bn[:, :, CHUNK // 2 - 1:CHUNK // 2].broadcast_to([P, NCH, CHUNK]), ALU.subtract))
        st.done(tt(g.rearrange("p (n c) -> p n c", c=CHUNK), bn[:, :, CHUNK - 1:CHUNK].broadcast_to([P, NCH, CHUNK]),
                   bn, ALU.subtract), s["span_ready"])
    for h in range(4):
        st.link(v.memset(T(ATT[h]), 0.0))
    dve.wait_ge(*proj.emptied(("gk", 1)))
    for t in range(2):
        dve.wait_ge(s["decay_ready"], t + 1)
        e = [T(i) for i in E_GLA[t]]
        st.link(tt(T(58 + t), T(26 + t), e[0], ALU.mult))
        st.link(tt(T(54 + t), T(28 + t), e[1], ALU.mult))
        st.link(tt(T(28 + t), T(28 + t), e[2], ALU.mult))
        st.done(tt(T(26 + t), T(26 + t), e[3], ALU.mult), s["gla_ready"])
    for t in range(9):
        if t < 8:
            inverse(("stat_d", t), T(50 + t % 2))
            st.done(stt(T(38 + t), T(46 + t % 2), c.v("dsa_q_norm" if t < 4 else "dsa_k_norm"), T(50 + t % 2),
                        ALU.mult, ALU.mult), s["head_normed"])
        if t >= 1:
            rotate(("rot_d", t - 1), T(38 + t - 1), T(38 + t - 1), T(10), T(11), T(52), s["head_roped"])
    mask = c.square("gla").bitcast(I32).unsqueeze(1).broadcast_to([P, NB, P])
    for h in range(4):
        dve.wait_ge(*mix.filled(("att", h)))
        st.last(v.copy_predicated(T(ATT[h]).rearrange("p (n c) -> p n c", c=P), mask,
                                  mix.bank(("att", h)).rearrange("p (n c) -> p n c", c=P)), mix.emptied(("att", h)))
    for t in range(2):
        dve.wait_ge(*mix.filled(("kv", t, 1)))
        states = T(5 + 2 * t, 2)
        for n in range(NCH - 1):
            own = mix.bank(("kv", t, n % 2))[:, (n // 2) * P:(n // 2 + 1) * P]
            out = states[:, (n + 1) * P:(n + 2) * P]
            if n == 0:
                ins = v.tensor_copy(out, own)
            else:
                ins = stt(out, states[:, n * P:(n + 1) * P], small[:, 40 + 8 * t + n:41 + 8 * t + n], own, ALU.mult, ALU.add)
            st.done(ins, s["state_ready"])
        for e in range(2):
            dve.sem_inc(*mix_release(mix, ("kv", t, e)))
    for h in range(4):
        inverse(("stat_o", h), T(50 + h % 2))
        st.done(stt(T(52), T(46 + h % 2), c.v("gla_out_norm"), T(50 + h % 2), ALU.mult, ALU.mult), s["head_normed"])
        st.done(tt(H(h), T(52), T(22 + h), ALU.mult), s["mixed"])
    units = [(b, h) for b in range(NB) for h in range(4)]
    for n in range(len(units) + 1):
        if n < 16:
            b, h = units[n]
            width, z, o = P * (b + 1), T(n % 2), n % 2
            if n >= 2:
                dve.wait_ge(*mix.filled(("pT", *units[n - 2])))
            dve.wait_ge(*mix.filled(("qk", b, h)))
            sel = c.square("causal_neg") if b == 0 else T(16 + b)[:, 0:width]
            st.last(v.tensor_tensor_reduce(z[:, 0:width], mix.bank(("qk", b, h))[:, 0:width], sel, 1.0, -3e38, ALU.add, ALU.max,
                                           small[:, 60 + o:61 + o]), mix.emptied(("qk", b, h)))
            st.done(ts(small[:, 56 + o:57 + o], small[:, 60 + o:61 + o], -P ** -0.5, ALU.mult), s["max_ready"])
        if n >= 1:
            b, h = units[n - 1]
            o, width = (n - 1) % 2, P * (b + 1)
            dve.wait_ge(s["p_ready"], n)
            st.link(v.reciprocal(small[:, 62 + o:63 + o], small[:, 58 + o:59 + o]))
            st.done(ts(T(o)[:, 0:width], T(o)[:, 0:width], small[:, 62 + o:63 + o], ALU.mult), s["pn_ready"])
    residual("abo", gate=lambda k: c.m(0, 2, k))

    def ada_iteration(i, layer, ctx, q4=4):
        for q in range(q4):
            first = 48 * layer + q
            dve.wait_ge(c.ada_landed[q % ADA_RING], i * (16 * 4 // ADA_RING) + 16 * (first // ADA_RING + 1))
            w = c.ada[:, (q % ADA_RING) * D:(q % ADA_RING + 1) * D]
            if ctx:
                v.tensor_tensor_reduce(T(26, 2), w, c.cond[:, D:2 * D], 1.0, 0.0, ALU.mult, ALU.add, c.acc[:, 4 + q:5 + q]) \
                    .then_inc(s["ada_first"], 1)
                dve.wait_ge(s["ada_first"], i * 4 + q + 1)
            v.tensor_tensor_reduce(w, w, c.cond[:, 0:D], 1.0, 0.0, ALU.mult, ALU.add, c.acc[:, q:q + 1]).then_inc(s["ada_used"], 1)
            dve.wait_ge(s["ada_used"], i * 4 + first + 1)
        done = 11 * (layer - 1)
        for n in range(2 if ctx else 1):
            to = 48 * layer if n == 0 else 3 * 48
            v.tensor_copy(c.mod[:, bass.ds(i * 4 + to, 4)], c.acc[:, 4 * n:4 * n + 4]).then_inc(s["ada_copied"], 1)
            dve.wait_ge(s["ada_copied"], i * (2 if ctx else 1) + done + n + 1)

    def swiglu(up, layer, ctx):
        u0 = proj.number[(up, 0)]
        with dve.Fori(0, 2 * FT // 4) as i:
            for p in range(2):
                u = u0 + 2 * p
                dve.wait_ge(proj.full_sem, i * 4 + u + 2)
                dve.wait_ge(proj.empty_sem[u % RING], i + u // RING + 1)
                out = c.pool[:, bass.ds(i * (2 * S) + p * S, S)]
                tt(out, T(22 + p), proj.banks[:, (u + 1) % RING, :], ALU.mult).then_inc(proj.empty_sem[(u + 1) % RING], 1)
            ada_iteration(i, layer, ctx)
        for j in range(44, 48):
            if ctx:
                chunk = 48 * layer + j
                dve.wait_ge(c.ada_landed[chunk % ADA_RING], 16 * (chunk // ADA_RING + 1))
                w = c.ada[:, (chunk % ADA_RING) * D:(chunk % ADA_RING + 1) * D]
                st.link(v.tensor_tensor_reduce(T(26, 2), w, c.cond[:, D:2 * D], 1.0, 0.0, ALU.mult, ALU.add, c.mod[:, 3 * 48 + j:3 * 48 + j + 1]))
            ada_row(48 * layer + j, c.cond[:, 0:D], c.mod[:, 48 * layer + j:48 * layer + j + 1])

    norm(1)
    swiglu("up0", 1, False)
    add_bias(1, 0, 48, "ada_b", 48)
    gains(2, 1, 1, "mix_norm", 8)
    gains(3, 1, 4, "ffn_norm", 8)
    residual("dn0", gate=lambda k: c.m(0, 5, k))
    norm(2)
    for g in range(4):
        dve.wait_ge(*proj.emptied(("cu", g)))
        src = T(g)
        for n in range(g + 1):
            sh, dst = 2 ** n, T(4 + n % 2)
            st.link(tt(dst[:, sh:S], src[:, sh:S], src[:, 0:S - sh], ALU.add))
            st.link(v.tensor_copy(dst[:, 0:sh], src[:, 0:sh]))
            src = dst
        st.link(tt(src[:, 0:16], src[:, 0:16], c.const("count")[:, 16 * g:16 * g + 16], ALU.mult))
        st.link(ts(src[:, 16:S], src[:, 16:S], 0.5 ** (g + 1), ALU.mult))
        st.done(tt(T(6 + g), src, T(g), ALU.subtract), s["pooled"])
    for t in range(8):
        inverse(("stat_s", t), T(22 + t % 2))
        st.done(stt(T(10 + t), T(18 + t % 2), c.v("sb_q_norm" if t < 4 else "sb_k_norm"), T(22 + t % 2), ALU.mult, ALU.mult),
                s["head_normed"])
    for h in range(5):
        if h < 4:
            z, sp = T(28 + 3 * (h % 2), 3)[:, 0:TRI[4]], T(34 + 3 * (h % 2), 3)[:, 0:TRI[4]]
            dve.wait_ge(s["z_ready"], h + 1)
            st.link(stt(sp, z, 0.0, sp, ALU.max, ALU.add))
            for j in range(NB - 1):
                w = slice(TRI[j], TRI[j] + P)
                st.link(tt(sp[:, w], sp[:, w], c.square("strict"), ALU.mult))
            w = slice(TRI[3], TRI[3] + P)
            st.done(tt(sp[:, w], sp[:, w], c.square("strict"), ALU.mult), s["sp_ready"])
            st.link(tt(z, z, sp, ALU.subtract))
            for j in range(NB):
                w = slice(TRI[j], TRI[j] + P)
                st.link(tt(z[:, w], z[:, w], c.square("strict_neg"), ALU.add))
        if h >= 1:
            z = T(28 + 3 * ((h - 1) % 2), 3)
            for j in range(NB):
                key = ("cum", h - 1, j)
                dve.wait_ge(*mix.filled(key))
                w = z[:, TRI[j]:TRI[j + 1]]
                st.last(tt(w, w, mix.bank(key)[:, 0:S - P * j], ALU.subtract), mix.emptied(key))
    residual("cdo", gate=lambda k: c.m(1, 2, k))
    norm(3)
    dve.wait_ge(s["cond_ready"], 2)
    swiglu("up1", 2, True)
    add_bias(2, 0, 48, "b_mod_3", 0)
    add_bias(3, 0, 48, "b_mod_3", 0)
    gains(6, 3, 1, "g_pre_mix_3", 0)
    gains(4, 2, 1, "g_pre_mix_3", 0)
    gains(5, 2, 4, "g_pre_mlp_3", 0)
    st.link(tt(c.g(7, 0, 8), c.m(2, 2, 0, 8), c.v("g_post_mix_3", 0, 8), ALU.mult))
    st.link(tt(c.g(8, 0, 8), c.m(2, 5, 0, 8), c.v("g_post_mlp_3", 0, 8), ALU.mult))
    residual("dn1", gate=lambda k: c.m(1, 5, k))
    norm(4)
    for t in range(8):
        dve.wait_ge(s["conv_init"], t + 1)
        bank = proj.bank(("mqk", t))
        for back in (1, 2, 3):
            out = T(t)[:, back:S]
            ins = stt(out, bank[:, 0:S - back], c.v("m_conv_w_2", 8 * (3 - back) + t), out, ALU.mult, ALU.add)
            if back < 3:
                st.link(ins)
            else:
                st.last(ins, proj.emptied(("mqk", t)))
    r4 = lambda i: T(i)[0:4, :]
    st.link(v.memset(r4(27), 1.0))
    dve.wait_ge(s["m_gate"], 1)
    st.link(stt(r4(25), r4(25), 0.0, r4(26), ALU.min, ALU.subtract))
    st.link(v.tensor_tensor_scan(r4(28), r4(27), r4(25), 0.0, ALU.mult, ALU.add))
    st.link(tt(r4(29), r4(24), r4(28), ALU.subtract))
    st.link(v.tensor_tensor_scan(r4(30), r4(29), r4(29), 0.0, ALU.max, ALU.max))
    st.link(ts(r4(31), r4(30), -1.0, ALU.mult))
    st.done(tt(r4(28), r4(28), r4(30), ALU.add), s["m_rows"])
    for h in range(4):
        nm, e, p = T(32 + h % 2), T(EH[h % 2], 3), T(38 + 3 * (h % 2), 3)
        dve.wait_ge(*mix.emptied(("mbc", h, 1)))
        for j in range(NB):
            ins = ts(e[:, TRI[j]:TRI[j + 1]], nm[:, P * j:S], small[:, 64 + 4 * j + h:65 + 4 * j + h], ALU.add, 0.0, ALU.min)
            if j < NB - 1:
                st.link(ins)
            else:
                st.done(ins, s["e_arg"])
        dve.wait_ge(s["e_ready"], h + 1)
        for j in range(NB):
            w = slice(TRI[j], TRI[j] + P)
            st.link(tt(e[:, w], e[:, w], c.square("before"), ALU.mult))
        for j in range(NB):
            key = ("ms", h, j)
            dve.wait_ge(*mix.filled(key))
            w = slice(TRI[j], TRI[j + 1])
            st.last(stt(p[:, w], mix.bank(key)[:, 0:S - P * j], P ** -0.5, e[:, w], ALU.mult, ALU.mult), mix.emptied(key))
        dve.wait_ge(*mix.emptied(("md", h)))
        st.link(tt(T(47), T(47), T(34 + h % 2), ALU.max))
        st.link(v.reciprocal(T(47), T(47)))
        for k in range(2):
            hm = T(48 + 2 * (h % 2) + k)
            st.done(tt(hm, mix.bank(("mn", h, k)), T(47), ALU.mult), s["hm_ready"])
            dve.sem_inc(*mix_release(mix, ("mn", h, k)))
        inverse(("stat_m", h), T(58))
        for k in range(2):
            hm = T(48 + 2 * (h % 2) + k)
            st.link(stt(hm, hm, c.v("m_head_norm_2", 2 * h + k), T(58), ALU.mult, ALU.mult))
            st.done(tt(H(2 * h + k), hm, T(16 + 2 * h + k), ALU.mult), s["mixed"])
    residual("mout")

    def conv_ffn(up, layer, base):
        u0 = proj.number[(up, 0)]
        w0 = VCOL["f_conv_w_2"] + 3 * 2 * FT * layer
        with dve.Fori(0, 2 * FT // 4) as i:
            for p in range(2):
                for g in range(2):
                    u, a = u0 + 2 * p + g, T(22 + 2 * p + g)
                    dve.wait_ge(s["conv_init"], i * 4 + (8 + 2 * base + 2 * p + g + 1))
                    for back in (1, 2):
                        col = w0 + 2 * FT * (2 - back) + FT * g + p
                        ins = stt(a[:, back:S], proj.banks[:, u % RING, 0:S - back], c.vec[:, bass.ds(i * 2 + col, 1)],
                                  a[:, back:S], ALU.mult, ALU.add)
                        if back == 1:
                            ins.then_inc(s["convolved"], 1)
                            dve.wait_ge(s["convolved"], i * 4 + (CONVOLVED[layer] + 2 * p + g + 1))
                        else:
                            ins.then_inc(proj.empty_sem[u % RING], 1)
                            dve.wait_ge(proj.empty_sem[u % RING], i + u // RING + 1)
                dve.wait_ge(s["conv_act"], i * 2 + (8 + base + p + 1))
                out = c.pool[:, bass.ds(i * (2 * S) + p * S, S)]
                tt(out, T(22 + 2 * p), T(23 + 2 * p), ALU.mult).then_inc(s["mid_ready"], 1)
                dve.wait_ge(s["mid_ready"], i * 2 + (2 + base + p + 1))

    dve.sem_inc(s["mid_ready"], 2)
    norm(5)
    conv_ffn("up2", 0, 0)
    residual("dn2")
    norm(6)
    pad = S + CONV - 1
    u_all = T(0, 9)[:, 0:KD * pad]
    st.link(v.memset(u_all.rearrange("p (k t) -> p k t", k=KD)[:, :, 0:CONV - 1], 0.0))
    for t in range(KD):
        key = ("ca", 2 * t)
        u = u_all[:, t * pad:(t + 1) * pad]
        dve.wait_ge(*proj.emptied(("ca", 2 * t + 1)))
        st.last(stt(u[:, CONV - 1:pad], proj.bank(key), c.v("c_b_in_2", t), T(9 + t % 2), ALU.add, ALU.mult), proj.emptied(key))
        acc = T(11 + t)
        st.link(ts(acc, u[:, 0:S], c.v("c_dw_w_2", t), ALU.mult, c.v("c_dw_b_2", t), ALU.add))
        for k in range(1, CONV):
            ins = stt(acc, u[:, k:k + S], c.v("c_dw_w_2", 8 * k + t), acc, ALU.mult, ALU.add)
            if k < CONV - 1:
                st.link(ins)
            else:
                ins.then_inc(s["u_ready"], 1)
                dve.wait_ge(s["u_ready"], t + 1)
    dve.wait_ge(*mix.filled(("lnm", 0)))
    st.last(ts(T(RSTD), mix.bank(("lnm", 0)), 1 / D, ALU.mult), mix.emptied(("lnm", 0)))
    for k in range(KD):
        st.done(tt(T(11 + k), T(11 + k), T(RSTD), ALU.subtract), s["u_centred"])
    inverse(("lnv", 0), T(RSTD))
    for k in range(KD):
        st.done(tt(T(11 + k), T(11 + k), T(RSTD), ALU.mult), s["u_normed"])
    residual("cout", bias=lambda k: c.v("c_b_out_2", k))
    norm(7)
    conv_ffn("up3", 1, FT)
    residual("dn3")
    norm(8)
    inverse(("ssc", 0), T(12)[:, 0:CTX])
    for k in range(KD):
        w = slice(k * CTX, (k + 1) * CTX)
        st.done(tt(T(4, 4)[:, w], T(0, 4)[:, w], T(12)[:, 0:CTX], ALU.mult), s["u_centred"])
    e, l, y, t8 = small[:, 80:88], small[:, 88:96], small[:, 128:136], small[:, 136:144]
    dve.wait_ge(s["lg_abs"], 1)
    st.link(ts(y, e, 1.0, ALU.add))
    st.link(ts(t8, y, -1.0, ALU.add))
    st.link(tt(t8, e, t8, ALU.subtract))
    st.link(v.reciprocal(y, y))
    st.link(tt(t8, t8, y, ALU.mult))
    st.link(tt(l, l, t8, ALU.add))
    st.link(stt(l, small[:, 0:8], 0.0, l, ALU.min, ALU.subtract))
    norm(9)
    for t in range(8):
        rotate(("rot_r", t), T(16 + t), T(24 + t % 2), T(41), T(42), T(26), s["head_roped"])
    dve.wait_ge(*proj.emptied(("fv", 3)))
    vs = T(33, 2).rearrange("p (g c) -> p g c", c=64)
    st.link(tt(T(61, 2), T(33, 2), T(33, 2), ALU.mult))
    st.done(v.tensor_reduce(small[:, 96:112], T(61, 2).rearrange("p (g c) -> p g c", c=64), AX.X, ALU.add), s["vs_var"])
    dve.wait_ge(s["vs_std"], 1)
    st.link(v.reciprocal(small[:, 96:112], small[:, 96:112]))
    st.link(tt(vs, vs, small[:, 96:112].unsqueeze(2).broadcast_to([P, 16, 64]), ALU.mult))
    dve.wait_ge(s["late"], 16 * 3)
    vb = T(33, 2).rearrange("p (n c) -> p n c", c=256)
    st.done(tt(vb, vb, c.sgu_norm[:, :].unsqueeze(1).broadcast_to([P, NB, 256]), ALU.mult), s["vs_ready"])
    dist = T(47, 6)
    for h in range(4):
        fwd, bwd = small[:, 88 + h:89 + h], small[:, 92 + h:93 + h]
        if h == 0:
            dve.wait_ge(*proj.emptied(("rg", 3)))
        own, before, after = (T(at, 2)[:, 0:width] for at, width in TABLES)
        st.link(ts(own, dist[:, 0:SELF_W], fwd, ALU.mult))
        st.done(stt(own, dist[:, SELF_W:2 * SELF_W], bwd, own, ALU.mult, ALU.add), s["table_arg"])
        st.done(ts(before, dist[:, 2 * SELF_W:2 * SELF_W + CTX_W], fwd, ALU.mult), s["table_arg"])
        st.done(ts(after, dist[:, 2 * SELF_W + CTX_W:6 * S], bwd, ALU.mult), s["table_arg"])
        dve.wait_ge(s["table_ready"], 3 * (h + 1))
        st.link(tt(before, before, after, ALU.add))
        for j in range(6):
            key = ("rs", h, j)
            dve.wait_ge(*mix.filled(key))
            w = own[:, 384 - P * j:896 - P * j] if j < 4 else before[:, P * (5 - j):P * (5 - j) + S]
            st.last(tt(T(RP[j]), mix.bank(key), w, ALU.mult), mix.emptied(key))
        inverse(("stat_r", h), T(59))
        st.link(tt(T(57), T(57), T(59), ALU.mult))
        st.done(tt(T(8 + h), T(57), T(37 + h), ALU.mult), s["mixed"])
    dve.wait_ge(s["dft_loaded"], 32)
    for t in range(2):
        key = ("sgu", t)
        dve.wait_ge(*mix.filled(key))
        for g in range(2):
            r = slice(64 * g, 64 * g + 64)
            bias = c.sgu_b[r, (2 * t + g) * P:(2 * t + g + 1) * P].unsqueeze(1).broadcast_to([64, NB, P])
            out = T(59 + t)[r, :].rearrange("p (n c) -> p n c", c=P)
            ins = tt(out, mix.bank(key)[r, :].rearrange("p (n c) -> p n c", c=P), bias, ALU.add)
            if g == 0:
                st.link(ins)
            else:
                st.last(ins, mix.emptied(key))
        st.done(tt(T(59 + t), T(59 + t), T(35 + t), ALU.mult), s["sgu_ready"])
    u0 = proj.number[("br", 0)]
    with dve.Fori(0, 4) as i:
        for n in range(2):
            out = c.pool[:, bass.ds(i * (2 * S) + (16 + n) * S, S)]
            for g in range(3):
                u = u0 + 6 * n + 3 + g
                dve.wait_ge(proj.full_sem, i * 12 + u + 1)
                dve.wait_ge(proj.empty_sem[(u - 3) % RING], i * 3 + ((u - 3) // RING + 1))
                dst = out if g == 0 else T(6)
                tt(dst, proj.banks[:, u % RING, :], T(3 * n + g), ALU.mult).then_inc(proj.empty_sem[u % RING], 1)
                dve.wait_ge(proj.empty_sem[u % RING], i * 3 + (u // RING + 1))
                if g > 0:
                    sem, m = (s["pr_ready"], 1) if g == 1 else (s["merged"], 1)
                    tt(out, out, T(6), ALU.add).then_inc(sem, 1)
                    dve.wait_ge(sem, i * 2 + (n + 1))

    def post_norm(stage, r, y, gain, sem):
        inverse(("ssy", r), T(RSTD))
        for k in range(KD):
            st.link(stt(T(y + k), T(y + k), c.g(gain, k), T(RSTD), ALU.mult, ALU.mult))
            st.done(tt(X(k), X(k), T(y + k), ALU.add), sem)

    post_norm("ro", 0, 27, 7, s["x_ready"])
    norm(10)
    dve.sem_inc(s["mlp_mid"], 4)
    u0 = proj.number[("upr", 0)]
    with dve.Fori(0, F3T // 4) as i:
        for j in range(4):
            u = u0 + j
            dve.wait_ge(proj.empty_sem[u % RING], i + (u // RING + 1))
            tt(c.pool[:, bass.ds(i * (4 * S) + j * S, S)], T(32 + j), T(32 + j), ALU.mult).then_inc(s["mlp_mid"], 1)
    post_norm("dnr", 1, 32, 8, s["out_ready"])


def mix_release(mix, key):
    sem, _ = mix.emptied(key)
    return sem, 1


ROUND = 1.5 * 2 ** 23
TURN = (6.28125, 0.0019354820251464844, -1.7484555314695172e-07)
CONVOLVED = (0, 2 * FT)



def build(nc, dram):
    with ExitStack() as ctx:
        c = Chip(nc, ctx, dram)
        block = ctx.enter_context(nc.Block())

        @block.sync
        def _(sp):
            sync_program(nc, sp, c)

        @block.gpsimd
        def _(pool):
            gpsimd_program(nc, pool, c)

        @block.tensor
        def _(pe):
            tensor_program(nc, pe, c)

        @block.scalar
        def _(act):
            scalar_program(nc, act, c)

        @block.vector
        def _(dve):
            vector_program(nc, dve, c)


def columns(w, kt):
    parts = pieces(kt)
    n = w.shape[1] // P
    a = w.reshape(len(parts), parts[0], P, n, P).transpose(3, 0, 2, 1, 4)
    return np.ascontiguousarray(a.reshape(n * len(parts), P, parts[0] * P))


def rows(w):
    m = w.shape[1] // S
    a = w.reshape(4, 2, P, m, S).transpose(3, 0, 2, 1, 4)
    return np.ascontiguousarray(a.reshape(4 * m, P, 2 * S))


def paired(w):
    k, n = w.shape
    return w.reshape(k, 2, n // (2 * P), P).transpose(0, 2, 1, 3).reshape(k, n)


def lay_out(a):
    f = {k: np.asarray(x) for k, x in a.items()}
    ab, cd, mw, w3 = f["ab_w_in"][0], f["cd_w_in"][0], f["m_w_in_2"][0], f["w_in_3"][0]
    col = lambda w, lo, hi, kt=8: columns(np.ascontiguousarray(w[:, lo:hi]), kt)
    row = lambda w, lo, hi: rows(np.ascontiguousarray(w[:, lo:hi]))
    w = {
        "iq": col(ab, 3088, 3600), "ik": columns(np.concatenate([ab[:, 3600:3664]] * 2, 1), 8), "gr": col(ab, 1040, 1552),
        "gq": col(ab, 0, 256), "gk": col(ab, 256, 512), "gv": row(ab, 512, 1024), "dv": row(ab, 2576, 3088),
        "dq": col(ab, 1552, 2064), "dk": col(ab, 2064, 2576), "abo": columns(f["ab_w_out"][0], 8),
        "cu": col(cd, 0, 512), "sq": col(cd, 512, 1024), "sk": col(cd, 1024, 1536), "sv": row(cd, 1536, 2048),
        "cdo": columns(f["cd_w_out"][0], 8),
        "mqk": col(mw, 0, 1024), "mv": row(mw, 1024, 2048), "mo": col(mw, 2048, 3072), "mout": columns(f["m_w_out_2"][0], 8),
        "ca": columns(paired(f["c_w_in_2"][0]), 8), "cout": columns(f["c_w_out_2"][0], 8),
        "ck": col(w3, 512, 1024), "cv": row(w3, 1024, 1536), "rk": col(w3, 512, 1024), "rq": col(w3, 0, 512),
        "rv": row(w3, 1024, 1536), "fv": rows(np.concatenate([w3[:, 2048:2304], w3[:, 2560:2816]], 1)),
        "ru": col(w3, 2304, 2560), "rg": col(w3, 1536, 2048), "ro": columns(f["w_out_3"][0], 8),
        "upr": columns(f["w_up_3"][0], 8), "dnr": columns(f["w_down_3"][0], 32),
    }
    for layer in range(2):
        w[f"up{layer}"] = columns(paired(f["ffn_w1"][layer]), 8)
        w[f"dn{layer}"] = columns(f["ffn_w2"][layer], FT)
        w[f"up{layer + 2}"] = columns(paired(f["f_w_up_2"][layer]), 8)
        w[f"dn{layer + 2}"] = columns(f["f_w_down_2"][layer], FT)
    gates = [w3[:, 2816 + D * g:2816 + D * (g + 1)] for g in range(3)]
    branch = np.concatenate([f["w_branch_a_3"][0], f["w_branch_b_3"][0], f["w_branch_c_3"][0]], 0)
    parts = [columns(np.ascontiguousarray(m), 8) for m in (*gates, branch)]
    w["br"] = np.stack(parts, 1).reshape(32, P, D)
    small = np.concatenate([ab[:, 1024:1040], ab[:, 3664:3672], mw[:, 3072:3080]], 1)
    out = {f"w_{k}": x for k, x in w.items()}
    out["w_small"] = np.ascontiguousarray(small.reshape(KD, P, 32).transpose(1, 0, 2).reshape(P, KD * 32))
    out["ada"] = np.concatenate([m.T for m in (f["ada_w"][0], f["ada_w"][1], f["w_mod_3"][0])], 0).reshape(144, P, D)
    out["x"] = np.ascontiguousarray(f["x"][0].T)
    out["ctx"] = np.ascontiguousarray(f["ctx_3"][0].T)
    out["vectors"] = np.ascontiguousarray(np.concatenate([f[n].reshape(-1, P).T for n, _ in VECTORS], 1))
    out["squares"] = np.concatenate(list(square_constants().values()), 1)
    out["others"] = np.concatenate([x.astype(np.float32) for x in other_constants().values()], 1)
    out.update({k: x.astype(np.float32) for k, x in late_constants().items()})
    out["c"], out["c_3"], out["c_ctx_3"] = f["c"][0], f["c_3"][0], f["c_ctx_3"]
    out["positions"] = f["positions"][0]
    out["gla_gate_up"] = f["gla_gate_up"][0]
    out["m_bias"] = np.ascontiguousarray(f["m_b_gates_2"][0].reshape(2, 4).T)
    out["pool_w"] = np.ascontiguousarray(f["pool_w"][0].transpose(1, 0, 2).reshape(P, 4 * P))
    out["sgu_w"] = np.ascontiguousarray(f["sgu_w_s_3"][0].transpose(2, 0, 1).reshape(P, 4 * P))
    out["sgu_norm"], out["sgu_b"] = f["sgu_norm_3"][0], f["sgu_b_s_3"][0].reshape(-1)
    out["decay"] = f["ret_decay_logit_3"][0].reshape(-1)
    return out


def kernel(**inputs):
    import concourse.bacc as bacc
    from concourse.bass_utils import run_bass_kernel_spmd

    nc = bacc.Bacc("TRN2", target_bir_lowering=False, num_devices=1, dynamic_dma_scratch_size=4096)
    arrays = lay_out(inputs)
    dram = {n: nc.dram_tensor(f"in_{n}", a.shape, mybir.dt.from_np(a.dtype), kind="ExternalInput").ap() for n, a in arrays.items()}
    dram["out"] = nc.dram_tensor("out", (D, S), F32, kind="ExternalOutput").ap()
    build(nc, dram)
    r = run_bass_kernel_spmd(nc, [{f"in_{n}": a for n, a in arrays.items()}], core_ids=[0])
    return np.ascontiguousarray(r.results[0]["out"].T)[None]
```

```python
from contextlib import ExitStack, contextmanager

import numpy as np

import concourse.bass as bass
from concourse import mybir

F32 = mybir.dt.float32
F32R = mybir.dt.float32r
I32 = mybir.dt.int32
ALU = mybir.AluOpType
ACT = mybir.ActivationFunctionType
AX = mybir.AxisListType

P = 128
S = 512
D = 1024
KD = D // P
NB = S // P
FF = 2816
FT = FF // P
F3 = 4096
F3T = F3 // P
EPS = 1e-6
NEG = -1e30
TAKEN = -3e38
TOPK = 128
CTX = 256
RING = 4
SLOT = 8 * P
ADA_RING = 4
POOL = 58
SPLIT_RING = 2
FIRST_ROWS = (0, 2, 4, 6, 8, 14, 16, 18, 20, 22, 24, 26, 28, 34, 36, 38)
CHUNK = 64
NCH = S // CHUNK
CONV = 31



def square_constants():
    p = np.arange(P)[:, None]
    c = np.arange(P)[None, :]
    a64 = 2 * np.pi * (np.arange(64)[:, None] * np.arange(64)[None, :] % 64) / 64
    cb, sb = np.zeros((P, P)), np.zeros((P, P))
    for g in range(2):
        s = slice(64 * g, 64 * g + 64)
        cb[s, s] = np.cos(a64)
        sb[s, s] = -np.sin(a64)
    norm = 1.0 / np.sqrt(S * 64.0)
    out = {
        "ones": np.ones((P, P)),
        "ident": (p == c),
        "swap64": (p == (c + 64) % P),
        "swap32": (p == (c ^ 32)),
        "later": (p > c),
        "causal_neg": np.where(c <= p, 0.0, NEG),
        "before": (p <= c),
        "strict": (p < c),
        "strict_neg": np.where(p < c, 0.0, NEG),
        "gla": (p <= c) & (p // CHUNK == c // CHUNK),
        "dft_cos": cb * norm,
        "dft_sin": sb * norm,
    }
    return {k: np.asarray(v, np.float32) for k, v in out.items()}


SQUARES = list(square_constants())


def other_constants():
    p = np.arange(P)
    inv = lambda half: (10000.0 ** (-np.arange(half) / half)).astype(np.float32)
    sel = np.zeros((P, 4, P))
    for h in range(4):
        sel[h, h] = 1
    t = np.arange(16)
    return {
        "reset": np.tile((np.arange(S) % CHUNK != 0).astype(np.float32), (P, 1)),
        "count": np.tile(np.stack([1.0 / np.minimum(t + 1, 2 ** (g + 1)) for g in range(4)]).reshape(1, 64), (P, 1)),
        "sel": sel.reshape(P, 4 * P),
        "freq_q": inv(64)[p % 64][:, None],
        "freq_i": inv(32)[p % 32][:, None],
        "sign_q": np.where(p < 64, -1.0, 1.0)[:, None],
        "sign_i": np.where(p % 64 < 32, -1.0, 1.0)[:, None],
        "eps": np.full((P, 1), EPS),
        "one": np.ones((P, 1)),
    }


SELF_W, CTX_W = 896, 640


def late_constants():
    p = np.arange(P)[:, None]
    x = np.arange(SELF_W)[None, :]
    d = x - 384 - p
    y = np.arange(CTX_W)[None, :]
    rows = np.repeat(np.arange(S // 64, dtype=np.float32), 64)
    cols = np.tile(np.arange(64, dtype=np.float32), S // 64)
    freqs = (np.float32(10000.0) ** (-np.arange(32, dtype=np.float32) / 32)).astype(np.float32)
    ang = np.concatenate([rows[:, None] * freqs, cols[:, None] * freqs], axis=-1).astype(np.float64).T
    aL = 2 * np.pi * (np.arange(S)[:, None] * np.arange(S)[None, :] % S) / S
    tok = lambda m: m.reshape(NB, P, S).transpose(1, 0, 2).reshape(P, NB * S)
    dist = np.zeros((P, 6 * S))
    dist[:, 0:SELF_W] = np.maximum(d, 0)
    dist[:, SELF_W:2 * SELF_W] = np.maximum(-d, 0)
    dist[:, 2 * SELF_W:2 * SELF_W + CTX_W] = y + P - p
    dist[:, 2 * SELF_W + CTX_W:] = CTX_W - y + p
    return {
        "grid": np.concatenate([np.tile(np.cos(ang), (2, 1)),
                                np.concatenate([-np.sin(ang), np.sin(ang)])], axis=1),
        "dist": dist,
        "dft": np.concatenate([tok(np.cos(aL)), tok(np.sin(aL))], axis=1),
    }


VECTORS = [
    ("mix_norm", 2 * D), ("ffn_norm", 2 * D), ("ada_b", 2 * 6 * D), ("gla_gate_b", 256), ("gla_out_norm", P),
    ("dsa_q_norm", P), ("dsa_k_norm", P), ("pool_scale", 4 * P), ("sb_q_norm", P), ("sb_k_norm", P),
    ("norm_mix_2", 2 * D), ("norm_ffn_2", 2 * D), ("norm_final_2", D), ("m_conv_w_2", 4 * D), ("m_conv_b_2", D),
    ("m_head_norm_2", D), ("c_b_in_2", 2 * D), ("c_dw_w_2", CONV * D), ("c_dw_b_2", D), ("c_ln_g_2", D),
    ("c_ln_b_2", D), ("c_b_out_2", D), ("f_conv_w_2", 2 * 3 * 2 * FF), ("f_conv_b_2", 2 * 2 * FF),
    ("b_mod_3", 6 * D), ("g_pre_mix_3", D), ("g_post_mix_3", D), ("g_pre_mlp_3", D), ("g_post_mlp_3", D),
]
VCOL = {}
NV = 0
for _name, _n in VECTORS:
    VCOL[_name] = NV
    NV += _n // P

STAGES = [
    ("iq", "feat", 4, 8), ("ik", "feat", 1, 8), ("gr", "feat", 4, 8), ("gq", "feat", 2, 8), ("gk", "feat", 2, 8),
    ("gv", "tok", 4, 8), ("dv", "tok", 4, 8), ("dq", "feat", 4, 8), ("dk", "feat", 4, 8), ("abo", "loop", 8, 8),
    ("up0", "loop", 2 * FT, 8), ("dn0", "loop", 8, FT),
    ("cu", "feat", 4, 8), ("sq", "feat", 4, 8), ("sk", "feat", 4, 8), ("sv", "tok", 4, 8), ("cdo", "loop", 8, 8),
    ("up1", "loop", 2 * FT, 8), ("dn1", "loop", 8, FT),
    ("mqk", "feat", 8, 8), ("mv", "tok", 8, 8), ("mo", "loop", 8, 8), ("mout", "loop", 8, 8),
    ("up2", "loop", 2 * FT, 8), ("dn2", "loop", 8, FT),
    ("ca", "loop", 16, 8), ("cout", "loop", 8, 8),
    ("up3", "loop", 2 * FT, 8), ("dn3", "loop", 8, FT),
    ("ck", "feat", 4, 8), ("cv", "tok", 2, 8),
    ("rk", "feat", 4, 8), ("rq", "feat", 4, 8), ("rv", "tok", 4, 8), ("fv", "tok", 4, 8), ("ru", "feat", 2, 8),
    ("rg", "feat", 4, 8), ("br", "branch", 48, 8), ("ro", "loop", 8, 8), ("upr", "loop", F3T, 8), ("dnr", "loop", 8, F3T),
]
STAGE = {s[0]: s for s in STAGES}

SPLIT = ("up0", "dn0", "cu", "sq", "sk", "sv", "up1", "dn1", "mqk", "mv", "mo", "up2", "dn2", "up3", "dn3", "rk", "rq", "rv", "fv", "ru", "rg", "br", "upr")
SPLIT_NORMS = (1, 2, 3, 4, 5, 7, 9, 10)


def pieces(k_tiles):
    return {8: [8], 22: [8, 8, 6], 32: [8, 8, 8, 8]}[k_tiles]


def splits_of(stage):
    if stage[0] not in SPLIT:
        return 0
    return 24 if stage[0] == "br" else chunks_of(stage)


def chunks_of(stage):
    name, kind, tiles, kt = stage
    if kind == "tok":
        return 4 * ((tiles + 3) // 4)
    if kind == "branch":
        return 32
    return tiles * len(pieces(kt))




def projection_keys():
    keys = []
    for name, kind, tiles, _ in STAGES:
        keys += [(name, t) for t in range(tiles)]
        if name == "ik":
            keys += [("iw", t) for t in range(NB)] + [("glow", 0)]
        if name == "mo":
            keys += [("mi", 0), ("mf", 0)]
    return keys


def mixing_keys():
    k = [("ss", 0)]
    k += [("rot_i", t) for t in range(5)]
    k += [("idx", b, h) for b in range(1, NB) for h in range(8)]
    k += [("gate", t) for t in range(2)]
    for t in range(9):
        k += [("stat_d", t)] if t < 8 else []
        k += [("rot_d", t - 1)] if t >= 1 else []
    k += [("kdt", t) for t in range(2)] + [("att", h) for h in range(4)]
    k += [("kv", t, e) for t in range(2) for e in range(2)]
    for h in range(5):
        k += [("o", h)] if h < 4 else []
        k += [("stat_o", h - 1)] if h >= 1 else []
    units = [(b, h) for b in range(NB) for h in range(4)]
    for n in range(len(units) + 2):
        k += [("qk", *units[n])] if n < 16 else []
        k += [("pT", *units[n - 1])] if 1 <= n <= 16 else []
        k += [("av", *units[n - 2])] if n >= 2 else []
    k += [("ss", 1), ("ss", 2)]
    k += [("stat_s", t) for t in range(8)] + [("pool", g) for g in range(4)]
    for h in range(6):
        k += [("z", h, j) for j in range(NB)] if h < 4 else []
        k += [("cum", h - 1, j) for j in range(NB)] if 1 <= h <= 4 else []
        k += [("sb", h - 2)] if h >= 2 else []
    k += [("ss", 3), ("ss", 4)]
    k += [("acol", 0)]
    for h in range(4):
        k += [("mbc", 0, 0), ("mbc", 0, 1)] if h == 0 else []
        k += [("ms", h, j) for j in range(NB)]
        k += [("mbc", h + 1, 0), ("mbc", h + 1, 1)] if h < 3 else []
        k += [("mn", h, 0), ("mn", h, 1), ("md", h), ("stat_m", h)]
    k += [("ss", 5), ("ss", 6), ("lnm", 0), ("lnv", 0), ("ss", 7), ("ss", 8), ("ssc", 0), ("ss", 9)]
    k += [("rot_r", t) for t in range(8)]
    for h in range(4):
        k += [("rs", h, j) for j in range(6)] + [("rout", h), ("stat_r", h)]
    k += [("dftl", t, c) for t in range(2) for c in range(2)] + [("four", t) for t in range(2)]
    k += [("sgu", t) for t in range(2)]
    k += [("ssy", 0), ("ss", 10), ("ssy", 1)]
    return k


class Ring:

    def __init__(self, banks, full, empty, keys):
        self.banks, self.full_sem, self.empty_sem = banks, full, empty
        self.number = {key: n for n, key in enumerate(keys)}
        assert len(self.number) == len(keys)

    def bank(self, key):
        return self.banks[:, self.number[key] % RING, :]

    def may_fill(self, key):
        n = self.number[key]
        return self.empty_sem[n % RING], n // RING

    def filled(self, key):
        return self.full_sem, self.number[key] + 1

    def emptied(self, key):
        n = self.number[key]
        return self.empty_sem[n % RING], n // RING + 1


class Chip:

    def __init__(self, nc, ctx, dram):
        self.dram = dram

        def sb(name, shape, dt=F32):
            return ctx.enter_context(nc.sbuf_tensor(name, shape, dt))

        def sem(name):
            return ctx.enter_context(nc.semaphore(name))

        self.x = sb("x_tiles", [P, KD * S])
        self.w = sb("weight_ring", [P, RING * SLOT])
        self.w_hi = sb("weight_hi", [P, SPLIT_RING * SLOT], F32R)
        self.w_lo = sb("weight_lo", [P, SPLIT_RING * SLOT], F32R)
        self.ada = sb("ada_ring", [P, (ADA_RING - 1) * D])
        self.cond = sb("cond", [P, 2 * D])
        self.sq_const = sb("squares", [P, len(SQUARES) * P])
        self.other = sb("others", [P, sum(v.shape[1] for v in other_constants().values())])
        self.vec = sb("vectors", [P, NV])
        self.wsmall = sb("small_weights", [P, KD * 32])
        self.gate_up = sb("gate_up", [16, 256])
        self.sgu_norm = sb("sgu_norm", [P, 256])
        self.m_bias = sb("m_bias", [4, 2])
        self.mod = sb("mod", [P, 4 * 48])
        self.gain = sb("gain", [P, 9 * 8])
        self.acc = sb("ada_acc", [P, 8])
        self.small = sb("small", [P, 160])
        with ExitStack() as mixing:
            self.h = mixing.enter_context(nc.sbuf_tensor("h_tiles", [P, KD * S], F32))
            self.pool = mixing.enter_context(nc.sbuf_tensor("scratch", [P, POOL * S], F32))
        with ExitStack() as mlstm:
            mlstm.enter_context(nc.sbuf_tensor("below_m_lo", [P, (KD + 36) * S], F32))
            self.m_lo = mlstm.enter_context(nc.sbuf_tensor("m_lo", [P, KD * S], F32R))
        self.h_lo = sb("h_lo", [P, KD * S], F32R)
        self.mid_hi = sb("mid_hi", [P, FT * S], F32R)
        self.mid_lo = sb("mid_lo", [P, FT * S], F32R)
        self.h_hi = sb("h_hi", [P, KD * S], F32R)
        self.unsplit = sb("unsplit", [P, (POOL - 2 * FT - KD) * S])
        self.pool_w = self.T(55)
        self.sgu_w = self.cond[:, 3 * S:4 * S]
        self.sgu_b = self.cond[:, 2 * S:3 * S]

        banks = [ctx.enter_context(nc.psum_tensor(n, [P, RING, S], F32)) for n in ("proj_banks", "mix_banks")]
        self.proj = Ring(banks[0], sem("proj_full"), [sem(f"proj_empty{i}") for i in range(RING)], projection_keys())
        self.mix = Ring(banks[1], sem("mix_full"), [sem(f"mix_empty{i}") for i in range(RING)], mixing_keys())
        self.landed = [sem(f"w_landed{i}") for i in range(RING)]
        self.first_rows = [sem(f"first_rows{i}") for i in range(4)]
        self.ada_landed = [sem(f"ada_landed{i}") for i in range(ADA_RING)]
        self.sem = {n: sem(n) for n in (
            "x_loaded", "c_loaded", "constants", "setup", "late", "pool_loaded", "dft_loaded", "cond_loaded", "ctx_loaded", "act_chain", "dve_chain",
            "cond_ready", "pos_ready", "trig_ready", "ada_used", "ada_copied", "ada_first", "mod_ready", "sq_ready", "xn_ready", "h_ready",
            "iq_ready", "idx_used", "gate_ready", "span_ready", "decay_ready", "gla_ready", "head_normed", "head_roped",
            "state_ready", "mixed", "max_ready", "p_ready", "pn_ready",
            "pooled", "z_ready", "sp_ready", "lw_ready", "w_ready", "wneg_ready",
            "convolved", "conv_init", "conv_act", "mid_raw", "mid_rounded", "mid_ready", "w_rounded", "w_split", "w_used", "h_raw", "h_rounded", "m_gate", "m_rows", "m_guard", "e_arg", "e_ready",
            "p_head", "hm_ready", "hsq_ready", "den_abs", "u_ready", "u_centred", "u_sq", "u_normed", "u_act",
            "x_ready", "hc_ready", "vs_var", "vs_std", "vs_ready", "lg_abs", "lg_ready", "table_arg", "table_ready",
            "pr_ready", "sgu_ready", "merged", "relu_ready", "mlp_mid", "y_ready", "out_ready", "out_stored",
        )}
        self.first_chunk, n = {}, 0
        self.first_split, m = {}, 0
        for s in STAGES:
            self.first_chunk[s[0]] = n
            n += chunks_of(s)
            if s[0] in SPLIT:
                self.first_split[s[0]] = m
                m += splits_of(s)

    def T(self, i, n=1):
        return self.pool[:, i * S:(i + n) * S]

    def X(self, k):
        return self.x[:, k * S:(k + 1) * S]

    def H(self, k):
        return self.h[:, k * S:(k + 1) * S]

    def ada_slot(self, row):
        q = row % ADA_RING
        if q < ADA_RING - 1:
            return self.ada[:, q * D:(q + 1) * D]
        return self.cond[:, D:2 * D] if row < 32 else self.T(56, 2)

    def ada_has_landed(self, row):
        return self.ada_landed[row % ADA_RING], 16 * (row // ADA_RING + 1)

    def late_tile(self, i):
        src = self.ada if i < 4 else self.cond
        return src[:, (i % 4) * S:(i % 4 + 1) * S]

    def H_hi(self, k):
        return self.h_hi[:, k * S:(k + 1) * S]

    def H_lo(self, k):
        return self.h_lo[:, k * S:(k + 1) * S]

    def norm_hi(self, norm, k):
        return self.mid_hi[:, k * S:(k + 1) * S] if norm == 9 else self.H_hi(k)

    def norm_lo(self, norm, k):
        return self.m_lo[:, k * S:(k + 1) * S] if norm == 4 else self.H_lo(k)

    def hi(self, n):
        return self.w_hi[:, (n % SPLIT_RING) * SLOT:(n % SPLIT_RING + 1) * SLOT]

    def lo(self, n):
        return self.w_lo[:, (n % SPLIT_RING) * SLOT:(n % SPLIT_RING + 1) * SLOT]

    def square(self, name):
        i = SQUARES.index(name)
        return self.sq_const[:, i * P:(i + 1) * P]

    def const(self, name):
        at = 0
        for k, v in other_constants().items():
            if k == name:
                return self.other[:, at:at + v.shape[1]]
            at += v.shape[1]
        raise KeyError(name)

    def v(self, name, k=0, n=1):
        return self.vec[:, VCOL[name] + k:VCOL[name] + k + n]

    def m(self, layer, part, k=0, n=1):
        at = 48 * layer + 8 * part + k
        return self.mod[:, at:at + n]

    def g(self, use, k=0, n=1):
        return self.gain[:, 8 * use + k:8 * use + k + n]

    def slot(self, chunk):
        i = chunk % RING
        return self.w[:, i * SLOT:(i + 1) * SLOT]

    def chunk_landed(self, chunk):
        return self.landed[chunk % RING], 16 * (chunk // RING + 1)


class Steps:

    def __init__(self, eng, chain):
        self.eng, self.chain, self.count = eng, chain, {}

    def next(self, sem):
        self.count[id(sem)] = self.count.get(id(sem), 0) + 1
        return self.count[id(sem)]

    def link(self, ins):
        self.done(ins, self.chain)

    def done(self, ins, sem):
        ins.then_inc(sem, 1)
        self.eng.wait_ge(sem, self.next(sem))

    def last(self, ins, emptied):
        sem, n = emptied
        ins.then_inc(sem, 1)
        self.eng.wait_ge(sem, n)

NORM_AFTER = {1: "abo", 2: "dn0", 3: "cdo", 4: "dn1", 5: "mout", 6: "dn2", 7: "cout", 8: "dn3"}
MODULATED = {0: (0, 0, 0, 1), 1: (1, 0, 3, 2), 2: (2, 1, 0, 3), 3: (3, 1, 3, 4), 9: (4, 2, 0, 6), 10: (5, 2, 3, 7)}
PLAIN = {4: ("norm_mix_2", 0), 5: ("norm_ffn_2", 0), 6: ("norm_mix_2", 8), 7: ("norm_ffn_2", 8), 8: ("norm_final_2", 0)}
SQ0, RSTD = 44, 54


def squares_at(norm):
    return 16 if norm == 9 else SQ0



def h_count(norm, k):
    return 8 * (norm if norm < 8 else norm - 1) + k + 1



def sync_program(nc, sp, c):
    d, s = c.dram, c.sem
    for dst, src in ((c.other, d["others"]), (c.vec, d["vectors"]), (c.sq_const, d["squares"])):
        sp.dma_start(dst[:, :], src).then_inc(s["constants"], 16)
    sp.dma_start(c.x[:, :].rearrange("p (k t) -> p k t", k=KD), d["x"].rearrange("(k p) t -> p k t", p=P)).then_inc(s["x_loaded"], 16)

    proj = c.proj
    sp.wait_ge(c.first_rows[1], 16 * 4)

    def load(stage, n, chunk):
        sp.dma_start(c.slot(chunk), d["w_" + stage][n]).then_inc(c.landed[chunk % RING], 16)

    for stage in STAGES:
        name, kind, tiles, kt = stage
        first, total = c.first_chunk[name], chunks_of(stage)
        if kt == FT:
            split = c.first_split[name]
            with sp.Fori(0, 2) as i:
                for q in range(12):
                    sp.wait_ge(s["w_split"], i * 12 + (split + q - RING + 1))
                    w = pieces(kt)[q % 3] * P
                    src = d["w_" + name][bass.ds(i * 4 + q // 3, 1)].rearrange("o p f -> p (o f)")[:, (q % 3) * SLOT:(q % 3) * SLOT + w]
                    sp.dma_start(c.slot(first + q)[:, 0:w], src).then_inc(c.landed[(first + q) % RING], 16)
            continue
        looped = kind in ("loop", "branch")
        for n in range(RING if looped else total):
            if first + n >= RING:
                sp.wait_ge(*chunk_use(c, first + n - RING))
            load(name, n, first + n)
        if looped:
            per = len(pieces(kt))
            use0 = proj.number[(name, 0)]
            with sp.Fori(1, total // RING) as i:
                for q in range(RING):
                    if kind == "branch":
                        if q < 3:
                            sp.wait_ge(s["w_split"], 3 * (i - 1) + (c.first_split[name] + q + 1))
                        else:
                            sp.wait_ge(proj.full_sem, 6 * (i - 1) + (use0 + 6))
                    elif name in SPLIT:
                        sp.wait_ge(s["w_split"], RING * (i - 1) + (c.first_split[name] + q + 1))
                    else:
                        sp.wait_ge(proj.full_sem, use0 + (RING // per) * (i - 1) + q // per + 1)
                    sp.dma_start(c.slot(first + q), d["w_" + name][bass.ds(i * RING + q, 1)].rearrange("o p f -> p (o f)")) \
                        .then_inc(c.landed[(first + q) % RING], 16)
    for k in range(KD):
        sp.wait_ge(s["out_ready"], k + 1)
        sp.dma_start(d["out"][k * P:(k + 1) * P, :], c.X(k)).then_inc(s["out_stored"], 16)
    sp.wait_ge(s["out_stored"], 16 * KD)


def chunk_use(c, chunk):
    name = [s[0] for s in STAGES if c.first_chunk[s[0]] <= chunk][-1]
    if name in SPLIT and (name != "br" or (chunk - c.first_chunk[name]) % 4 < 3):
        n = chunk - c.first_chunk[name]
        return c.sem["w_split"], c.first_split[name] + (n if name != "br" else 3 * (n // 4) + n % 4) + 1
    _, kind, tiles, kt = STAGE[name]
    n = chunk - c.first_chunk[name]
    if kind == "tok":
        toks = min(tiles, 4)
        t = toks * (n // 4) + (toks - 1 if n % 4 == 3 else 0)
    elif kind == "branch":
        t = 6 * (n // 4) + (n % 4 if n % 4 < 3 else 5)
    else:
        t = n // len(pieces(kt))
    return c.proj.filled((name, t))


def gpsimd_program(nc, pool, c):
    d, s = c.dram, c.sem
    row = lambda ap: ap.partition_broadcast(P)
    pool.dma_start(c.cond[:, 0:D], row(d["c"])).then_inc(s["c_loaded"], 16)
    for dst, src in (
        (c.T(31).bitcast(I32), row(d["positions"])),
        (c.wsmall[:, :], d["w_small"]), (c.gate_up[:, :], d["gla_gate_up"]), (c.m_bias[:, :], d["m_bias"]),
    ):
        pool.dma_start(dst, src).then_inc(s["setup"], 16)

    def modulation(first, count):
        dram = first + len(FIRST_ROWS)
        for q in range(ADA_RING):
            if first > 0:
                pool.wait_ge(s["ada_used"], first + q - ADA_RING + 1)
            pool.dma_start(c.ada_slot(first + q), d["ada"][dram + q]).then_inc(c.ada_landed[q], 16)
        with pool.Fori(1, count // ADA_RING) as i:
            for q in range(ADA_RING):
                pool.wait_ge(s["ada_used"], i * ADA_RING + (first + q - ADA_RING + 1))
                pool.dma_start(c.ada_slot(first + q), d["ada"][bass.ds(i * ADA_RING + (dram + q), 1)].rearrange("o p f -> p (o f)")) \
                    .then_inc(c.ada_landed[q], 16)

    pool.wait_ge(c.first_rows[3], 16 * 4)
    modulation(0, 32)
    for dst, src in (
        (c.sgu_norm[:, :], row(d["sgu_norm"])), (c.small[:, 0:8], row(d["decay"])),
    ):
        pool.dma_start(dst, src).then_inc(s["late"], 16)
    pool.wait_ge(s["gla_ready"], 2)
    modulation(32, 48)
    pool.wait_ge(*c.proj.filled(("up0", 2 * FT - 1)))
    pool.dma_start(c.pool_w, d["pool_w"]).then_inc(s["pool_loaded"], 16)
    pool.wait_ge(s["ada_used"], 80)
    pool.dma_start(c.cond[:, 0:D], row(d["c_3"])).then_inc(s["cond_loaded"], 16)
    pool.dma_start(c.cond[:, D:2 * D], row(d["c_ctx_3"])).then_inc(s["cond_loaded"], 16)
    modulation(80, 48)
    pool.wait_ge(*c.proj.filled(("dn3", 7)))
    pool.dma_start(c.T(24, 4).rearrange("p (k t) -> p k t", k=KD), d["ctx"].rearrange("(k p) t -> p k t", p=P)).then_inc(s["ctx_loaded"], 16)
    pool.dma_start(c.T(41, 2), d["grid"]).then_inc(s["ctx_loaded"], 16)
    pool.wait_ge(*c.mix.filled(("ss", 8)))
    pool.dma_start(c.T(47, 6), d["dist"]).then_inc(s["ctx_loaded"], 16)
    pool.wait_ge(*c.mix.filled(("rs", 3, 5)))
    pool.dma_start(c.T(16, 8), d["dft"]).then_inc(s["dft_loaded"], 16)
    pool.dma_start(c.sgu_w, d["sgu_w"]).then_inc(s["dft_loaded"], 16)
    pool.dma_start(c.sgu_b, row(d["sgu_b"])).then_inc(s["dft_loaded"], 16)



def tensor_program(nc, pe, c):
    s, proj, mix, T, H = c.sem, c.proj, c.mix, c.T, c.H
    mm = nc.tensor.matmul

    def open_bank(ring, key):
        pe.wait_ge(*ring.may_fill(key))
        return ring.bank(key)

    def feature_tile(name, t, rhs, n=S, ready=None):
        bank = open_bank(proj, (name, t))
        per = pieces(STAGE[name][3])
        k = 0
        for q, size in enumerate(per):
            chunk = c.first_chunk[name] + t * len(per) + q
            pe.wait_ge(*c.chunk_landed(chunk))
            for i in range(size):
                if ready is not None:
                    pe.wait_ge(*ready(k))
                last = mm(bank[:, 0:n], c.slot(chunk)[:, i * P:(i + 1) * P], rhs(k), start=k == 0, stop=k == sum(per) - 1)
                k += 1
        last.then_inc(proj.full_sem, 1)

    def feature_loop(name, rhs, ready, body=RING):
        _, _, tiles, kt = STAGE[name]
        per = pieces(kt)
        use0, chunk0 = proj.number[(name, 0)], c.first_chunk[name]
        with pe.Fori(0, tiles // body) as i:
            for j in range(body):
                u = use0 + j
                pe.wait_ge(proj.empty_sem[u % RING], i * (body // RING) + u // RING)
                k = 0
                for q, size in enumerate(per):
                    ch = chunk0 + j * len(per) + q
                    pe.wait_ge(c.landed[ch % RING], i * (16 * body * len(per) // RING) + 16 * (ch // RING + 1))
                    for n in range(size):
                        if j == 0 and ready(k) is not None:
                            pe.wait_ge(*ready(k))
                        last = mm(proj.banks[:, u % RING, :], c.slot(ch)[:, n * P:(n + 1) * P], rhs(k),
                                  start=k == 0, stop=k == kt - 1)
                        k += 1
                last.then_inc(proj.full_sem, 1)

    def first_pair(name, r, lo):
        split0 = c.first_split[name]
        for k in range(KD):
            pe.wait_ge(s["h_rounded"], 8 * SPLIT_NORMS.index(r) + k + 1)
            w = slice(k * P, (k + 1) * P)
            for t in range(2):
                bank = open_bank(proj, (name, t)) if k == 0 else proj.bank((name, t))
                if k == 0:
                    pe.wait_ge(s["w_split"], split0 + t + 1)
                mm(bank, c.hi(split0 + t)[:, w], c.H_hi(k), start=k == 0, stop=False)
                mm(bank, c.lo(split0 + t)[:, w], c.H_hi(k), start=False, stop=False)
        for t in range(2):
            for k in range(KD):
                if t == 0:
                    pe.wait_ge(s["h_ready"], h_count(r, k))
                last = mm(proj.bank((name, t)), c.hi(split0 + t)[:, k * P:(k + 1) * P], lo(k), start=False, stop=k == KD - 1)
            last.then_inc(proj.full_sem, 1)

    def split_loop(name, hi, lo, ready, norm=None):
        _, _, tiles, kt = STAGE[name]
        per = pieces(kt)
        use0, split0 = proj.number[(name, 0)], c.first_split[name]

        def four_tiles(i, first=0):
            for j in range(first, 4):
                u = use0 + j
                pe.wait_ge(proj.empty_sem[u % RING], i + u // RING)
                k = 0
                for q, size in enumerate(per):
                    n = j * len(per) + q
                    pe.wait_ge(s["w_split"], i * (4 * len(per)) + (split0 + n + 1))
                    for b in range(size):
                        if j == 0 and ready is not None and ready(k) is not None:
                            pe.wait_ge(*ready(k))
                        w = slice(b * P, (b + 1) * P)
                        for m, (stationary, moving) in enumerate(((c.hi, hi), (c.hi, lo), (c.lo, hi))):
                            last = mm(proj.banks[:, u % RING, :], stationary(split0 + n)[:, w], moving(k),
                                      start=k + m == 0, stop=k == kt - 1 and m == 2)
                        k += 1
                    if q < len(per) - 1:
                        last.then_inc(s["w_used"], 1)
                last.then_inc(proj.full_sem, 1)

        if norm is not None:
            first_pair(name, norm, lo)
            four_tiles(0, first=2)
        with pe.Fori(0 if norm is None else 1, tiles // 4) as i:
            four_tiles(i)

    def split_feature_tile(name, t, hi, lo):
        bank, n = open_bank(proj, (name, t)), c.first_split[name] + t
        pe.wait_ge(s["w_split"], n + 1)
        for k in range(KD):
            w = slice(k * P, (k + 1) * P)
            for m, (stationary, moving) in enumerate(((c.hi, hi), (c.hi, lo), (c.lo, hi))):
                last = mm(bank, stationary(n)[:, w], moving(k), start=k + m == 0, stop=k == KD - 1 and m == 2)
        last.then_inc(proj.full_sem, 1)

    def split_token_tiles(name, part, hi, lo):
        for q in range(4):
            n = c.first_split[name] + 4 * part + q
            pe.wait_ge(s["w_split"], n + 1)
            for t in range(NB):
                key = (name, NB * part + t)
                bank = open_bank(proj, key) if q == 0 else proj.bank(key)
                for i in range(2):
                    k = 2 * q + i
                    for m, (stationary, moving) in enumerate(((hi, c.hi), (lo, c.hi), (hi, c.lo))):
                        last = mm(bank, stationary(k)[:, t * P:(t + 1) * P], moving(n)[:, i * S:(i + 1) * S],
                                  start=k + m == 0, stop=k == KD - 1 and m == 2)
                if q == 3:
                    last.then_inc(proj.full_sem, 1)
                elif t == NB - 1:
                    last.then_inc(s["w_used"], 1)

    def token_tiles(name, part, lhs, toks=4):
        for q in range(4):
            chunk = c.first_chunk[name] + 4 * part + q
            pe.wait_ge(*c.chunk_landed(chunk))
            for t in range(toks):
                key = (name, toks * part + t)
                bank = open_bank(proj, key) if q == 0 else proj.bank(key)
                for i in range(2):
                    k = 2 * q + i
                    last = mm(bank, lhs(k, t), c.slot(chunk)[:, i * S:(i + 1) * S], start=k == 0, stop=k == 7)
                if q == 3:
                    last.then_inc(proj.full_sem, 1)

    def sum_squares(key, ready, tile, count, n=S):
        bank = open_bank(mix, key)
        for k in range(count):
            pe.wait_ge(*ready(k))
            last = mm(bank[:, 0:n], c.square("ones"), tile(k), start=k == 0, stop=k == count - 1)
        last.then_inc(mix.full_sem, 1)

    def norm(r):
        sum_squares(("ss", r), lambda k: (s["sq_ready"], 8 * r + k + 1), lambda k: T(squares_at(r) + k), KD)

    def swap(key, name, src):
        mm(open_bank(mix, key), c.square(name), src, start=True, stop=True).then_inc(mix.full_sem, 1)

    def h_ready(r):
        return lambda k: (s["h_ready"], h_count(r, k))

    def h_tok(k, t):
        return c.h[:, k * S + t * P:k * S + (t + 1) * P]

    def mixed(n, more=()):
        def ready(k):
            if k > 0:
                return None
            for w in more:
                pe.wait_ge(*w)
            return s["mixed"], n
        return ready

    pe.wait_ge(s["constants"], 16 * 3)
    pe.wait_ge(s["setup"], 16 * 4)
    norm(0)
    for t in range(6):
        if t < 5:
            feature_tile(*(("iq", t) if t < 4 else ("ik", 0)), H, ready=h_ready(0))
        if t >= 1:
            pe.wait_ge(*proj.emptied(("iq", t - 1) if t < 5 else ("ik", 0)))
            swap(("rot_i", t - 1), "swap32", T(5 + t - 1))
        if t == 4:
            for n in range(NB):
                bank = open_bank(proj, ("iw", n))
                for k in range(KD):
                    last = mm(bank[:, 0:8], h_tok(k, n), c.wsmall[:, 32 * k + 16:32 * k + 24], start=k == 0, stop=k == 7)
                last.then_inc(proj.full_sem, 1)
            bank = open_bank(proj, ("glow", 0))
            for k in range(KD):
                last = mm(bank[0:16, :], c.wsmall[:, 32 * k:32 * k + 16], H(k), start=k == 0, stop=k == 7)
            last.then_inc(proj.full_sem, 1)
    pe.wait_ge(s["iq_ready"], 5)
    for b in range(1, NB):
        for h in range(8):
            r, n = 64 * (h % 2), P * (b + 1)
            q = T(h // 2)[r:r + 64, b * P:(b + 1) * P]
            mm(open_bank(mix, ("idx", b, h))[:, 0:n], q, T(4)[r:r + 64, 0:n], start=True, stop=True).then_inc(mix.full_sem, 1)
    pe.wait_ge(*proj.emptied(("glow", 0)))
    for t in range(2):
        mm(open_bank(mix, ("gate", t)), c.gate_up[0:16, t * P:(t + 1) * P], T(53)[0:16, :], start=True, stop=True) \
            .then_inc(mix.full_sem, 1)
    for name in ("gr", "gq", "gk"):
        for t in range(STAGE[name][2]):
            feature_tile(name, t, H)
    token_tiles("gv", 0, h_tok)
    token_tiles("dv", 0, h_tok)
    for t in range(10):
        if t < 8:
            feature_tile("dq" if t < 4 else "dk", t % 4, H)
        if 1 <= t <= 8:
            pe.wait_ge(*proj.emptied(("dq" if t <= 4 else "dk", (t - 1) % 4)))
            mm(open_bank(mix, ("stat_d", t - 1)), c.square("ones"), T(48 + (t - 1) % 2), start=True, stop=True).then_inc(mix.full_sem, 1)
        if t >= 2:
            pe.wait_ge(s["head_normed"], t - 1)
            swap(("rot_d", t - 2), "swap64", T(38 + t - 2))
    pe.wait_ge(s["gla_ready"], 2)
    for t in range(2):
        bank = open_bank(mix, ("kdt", t))
        for n in range(NB):
            last = nc.tensor.transpose(bank[:, n * P:(n + 1) * P], T(28 + t)[:, n * P:(n + 1) * P], c.square("ident"))
        last.then_inc(mix.full_sem, 1)
    for h in range(4):
        bank, r = open_bank(mix, ("att", h)), 64 * (h % 2)
        for n in range(NB):
            w = slice(n * P, (n + 1) * P)
            last = mm(bank[:, w], T(54 + h // 2)[r:r + 64, w], T(12 + h // 2)[r:r + 64, w], start=True, stop=True)
        last.then_inc(mix.full_sem, 1)
    for t in range(2):
        pe.wait_ge(*mix.emptied(("kdt", t)))
        for e in range(2):
            bank = open_bank(mix, ("kv", t, e))
            for n in range(NB - e):
                for hh in range(2):
                    last = mm(bank[64 * hh:64 * hh + 64, n * P:(n + 1) * P],
                              T(14 + t)[64 * e:64 * e + 64, n * P + 64 * hh:n * P + 64 * hh + 64],
                              T(30 + n)[64 * e:64 * e + 64, (2 * t + hh) * P:(2 * t + hh + 1) * P], start=True, stop=True)
            last.then_inc(mix.full_sem, 1)
    for h in range(5):
        if h < 4:
            t, r = h // 2, 64 * (h % 2)
            pe.wait_ge(*mix.emptied(("att", h)))
            pe.wait_ge(s["state_ready"], 7 * (t + 1))
            bank = open_bank(mix, ("o", h))
            for n in range(NB):
                w = slice(n * P, (n + 1) * P)
                mm(bank[:, w], T(30 + n)[:, h * P:(h + 1) * P], T(ATT[h])[:, w], start=n == 0, stop=False, skip_group_check=True)
                for ch in (2 * n, 2 * n + 1):
                    if ch > 0:
                        w = slice(ch * CHUNK, (ch + 1) * CHUNK)
                        last = mm(bank[:, w], T(5 + 2 * t, 2)[r:r + 64, ch * P:(ch + 1) * P], T(26 + t)[r:r + 64, w],
                                  start=False, stop=ch == NCH - 1, skip_group_check=True)
            last.then_inc(mix.full_sem, 1)
        if h >= 1:
            pe.wait_ge(*mix.emptied(("o", h - 1)))
            mm(open_bank(mix, ("stat_o", h - 1)), c.square("ones"), T(48 + (h - 1) % 2), start=True, stop=True).then_inc(mix.full_sem, 1)
    units = [(b, h) for b in range(NB) for h in range(4)]
    pe.wait_ge(s["head_roped"], 8)
    for n in range(len(units) + 2):
        if n < 16:
            b, h = units[n]
            mm(open_bank(mix, ("qk", b, h))[:, 0:P * (b + 1)], T(38 + h)[:, b * P:(b + 1) * P], T(42 + h)[:, 0:P * (b + 1)],
               start=True, stop=True).then_inc(mix.full_sem, 1)
        if 1 <= n <= 16:
            b, h = units[n - 1]
            pe.wait_ge(s["pn_ready"], n)
            bank = open_bank(mix, ("pT", b, h))
            for j in range(b + 1):
                last = nc.tensor.transpose(bank[:, j * P:(j + 1) * P], T((n - 1) % 2)[:, j * P:(j + 1) * P], c.square("ident"))
            last.then_inc(mix.full_sem, 1)
        if n >= 2:
            b, h = units[n - 2]
            pe.wait_ge(*mix.emptied(("pT", b, h)))
            bank = open_bank(mix, ("av", b, h))
            for j in range(b + 1):
                last = mm(bank[:, 0:P], T(34 + j)[:, h * P:(h + 1) * P], T(2 + n % 2)[:, j * P:(j + 1) * P], start=j == 0, stop=j == b)
            last.then_inc(mix.full_sem, 1)
    feature_loop("abo", H, mixed(4, [mix.emptied(("av", NB - 1, 3))]))

    def feed_forward(layer):
        r = 2 * layer + 1
        norm(r)
        split_loop(f"up{layer}", c.H_hi, c.H_lo, None, norm=r)

        def mid(k):
            if k not in (0, 18, 20, 21):
                return None
            k = 17 if k == 0 else 19 if k == 18 else k
            return s["mid_ready"], 2 + FT * layer + k + 1

        def tile(of):
            return lambda k: of[:, k * S:(k + 1) * S]
        split_loop(f"dn{layer}", tile(c.mid_hi), tile(c.mid_lo), mid)

    feed_forward(0)
    norm(2)
    first_pair("cu", 2, c.H_lo)
    for t in range(2, 4):
        split_feature_tile("cu", t, c.H_hi, c.H_lo)
    for t in range(9):
        if t < 8:
            split_feature_tile("sq" if t < 4 else "sk", t % 4, c.H_hi, c.H_lo)
        if t >= 1:
            pe.wait_ge(*proj.emptied(("sq" if t <= 4 else "sk", (t - 1) % 4)))
            mm(open_bank(mix, ("stat_s", t - 1)), c.square("ones"), T(20 + (t - 1) % 2), start=True, stop=True).then_inc(mix.full_sem, 1)
    split_token_tiles("sv", 0, c.H_hi, c.H_lo)
    for g in range(4):
        pe.wait_ge(s["pooled"], g + 1)
        if g == 0:
            pe.wait_ge(s["pool_loaded"], 16)
        mm(open_bank(mix, ("pool", g)), c.pool_w[:, g * P:(g + 1) * P], T(6 + g), start=True, stop=True).then_inc(mix.full_sem, 1)
    pe.wait_ge(s["head_normed"], 8 + 4 + 8)
    pe.wait_ge(*proj.emptied(("sv", 3)))
    for h in range(6):
        if h < 4:
            for j in range(NB):
                mm(open_bank(mix, ("z", h, j))[:, 0:S - P * j], T(14 + h)[:, j * P:(j + 1) * P], T(10 + h)[:, j * P:S],
                   start=True, stop=True).then_inc(mix.full_sem, 1)
        if 1 <= h <= 4:
            pe.wait_ge(s["sp_ready"], h)
            sp = T(34 + 3 * ((h - 1) % 2), 3)
            for j in range(NB):
                bank = open_bank(mix, ("cum", h - 1, j))
                last = mm(bank[:, 0:S - P * j], c.square("later"), sp[:, TRI[j]:TRI[j + 1]], start=True, stop=j == NB - 1, skip_group_check=True)
                for i in range(j + 1, NB):
                    last = mm(bank[:, P * (i - j):S - P * j], c.square("ones"), sp[:, TRI[i]:TRI[i + 1]], start=False,
                              stop=i == NB - 1, skip_group_check=True)
                last.then_inc(mix.full_sem, 1)
        if h >= 2:
            pe.wait_ge(s["w_ready"], h - 1)
            w = T(40 + 3 * (h % 2), 3)
            bank = open_bank(mix, ("sb", h - 2))
            for j in range(NB):
                last = mm(bank[:, P * j:S], T(24 + j)[:, (h - 2) * P:(h - 1) * P], w[:, TRI[j]:TRI[j + 1]], start=j == 0,
                          stop=j == NB - 1, skip_group_check=True)
            last.then_inc(mix.full_sem, 1)
    feature_loop("cdo", H, lambda k: mix.emptied(("sb", 3)) if k == 0 else None)
    feed_forward(1)
    norm(4)
    m_lo = lambda k: c.norm_lo(4, k)
    first_pair("mqk", 4, m_lo)
    for t in range(2, 8):
        split_feature_tile("mqk", t, c.H_hi, m_lo)
    for part in range(2):
        split_token_tiles("mv", part, c.H_hi, m_lo)
    for t in range(8):
        split_feature_tile("mo", t, c.H_hi, m_lo)
    for n, key in enumerate((("mi", 0), ("mf", 0))):
        bank = open_bank(proj, key)
        for k in range(KD):
            last = mm(bank[0:4, :], c.wsmall[:, 32 * k + 24 + 4 * n:32 * k + 28 + 4 * n], H(k), start=k == 0, stop=k == 7)
        last.then_inc(proj.full_sem, 1)
    pe.wait_ge(s["m_rows"], 1)
    bank = open_bank(mix, ("acol", 0))
    for j in range(NB):
        last = nc.tensor.transpose(bank[:, 4 * j:4 * j + 4], T(29)[0:4, j * P:(j + 1) * P], c.square("ident")[0:4, 0:4])
    last.then_inc(mix.full_sem, 1)
    pe.wait_ge(s["m_guard"], 1)

    def spread(h):
        for n, row in enumerate((T(31), T(28))):
            mm(open_bank(mix, ("mbc", h, n)), c.const("sel")[0:4, h * P:(h + 1) * P], row[0:4, :], start=True, stop=True) \
                .then_inc(mix.full_sem, 1)

    spread(0)
    for h in range(4):
        if h == 0:
            pe.wait_ge(s["conv_act"], 8)
        for j in range(NB):
            mm(open_bank(mix, ("ms", h, j))[:, 0:S - P * j], T(4 + h)[:, j * P:(j + 1) * P], T(h)[:, P * j:S],
               start=True, stop=True).then_inc(mix.full_sem, 1)
        if h < 3:
            spread(h + 1)
        p = T(38 + 3 * (h % 2), 3)
        for n in range(3):
            bank = open_bank(mix, ("mn", h, n) if n < 2 else ("md", h))
            for j in range(NB):
                if n == 0:
                    pe.wait_ge(*mix.emptied(("ms", h, j)))
                v = T(8 + 2 * j, 2)[:, (2 * h + n) * P:(2 * h + n + 1) * P] if n < 2 else c.square("ones")
                last = mm(bank[:, P * j:S], v, p[:, TRI[j]:TRI[j + 1]], start=j == 0, stop=j == NB - 1, skip_group_check=True)
            last.then_inc(mix.full_sem, 1)
        sum_squares(("stat_m", h), lambda k: (s["hsq_ready"], 2 * h + k + 1), lambda k: T(36 + k), 2)
    feature_loop("mout", H, mixed(MIXED_M))
    feed_forward(2)
    norm(6)
    feature_loop("ca", H, h_ready(6))
    sum_squares(("lnm", 0), lambda k: (s["u_ready"], k + 1), lambda k: T(11 + k), KD)
    sum_squares(("lnv", 0), lambda k: (s["u_sq"], k + 1), lambda k: T(SQ0 + k), KD)
    feature_loop("cout", H, lambda k: (s["u_act"], k + 1))
    feed_forward(3)
    norm(8)
    sum_squares(("ssc", 0), lambda k: (s["u_sq"], 8 + k + 1), lambda k: T(8, 4)[:, k * CTX:(k + 1) * CTX], KD, n=CTX)
    norm(9)
    hc = lambda k: T(28, 4)[:, k * CTX:(k + 1) * CTX]
    hi9 = lambda k: c.norm_hi(9, k)
    for t in range(4):
        feature_tile("ck", t, hc, n=CTX, ready=lambda k: (s["hc_ready"], k + 1))
    token_tiles("cv", 0, lambda k, t: hc(k)[:, t * P:(t + 1) * P], toks=2)
    for t in range(9):
        if t < 8:
            if t == 0:
                pe.wait_ge(s["h_ready"], h_count(9, KD - 1))
            split_feature_tile("rk" if t < 4 else "rq", t % 4, hi9, c.H_lo)
        if t >= 1:
            pe.wait_ge(*proj.emptied(("rk" if t <= 4 else "rq", (t - 1) % 4)))
            swap(("rot_r", t - 1), "swap64", T(24 + (t - 1) % 2))
    split_token_tiles("rv", 0, hi9, c.H_lo)
    split_token_tiles("fv", 0, hi9, c.H_lo)
    for name in ("ru", "rg"):
        for t in range(STAGE[name][2]):
            split_feature_tile(name, t, hi9, c.H_lo)
    pe.wait_ge(s["head_roped"], 16)
    for h in range(4):
        for j in range(6):
            keys = T(16 + h)[:, j * P:(j + 1) * P] if j < 4 else T(12, 2)[:, h * CTX + (j - 4) * P:h * CTX + (j - 3) * P]
            mm(open_bank(mix, ("rs", h, j)), keys, T(20 + h), start=True, stop=True).then_inc(mix.full_sem, 1)
        bank = open_bank(mix, ("rout", h))
        for j in range(6):
            pe.wait_ge(*mix.emptied(("rs", h, j)))
            v = T(27 + j) if j < 4 else T(14 + j - 4)
            last = mm(bank, v[:, h * P:(h + 1) * P], T(RP[j]), start=j == 0, stop=j == 5)
        last.then_inc(mix.full_sem, 1)
        pe.wait_ge(*mix.emptied(("rout", h)))
        mm(open_bank(mix, ("stat_r", h)), c.square("ones"), c.late_tile(0), start=True, stop=True).then_inc(mix.full_sem, 1)
    pe.wait_ge(s["dft_loaded"], 48)
    for t in range(2):
        for n in range(2):
            bank = open_bank(mix, ("dftl", t, n))
            for j in range(NB):
                last = mm(bank, T(31, 2)[:, j * 256 + t * P:j * 256 + (t + 1) * P], T(16 + 4 * n + j), start=j == 0, stop=j == NB - 1)
            last.then_inc(mix.full_sem, 1)
    for t in range(2):
        pe.wait_ge(*mix.emptied(("dftl", t, 1)))
        bank = open_bank(mix, ("four", t))
        mm(bank, c.square("dft_cos"), T(53 + t), start=True, stop=False)
        mm(bank, c.square("dft_sin"), T(55 + t), start=False, stop=True).then_inc(mix.full_sem, 1)
    pe.wait_ge(s["vs_ready"], 1)
    pe.wait_ge(s["late"], 16 * 2)
    for t in range(2):
        bank = open_bank(mix, ("sgu", t))
        for n in range(NB):
            for g in range(2):
                last = mm(bank[64 * g:64 * g + 64, n * P:(n + 1) * P],
                          T(33, 2)[:, n * 256 + (2 * t + g) * 64:n * 256 + (2 * t + g) * 64 + 64],
                          c.sgu_w[:, (2 * t + g) * P:(2 * t + g + 1) * P], start=True, stop=True)
        last.then_inc(mix.full_sem, 1)
    use0, chunk0 = proj.number[("br", 0)], c.first_chunk["br"]
    pe.wait_ge(s["mixed"], MIXED_M + 4)
    pe.wait_ge(*mix.emptied(("four", 1)))
    pe.wait_ge(s["sgu_ready"], 2)
    with pe.Fori(0, 4) as i:
        for j in range(12):
            u, n, g = use0 + j, j // 6, j % 6
            pe.wait_ge(proj.empty_sem[u % RING], i * 3 + u // RING)
            ch = chunk0 + 4 * n + min(g, 3)
            if g < 3:
                sn = c.first_split["br"] + 3 * n + g
                pe.wait_ge(s["w_split"], i * 6 + (sn + 1))
                for k in range(KD):
                    w = slice(k * P, (k + 1) * P)
                    for m, (stationary, moving) in enumerate(((c.hi, hi9), (c.hi, c.H_lo), (c.lo, hi9))):
                        last = mm(proj.banks[:, u % RING, :], stationary(sn)[:, w], moving(k), start=k + m == 0, stop=k == KD - 1 and m == 2)
                last.then_inc(proj.full_sem, 1)
                continue
            pe.wait_ge(c.landed[ch % RING], i * 32 + 16 * (ch // RING + 1))
            srcs = [[T(8 + k) for k in range(4)], [c.late_tile(2), c.late_tile(3)], [c.late_tile(4), c.late_tile(5)]][g - 3]
            at = (0, 4, 6)[g - 3]
            for k, src in enumerate(srcs):
                last = mm(proj.banks[:, u % RING, :], c.slot(ch)[:, (at + k) * P:(at + k + 1) * P], src,
                          start=k == 0, stop=k == len(srcs) - 1)
            last.then_inc(proj.full_sem, 1)
    feature_loop("ro", lambda k: T(16 + k), lambda k: (s["merged"], k + 1))
    sum_squares(("ssy", 0), lambda k: proj.emptied(("ro", k)), lambda k: T(SQ0 + k), KD)
    norm(10)
    split_loop("upr", c.H_hi, c.H_lo, None, norm=10)
    feature_loop("dnr", T, lambda k: (s["mlp_mid"], 4 + (28 if k == 0 else k + 1)) if k == 0 or k >= 28 else None)
    sum_squares(("ssy", 1), lambda k: proj.emptied(("dnr", k)), lambda k: T(SQ0 + k), KD)


ATT = (16, 20, 21, 9)
TRI = (0, 512, 896, 1152, 1280)
RP = (24, 25, 26, 53, 54, 55)
MIXED_M = 12



def scalar_program(nc, act, c):
    s, proj, mix, T, H, X = c.sem, c.proj, c.mix, c.T, c.H, c.X
    st = Steps(act, s["act_chain"])

    def f(out, in_, func, **kw):
        return nc.scalar.activation(out, in_, func, **kw)

    def copy_out(ring, key, dst, func=ACT.Copy, rows=P, n=S, **kw):
        act.wait_ge(*ring.filled(key))
        st.last(f(dst, ring.bank(key)[0:rows, 0:n], func, **kw), ring.emptied(key))

    eps = c.const("eps")

    def root(key, dst, count, n=S):
        copy_out(mix, key, dst, ACT.Sqrt, n=n, scale=1.0 / count, bias=eps)

    def round_h(r, k):
        n = 8 * SPLIT_NORMS.index(r) + k + 1
        act.wait_ge(s["h_raw"], n)
        st.done(f(c.norm_hi(r, k), H(k), ACT.Copy), s["h_rounded"])

    def round_chunk(name, n):
        split, chunk = c.first_split[name] + n, c.first_chunk[name] + n
        if split >= SPLIT_RING:
            act.wait_ge(*split_use(c, split - SPLIT_RING))
        act.wait_ge(*c.chunk_landed(chunk))
        w = chunk_floats(name, n)
        st_round(f(c.hi(split)[:, 0:w], c.slot(chunk)[:, 0:w], ACT.Copy))

    def st_round(ins):
        ins.then_inc(s["w_rounded"], 1)

    def round_ahead(name, i, j):
        split, chunk = c.first_split[name] + j + SPLIT_RING, c.first_chunk[name] + j + SPLIT_RING
        act.wait_ge(c.landed[chunk % RING], i * 16 + 16 * (chunk // RING + 1))
        st_round(f(c.hi(split), c.slot(chunk), ACT.Copy))

    def round_down(layer):
        for n in range(SPLIT_RING, 3 * KD):
            round_chunk(f"dn{layer}", n)

    def norm(r):
        for k in range(KD):
            if r == 0:
                act.wait_ge(s["x_loaded"], 16)
            elif r in NORM_AFTER:
                act.wait_ge(*proj.emptied((NORM_AFTER[r], k)))
            else:
                act.wait_ge(s["x_ready"], 8 * (r - 9) + k + 1)
            st.done(f(T(squares_at(r) + k), X(k), ACT.Square), s["sq_ready"])
            if r in SPLIT_UP and k == KD - 2:
                up = SPLIT_UP[r]
                for n in range(SPLIT_RING):
                    round_chunk(up, n)
        root(("ss", r), T(RSTD), D)
        if r in MODULATED:
            use, layer, part, ready = MODULATED[r]
            act.wait_ge(s["mod_ready"], ready)
            for k in range(KD):
                act.wait_ge(s["xn_ready"], 8 * list(MODULATED).index(r) + k + 1)
                ins = f(H(k), H(k), ACT.Identity, scale=c.g(use, k), bias=c.m(layer, part, k))
                ins.then_inc(s["h_raw"] if r in SPLIT_NORMS else s["h_ready"], 1)
                if r in SPLIT_NORMS:
                    round_h(r, k)
        elif r in SPLIT_NORMS:
            for k in range(KD):
                round_h(r, k)

    def head_stat(ring, key, raw, sq):
        act.wait_ge(*ring.filled(key))
        f(raw, ring.bank(key), ACT.Copy)
        st.last(f(sq, ring.bank(key), ACT.Square), ring.emptied(key))

    for r, at in enumerate(FIRST_ROWS):
        act.dma_start(T(at, 2), c.dram["ada"][r]).then_inc(c.first_rows[r // 4], 16)
    act.wait_ge(s["c_loaded"], 16)
    st.done(f(c.cond[:, 0:D], c.cond[:, 0:D], ACT.Silu), s["cond_ready"])
    act.wait_ge(s["constants"], 16 * 3)
    act.wait_ge(s["setup"], 16 * 4)
    for n in range(4):
        act.wait_ge(s["pos_ready"], n + 1)
        st.done(f(T(10 + n), T(10 + n), ACT.Sin), s["trig_ready"])
    norm(0)
    for t in range(5):
        key = ("iq", t) if t < 4 else ("ik", 0)
        copy_out(proj, key, T(5 + t))
    for n in range(NB):
        copy_out(proj, ("iw", n), c.small[:, 8 + 8 * n:16 + 8 * n], n=8, scale=(8 ** -0.5) * (64 ** -0.5))
    copy_out(proj, ("glow", 0), T(53)[0:16, :], rows=16)
    n = 0
    for b in range(1, NB):
        for h in range(8):
            if n >= 2:
                act.wait_ge(s["idx_used"], n - 1)
            copy_out(mix, ("idx", b, h), T(20 + n % 2)[:, 0:P * (b + 1)], ACT.Relu, n=P * (b + 1))
            n += 1
    for t in range(2):
        act.wait_ge(*mix.filled(("gate", t)))
        f(T(54 + t), mix.bank(("gate", t)), ACT.Identity, bias=c.v("gla_gate_b", t))
        st.last(f(T(56 + t), mix.bank(("gate", t)), ACT.Abs, bias=c.v("gla_gate_b", t)), mix.emptied(("gate", t)))
    st.link(f(T(56, 2), T(56, 2), ACT.Exp, scale=-1.0))
    st.done(f(T(56, 2), T(56, 2), ACT.Ln, bias=c.const("one")), s["gate_ready"])
    for t in range(4):
        copy_out(proj, ("gr", t), T(22 + t), ACT.Silu)
    for t in range(2):
        copy_out(proj, ("gq", t), T(26 + t), scale=64 ** -0.5)
    for t in range(2):
        copy_out(proj, ("gk", t), T(28 + t))
    for t in range(4):
        copy_out(proj, ("gv", t), T(30 + t))
    for t in range(4):
        copy_out(proj, ("dv", t), T(34 + t))
    for t in range(2):
        act.wait_ge(s["span_ready"], t + 1)
        f(T(E_GLA[t][0]), T(12 + t), ACT.Exp, scale=1 / 16)
        f(T(E_GLA[t][1]), T(12 + t), ACT.Exp, scale=-1 / 16)
        f(T(E_GLA[t][2]), T(54 + t), ACT.Exp, scale=1 / 16)
        f(T(E_GLA[t][3]), T(56 + t), ACT.Exp, scale=1 / 16)
        last = T(56 + t).rearrange("p (n c) -> p n c", c=CHUNK)[:, :, CHUNK - 1:CHUNK]
        st.done(f(c.small[:, 40 + 8 * t:48 + 8 * t].unsqueeze(2), last, ACT.Exp, scale=1 / 16), s["decay_ready"])

    def d_key(t):
        return ("dq" if t < 4 else "dk", t % 4)

    for t in range(9):
        if t < 8:
            if t >= 2:
                act.wait_ge(s["head_normed"], t - 1)
            head_stat(proj, d_key(t), T(46 + t % 2), T(48 + t % 2))
        if t >= 1:
            root(("stat_d", t - 1), T(50 + (t - 1) % 2), P)
    for t in range(2):
        copy_out(mix, ("kdt", t), T(14 + t))
    for h in range(5):
        if h < 4:
            if h >= 2:
                act.wait_ge(s["head_normed"], 8 + h - 1)
            head_stat(mix, ("o", h), T(46 + h % 2), T(48 + h % 2))
        if h >= 1:
            root(("stat_o", h - 1), T(50 + (h - 1) % 2), P)
    units = [(b, h) for b in range(NB) for h in range(4)]
    for n in range(len(units) + 2):
        if n < 16:
            b, h = units[n]
            act.wait_ge(s["max_ready"], n + 1)
            z = T(n % 2)[:, 0:P * (b + 1)]
            st.done(f(z, z, ACT.Exp, scale=P ** -0.5, bias=c.small[:, 56 + n % 2:57 + n % 2],
                      accum_out=c.small[:, 58 + n % 2:59 + n % 2]), s["p_ready"])
        if 1 <= n <= 16:
            b, h = units[n - 1]
            if n >= 3:
                act.wait_ge(*mix.filled(("av", *units[n - 3])))
            copy_out(mix, ("pT", b, h), T(2 + (n - 1) % 2)[:, 0:P * (b + 1)], n=P * (b + 1))
        if n >= 2:
            b, h = units[n - 2]
            copy_out(mix, ("av", b, h), H(4 + h)[:, b * P:(b + 1) * P], n=P)

    def swiglu(layer):
        up = f"up{layer}"
        u0 = proj.number[(up, 0)]
        with act.Fori(0, 2 * FT // 4) as i:
            for j in range(4):
                u, p = u0 + j, j // 2
                act.wait_ge(proj.full_sem, i * 4 + u + 1)
                round_ahead(up, i, j)
                if j % 2 == 0:
                    act.wait_ge(s["mid_ready"], i * 2 + (FT * layer + p + 1))
                    f(T(52 + p), proj.banks[:, u % RING, :], ACT.Silu).then_inc(proj.empty_sem[u % RING], 1)
        round_down(layer)

    norm(1)
    swiglu(0)
    norm(2)

    def round_s(n):
        round_chunk(("cu", "sq", "sk", "sv")[n // 4], n % 4)

    for t in range(4):
        round_s(t + SPLIT_RING)
        copy_out(proj, ("cu", t), T(t))

    def s_key(t):
        return ("sq" if t < 4 else "sk", t % 4)

    for t in range(9):
        if t < 8:
            if t >= 2:
                act.wait_ge(s["head_normed"], 12 + t - 1)
            round_s(4 + t + SPLIT_RING)
            head_stat(proj, s_key(t), T(18 + t % 2), T(20 + t % 2))
        if t >= 1:
            root(("stat_s", t - 1), T(22 + (t - 1) % 2), P)
    for n in range(12 + SPLIT_RING, 16):
        round_s(n)
    for t in range(4):
        copy_out(proj, ("sv", t), T(24 + t))
    for g in range(4):
        copy_out(mix, ("pool", g), H(g), scale=c.v("pool_scale", g))
    for h in range(6):
        if h < 4:
            z, l = T(28 + 3 * (h % 2), 3), T(34 + 3 * (h % 2), 3)
            for j in range(NB):
                act.wait_ge(*mix.filled(("z", h, j)))
                bank = mix.bank(("z", h, j))[:, 0:S - P * j]
                f(z[:, TRI[j]:TRI[j + 1]], bank, ACT.Copy, scale=P ** -0.5)
                st.last(f(l[:, TRI[j]:TRI[j + 1]], bank, ACT.Abs, scale=P ** -0.5), mix.emptied(("z", h, j)))
            l = l[:, 0:TRI[4]]
            st.link(f(l, l, ACT.Exp, scale=-1.0))
            st.done(f(l, l, ACT.Ln, bias=c.const("one")), s["z_ready"])
        if 1 <= h <= 4:
            act.wait_ge(*mix.emptied(("cum", h - 1, 3)))
            z, w = T(28 + 3 * ((h - 1) % 2), 3)[:, 0:TRI[4]], T(40 + 3 * ((h - 1) % 2), 3)[:, 0:TRI[4]]
            st.done(f(w, z, ACT.Exp), s["w_ready"])
        if h >= 2:
            copy_out(mix, ("sb", h - 2), H(4 + h - 2))
    norm(3)
    act.wait_ge(s["cond_loaded"], 32)
    st.done(f(c.cond[:, :], c.cond[:, :], ACT.Silu), s["cond_ready"])
    swiglu(1)
    norm(4)

    def round_m(n):
        if n < 24:
            round_chunk(("mqk", "mv", "mo")[n // 8], n % 8)

    for t in range(9):
        if t < 8:
            act.wait_ge(*proj.filled(("mqk", t)))
            round_m(t + SPLIT_RING)
            st.done(f(T(t), proj.bank(("mqk", t)), ACT.Identity, scale=c.v("m_conv_w_2", 24 + t), bias=c.v("m_conv_b_2", t)), s["conv_init"])
        if t >= 1:
            act.wait_ge(*proj.emptied(("mqk", t - 1)))
            st.done(f(T(t - 1), T(t - 1), ACT.Silu), s["conv_act"])
    for part in range(2):
        for q in range(4):
            round_m(8 + 4 * part + q + SPLIT_RING)
        for t in range(4):
            copy_out(proj, ("mv", 4 * part + t), T(8 + 2 * t + part))
    for t in range(8):
        act.wait_ge(*proj.filled(("mo", t)))
        round_m(16 + t + SPLIT_RING)
        copy_out(proj, ("mo", t), T(16 + t), ACT.Sigmoid)
    copy_out(proj, ("mi", 0), T(24)[0:4, :], ACT.Identity, rows=4, bias=c.m_bias[0:4, 0:1])
    act.wait_ge(*proj.filled(("mf", 0)))
    f(T(25)[0:4, :], proj.bank(("mf", 0))[0:4, :], ACT.Identity, bias=c.m_bias[0:4, 1:2])
    st.last(f(T(26)[0:4, :], proj.bank(("mf", 0))[0:4, :], ACT.Abs, bias=c.m_bias[0:4, 1:2]), proj.emptied(("mf", 0)))
    st.link(f(T(26)[0:4, :], T(26)[0:4, :], ACT.Exp, scale=-1.0))
    st.done(f(T(26)[0:4, :], T(26)[0:4, :], ACT.Ln, bias=c.const("one")[0:4, :]), s["m_gate"])
    act.wait_ge(s["m_rows"], 1)
    st.done(f(T(28)[0:4, :], T(28)[0:4, :], ACT.Exp, scale=-1.0), s["m_guard"])
    copy_out(mix, ("acol", 0), c.small[:, 64:80], n=16)

    def decays(h):
        copy_out(mix, ("mbc", h, 0), T(32 + h % 2))
        copy_out(mix, ("mbc", h, 1), T(34 + h % 2))
        e = T(EH[h % 2], 3)[:, 0:TRI[4]]
        act.wait_ge(s["e_arg"], h + 1)
        st.done(f(e, e, ACT.Exp), s["e_ready"])

    decays(0)
    for h in range(4):
        if h < 3:
            decays(h + 1)
        copy_out(mix, ("md", h), T(47), ACT.Abs)
        for k in range(2):
            act.wait_ge(s["hm_ready"], 2 * h + k + 1)
            st.done(f(T(36 + k), T(48 + 2 * (h % 2) + k), ACT.Square), s["hsq_ready"])
        root(("stat_m", h), T(52), 2 * P)

    def conv_ffn(layer):
        up = f"up{layer}"
        u0 = proj.number[(up, 0)]
        w0 = VCOL["f_conv_w_2"] + 3 * 2 * FT * (layer - 2) + 2 * 2 * FT
        b0 = VCOL["f_conv_b_2"] + 2 * FT * (layer - 2)
        with act.Fori(0, 2 * FT // 4) as i:
            for p in range(2):
                for g in range(2):
                    u = u0 + 2 * p + g
                    act.wait_ge(proj.full_sem, i * 4 + u + 1)
                    round_ahead(up, i, 2 * p + g)
                    if g == 0:
                        act.wait_ge(s["mid_ready"], i * 2 + (FT * layer + p + 1))
                    col = FT * g + p
                    f(T(52 + 2 * p + g), proj.banks[:, u % RING, :], ACT.Identity,
                      scale=c.vec[:, bass.ds(i * 2 + (w0 + col), 1)], bias=c.vec[:, bass.ds(i * 2 + (b0 + col), 1)]) \
                        .then_inc(s["conv_init"], 1)
                u = u0 + 2 * p
                act.wait_ge(proj.empty_sem[u % RING], i + u // RING + 1)
                f(T(52 + 2 * p), T(52 + 2 * p), ACT.Silu).then_inc(s["conv_act"], 1)
        round_down(layer)

    norm(5)
    conv_ffn(2)
    norm(6)
    for t in range(8):
        if t >= 2:
            act.wait_ge(*proj.emptied(("ca", 2 * t - 4)))
        copy_out(proj, ("ca", 2 * t + 1), T(9 + t % 2), ACT.Sigmoid, bias=c.v("c_b_in_2", 8 + t))
    for k in range(KD):
        act.wait_ge(s["u_centred"], k + 1)
        st.done(f(T(SQ0 + k), T(11 + k), ACT.Square), s["u_sq"])
    root(("lnv", 0), T(RSTD), D)
    for k in range(KD):
        act.wait_ge(s["u_normed"], k + 1)
        st.done(f(H(k), T(11 + k), ACT.Silu, scale=c.v("c_ln_g_2", k), bias=c.v("c_ln_b_2", k)), s["u_act"])
    norm(7)
    conv_ffn(3)
    norm(8)
    act.wait_ge(s["ctx_loaded"], 48)
    for k in range(KD):
        st.done(f(T(8, 4)[:, k * CTX:(k + 1) * CTX], T(24, 4)[:, k * CTX:(k + 1) * CTX], ACT.Square), s["u_sq"])
    root(("ssc", 0), T(12)[:, 0:CTX], D, n=CTX)
    act.wait_ge(s["mod_ready"], 5)
    for k in range(KD):
        act.wait_ge(s["u_centred"], 8 + k + 1)
        hc = T(28, 4)[:, k * CTX:(k + 1) * CTX]
        st.done(f(hc, hc, ACT.Identity, scale=c.g(6, k), bias=c.m(3, 0, k)), s["hc_ready"])
    act.wait_ge(s["late"], 16 * 2)
    st.link(f(c.small[:, 80:88], c.small[:, 0:8], ACT.Abs))
    st.link(f(c.small[:, 80:88], c.small[:, 80:88], ACT.Exp, scale=-1.0))
    st.done(f(c.small[:, 88:96], c.small[:, 80:88], ACT.Ln, bias=c.const("one")), s["lg_abs"])
    norm(9)
    for t in range(4):
        copy_out(proj, ("ck", t), T(12, 2)[:, t * CTX:(t + 1) * CTX], n=CTX, scale=P ** -0.5)
    for t in range(2):
        copy_out(proj, ("cv", t), T(14 + t))

    def round_r(n):
        round_chunk(*R_CHUNKS[n])

    for n in range(SPLIT_RING):
        round_r(n)
    for t in range(8):
        if t >= 2:
            act.wait_ge(s["head_roped"], 8 + t - 1)
        round_r(t + SPLIT_RING)
        copy_out(proj, ("rk" if t < 4 else "rq", t % 4), T(24 + t % 2), scale=P ** -0.5 if t < 4 else 1.0)
    for n in range(8 + SPLIT_RING, 12 + SPLIT_RING):
        round_r(n)
    for t in range(4):
        copy_out(proj, ("rv", t), T(27 + t))
    for n in range(12 + SPLIT_RING, 16 + SPLIT_RING):
        round_r(n)
    for t in range(4):
        act.wait_ge(*proj.filled(("fv", t)))
        f(T(31, 2)[:, t * 256:(t + 1) * 256], proj.bank(("fv", t))[:, 0:256], ACT.Copy)
        st.last(f(T(33, 2)[:, t * 256:(t + 1) * 256], proj.bank(("fv", t))[:, 256:512], ACT.Gelu_apprx_tanh), proj.emptied(("fv", t)))
    for t in range(2):
        round_r(16 + t + SPLIT_RING)
        copy_out(proj, ("ru", t), T(35 + t), ACT.Gelu_apprx_tanh)
    for t in range(4):
        round_r(18 + t + SPLIT_RING)
        copy_out(proj, ("rg", t), T(37 + t), ACT.Silu)
    act.wait_ge(s["vs_var"], 1)
    st.done(f(c.small[:, 96:112], c.small[:, 96:112], ACT.Sqrt, scale=1 / 64, bias=eps), s["vs_std"])
    for h in range(4):
        for n, (at, width) in enumerate(TABLES):
            act.wait_ge(s["table_arg"], 3 * h + n + 1)
            st.done(f(T(at, 2)[:, 0:width], T(at, 2)[:, 0:width], ACT.Exp), s["table_ready"])
        if h >= 1:
            act.wait_ge(s["mixed"], MIXED_M + h)
        head_stat(mix, ("rout", h), T(57), c.late_tile(0))
        root(("stat_r", h), c.late_tile(1), P)
    for t in range(2):
        for n in range(2):
            copy_out(mix, ("dftl", t, n), T(53 + 2 * n + t))
    act.wait_ge(s["mixed"], MIXED_M + 4)
    for t in range(2):
        copy_out(mix, ("four", t), c.late_tile(2 + t))
    u0 = proj.number[("br", 0)]

    def gate_tiles(i, last=False):
        for n in range(2):
            for g in range(3):
                u = u0 + 6 * n + g
                act.wait_ge(proj.full_sem, i * 12 + u + 1)
                ahead = 3 * n + g + SPLIT_RING
                if not (last and ahead >= 6):
                    split, chunk = c.first_split["br"] + ahead, c.first_chunk["br"] + 4 * (ahead // 3) + ahead % 3
                    act.wait_ge(c.landed[chunk % RING], i * 32 + 16 * (chunk // RING + 1))
                    st_round(f(c.hi(split), c.slot(chunk), ACT.Copy))
                act.wait_ge(proj.empty_sem[(u + 3) % RING], i * 3 + ((u + 3) // RING - 2))
                f(T(24 + 3 * n + g), proj.banks[:, u % RING, :], ACT.Sigmoid).then_inc(proj.empty_sem[u % RING], 1)

    with act.Fori(0, 3) as i:
        gate_tiles(i)
    gate_tiles(3, last=True)

    def post_norm(stage, r, y):
        for k in range(KD):
            act.wait_ge(*proj.filled((stage, k)))
            st.link(f(T(y + k), proj.bank((stage, k)), ACT.Copy))
            st.last(f(T(SQ0 + k), T(y + k), ACT.Square), proj.emptied((stage, k)))
        root(("ssy", r), T(RSTD), D)

    post_norm("ro", 0, 27)
    norm(10)
    u0 = proj.number[("upr", 0)]

    def relu_tiles(i, last=False):
        for j in range(4):
            u = u0 + j
            act.wait_ge(proj.full_sem, i * 4 + u + 1)
            if not (last and j >= 2):
                round_ahead("upr", i, j)
            act.wait_ge(s["mlp_mid"], i * 4 + j + 1)
            f(T(32 + j), proj.banks[:, u % RING, :], ACT.Relu).then_inc(proj.empty_sem[u % RING], 1)

    with act.Fori(0, F3T // 4 - 1) as i:
        relu_tiles(i)
    relu_tiles(F3T // 4 - 1, last=True)
    post_norm("dnr", 1, 32)


SPLIT_UP = {1: "up0", 2: "cu", 3: "up1", 4: "mqk", 5: "up2", 7: "up3", 10: "upr"}


R_CHUNKS = [(name, n) for name in ("rk", "rq", "rv", "fv", "ru", "rg") for n in range(splits_of(STAGE[name]))] + [("br", 0), ("br", 1)]


def chunk_floats(name, n):
    per = pieces(STAGE[name][3])
    return per[n % len(per)] * P


def split_use(c, split):
    name = [x for x in SPLIT if c.first_split[x] <= split][-1]
    n, per = split - c.first_split[name], len(pieces(STAGE[name][3]))
    earlier = sum({FT: 2 * KD}.get(STAGE[x][3], {"sv": 3, "mv": 6, "rv": 3, "fv": 3}.get(x, 0)) for x in SPLIT[:SPLIT.index(name)])
    if STAGE[name][1] == "tok":
        if n % 4 == 3:
            return c.proj.filled((name, n))
        return c.sem["w_used"], earlier + 3 * (n // 4) + n % 4 + 1
    if n % per == per - 1:
        return c.proj.filled((name, n // per))
    return c.sem["w_used"], earlier + 2 * (n // per) + n % per + 1


EH = (53, 44)
E_GLA = ((5, 6, 7, 8), (0, 1, 2, 3))
TABLES = ((43, SELF_W), (45, CTX_W), (41, CTX_W))



def vector_program(nc, dve, c):
    s, proj, mix, T, H, X, small = c.sem, c.proj, c.mix, c.T, c.H, c.X, c.small
    st = Steps(dve, s["dve_chain"])
    v = nc.vector

    def tt(out, a, b, op):
        return v.tensor_tensor(out, a, b, op)

    def ts(out, a, x, op0, y=None, op1=None):
        if op1 is None:
            return v.tensor_scalar(out, a, x, None, op0)
        return v.tensor_scalar(out, a, x, y, op0, op1)

    def stt(out, a, x, b, op0, op1):
        return v.scalar_tensor_tensor(out=out, in0=a, scalar=x, in1=b, op0=op0, op1=op1)

    def ada_row(row, cond, column):
        dve.wait_ge(*c.ada_has_landed(row))
        w = c.ada_slot(row)
        v.tensor_tensor_reduce(w, w, cond, 1.0, 0.0, ALU.mult, ALU.add, column).then_inc(s["ada_used"], 1)
        dve.wait_ge(s["ada_used"], row + 1)

    def ada_rows(first, n):
        for row in range(first, first + n):
            j = row + len(FIRST_ROWS)
            ada_row(row, c.cond[:, 0:D], c.mod[:, j:j + 1])

    def add_bias(layer, first, n, bias, at):
        cols = c.mod[:, 48 * layer + first:48 * layer + first + n]
        st.link(tt(cols, cols, c.v(bias, at + first, n), ALU.add))

    def gains(use, layer, part, w, at):
        st.done(stt(c.g(use, 0, 8), c.m(layer, part, 0, 8), 1.0, c.v(w, at, 8), ALU.add, ALU.mult), s["mod_ready"])

    def inverse(key, rt):
        dve.wait_ge(*mix.emptied(key))
        st.link(v.reciprocal(rt, rt))

    def norm(r):
        if r in SPLIT_UP:
            for n in range(SPLIT_RING):
                rest_chunk(SPLIT_UP[r], n)
        inverse(("ss", r), T(RSTD))
        for k in range(KD):
            if r in MODULATED:
                st.done(tt(H(k), X(k), T(RSTD), ALU.mult), s["xn_ready"])
            else:
                name, at = PLAIN[r]
                out = X(k) if r == 8 else H(k)
                ins = stt(out, X(k), c.v(name, at + k), T(RSTD), ALU.mult, ALU.mult)
                if r == 8:
                    st.done(ins, s["x_ready"])
                elif r in SPLIT_NORMS:
                    ins.then_inc(s["h_raw"], 1)
                else:
                    ins.then_inc(s["h_ready"], 1)
                    dve.wait_ge(s["h_ready"], h_count(r, k))
        if r in SPLIT_NORMS:
            for k in range(KD):
                dve.wait_ge(s["h_rounded"], 8 * SPLIT_NORMS.index(r) + k + 1)
                tt(c.norm_lo(r, k), H(k), c.norm_hi(r, k).bitcast(F32), ALU.subtract).then_inc(s["h_ready"], 1)
                dve.wait_ge(s["h_ready"], h_count(r, k))

    def rest_chunk(name, n):
        split, chunk = c.first_split[name] + n, c.first_chunk[name] + n
        w = chunk_floats(name, n)
        dve.wait_ge(s["w_rounded"], split + 1)
        tt(c.lo(split)[:, 0:w], c.slot(chunk)[:, 0:w], c.hi(split)[:, 0:w].bitcast(F32), ALU.subtract).then_inc(s["w_split"], 1)

    def rest_ahead(name, i, j):
        split, chunk = c.first_split[name] + j + SPLIT_RING, c.first_chunk[name] + j + SPLIT_RING
        dve.wait_ge(s["w_rounded"], i * 4 + (split + 1))
        tt(c.lo(split), c.slot(chunk), c.hi(split).bitcast(F32), ALU.subtract).then_inc(s["w_split"], 1)

    def split_mid(i, layer, p, raw):
        n = FT * layer + p + 1
        hi, lo = (t[:, bass.ds(i * (2 * S) + p * S, S)] for t in (c.mid_hi, c.mid_lo))
        v.tensor_copy(hi, raw).then_inc(s["mid_rounded"], 1)
        dve.wait_ge(s["mid_rounded"], i * 2 + n)
        tt(lo, raw, hi.bitcast(F32), ALU.subtract).then_inc(s["mid_ready"], 1)

    def residual(stage, gate=None, bias=None):
        for k in range(KD):
            key = (stage, k)
            if stage in SPLIT:
                for n in range(3 * k + 2, min(3 * k + 5, 3 * KD)):
                    rest_chunk(stage, n)
            dve.wait_ge(*proj.filled(key))
            if gate is not None:
                ins = stt(X(k), proj.bank(key), gate(k), X(k), ALU.mult, ALU.add)
            elif bias is not None:
                ins = stt(X(k), proj.bank(key), bias(k), X(k), ALU.add, ALU.add)
            else:
                ins = tt(X(k), proj.bank(key), X(k), ALU.add)
            st.last(ins, proj.emptied(key))

    def rotation_table(n):
        name, phase, out = ("q", "q", "i", "i")[n], (np.pi / 2, 0.0)[n % 2], T(10 + n)
        if n % 2 == 0:
            st.link(ts(T(32), T(30), c.const("freq_" + name), ALU.mult))
        st.link(ts(T(33), T(32), 1 / (2 * np.pi), ALU.mult, phase / (2 * np.pi), ALU.add))
        st.link(ts(T(33), T(33), ROUND, ALU.add, ROUND, ALU.subtract))
        st.link(stt(out, T(33), -TURN[0], T(32), ALU.mult, ALU.add))
        st.link(stt(out, T(33), -TURN[1], out, ALU.mult, ALU.add))
        st.link(stt(out, T(33), -TURN[2], out, ALU.mult, ALU.add))
        if phase:
            st.link(ts(out, out, phase, ALU.add))
        st.done(ts(out, out, 3.1415925, ALU.min, -3.1415925, ALU.max), s["pos_ready"])

    dve.wait_ge(s["cond_ready"], 1)
    for r, at in enumerate(FIRST_ROWS):
        dve.wait_ge(c.first_rows[r // 4], 16 * 4)
        if r in (4, 8):
            if r == 4:
                dve.wait_ge(s["constants"], 16 * 3)
                dve.wait_ge(s["setup"], 16 * 4)
                st.link(v.tensor_copy(T(30), T(31).bitcast(I32)))
            for n in (r // 2 - 2, r // 2 - 1):
                rotation_table(n)
        st.link(v.tensor_tensor_reduce(T(at, 2), T(at, 2), c.cond[:, 0:D], 1.0, 0.0, ALU.mult, ALU.add, c.mod[:, r:r + 1]))
    add_bias(0, 0, 16, "ada_b", 0)
    gains(0, 0, 1, "mix_norm", 0)
    norm(0)
    dve.wait_ge(s["trig_ready"], 4)
    for n, name in ((1, "q"), (3, "i")):
        st.link(ts(T(10 + n), T(10 + n), c.const("sign_" + name), ALU.mult))

    def rotate(key, dst, src, cos, sin, tmp, sem):
        dve.wait_ge(*mix.filled(key))
        st.last(tt(tmp, mix.bank(key), sin, ALU.mult), mix.emptied(key))
        st.link(tt(dst, src, cos, ALU.mult))
        st.done(tt(dst, dst, tmp, ALU.add), sem)

    for t in range(5):
        rotate(("rot_i", t), T(t), T(5 + t), T(12), T(13), T(31), s["iq_ready"])
        ada_rows(3 * t, 3)
    n = 0
    for b in range(1, NB):
        score, width = T(13 + b), P * (b + 1)
        if b == 1:
            dve.wait_ge(*proj.emptied(("iw", 3)))
        for h in range(8):
            rel, w = T(20 + n % 2), small[:, 8 + 8 * b + h:9 + 8 * b + h]
            dve.wait_ge(*mix.emptied(("idx", b, h)))
            if h == 0:
                st.link(ts(score[:, 0:P * b], rel[:, 0:P * b], w, ALU.mult))
                st.done(stt(score[:, P * b:width], rel[:, P * b:width], w, c.square("causal_neg"), ALU.mult, ALU.add), s["idx_used"])
            else:
                st.done(stt(score[:, 0:width], rel[:, 0:width], w, score[:, 0:width], ALU.mult, ALU.add), s["idx_used"])
            n += 1
    top8 = small[:, 120:128]
    for b in range(1, NB):
        score, width = T(13 + b)[:, 0:P * (b + 1)], P * (b + 1)
        for _ in range(TOPK // 8):
            st.link(v.max(top8, score))
            st.link(v.match_replace(score, top8, score, TAKEN))
        st.link(ts(T(16 + b)[:, 0:width], score, -2e38, ALU.is_gt, NEG, ALU.mult))
    ada_rows(15, 8)
    dve.wait_ge(s["gate_ready"], 1)
    for t in range(2):
        g, b, mid = T(54 + t), T(56 + t), T(12 + t)
        st.link(stt(g, g, 0.0, b, ALU.min, ALU.subtract))
        st.link(v.tensor_tensor_scan(b, c.const("reset"), g, 0.0, ALU.mult, ALU.add))
        bn = b.rearrange("p (n c) -> p n c", c=CHUNK)
        st.link(tt(mid.rearrange("p (n c) -> p n c", c=CHUNK), bn,
                   bn[:, :, CHUNK // 2 - 1:CHUNK // 2].broadcast_to([P, NCH, CHUNK]), ALU.subtract))
        st.done(tt(g.rearrange("p (n c) -> p n c", c=CHUNK), bn[:, :, CHUNK - 1:CHUNK].broadcast_to([P, NCH, CHUNK]),
                   bn, ALU.subtract), s["span_ready"])
    for h in range(4):
        st.link(v.memset(T(ATT[h]), 0.0))
    dve.wait_ge(*proj.emptied(("gk", 1)))
    for t in range(2):
        dve.wait_ge(s["decay_ready"], t + 1)
        e = [T(i) for i in E_GLA[t]]
        st.link(tt(T(12 + t), T(26 + t), e[0], ALU.mult))
        st.link(tt(T(54 + t), T(28 + t), e[1], ALU.mult))
        st.link(tt(T(28 + t), T(28 + t), e[2], ALU.mult))
        st.done(tt(T(26 + t), T(26 + t), e[3], ALU.mult), s["gla_ready"])
    for t in range(9):
        if t < 8:
            inverse(("stat_d", t), T(50 + t % 2))
            st.done(stt(T(38 + t), T(46 + t % 2), c.v("dsa_q_norm" if t < 4 else "dsa_k_norm"), T(50 + t % 2),
                        ALU.mult, ALU.mult), s["head_normed"])
        if t >= 1:
            rotate(("rot_d", t - 1), T(38 + t - 1), T(38 + t - 1), T(10), T(11), T(52), s["head_roped"])
            ada_rows(22 + t, 1)
    mask = c.square("gla").bitcast(I32).unsqueeze(1).broadcast_to([P, NB, P])
    for h in range(4):
        dve.wait_ge(*mix.filled(("att", h)))
        st.last(v.copy_predicated(T(ATT[h]).rearrange("p (n c) -> p n c", c=P), mask,
                                  mix.bank(("att", h)).rearrange("p (n c) -> p n c", c=P)), mix.emptied(("att", h)))
    for t in range(2):
        dve.wait_ge(*mix.filled(("kv", t, 1)))
        states = T(5 + 2 * t, 2)
        for n in range(NCH - 1):
            own = mix.bank(("kv", t, n % 2))[:, (n // 2) * P:(n // 2 + 1) * P]
            out = states[:, (n + 1) * P:(n + 2) * P]
            if n == 0:
                ins = v.tensor_copy(out, own)
            else:
                ins = stt(out, states[:, n * P:(n + 1) * P], small[:, 40 + 8 * t + n:41 + 8 * t + n], own, ALU.mult, ALU.add)
            st.done(ins, s["state_ready"])
        for e in range(2):
            dve.sem_inc(*mix_release(mix, ("kv", t, e)))
    for h in range(4):
        inverse(("stat_o", h), T(50 + h % 2))
        st.done(stt(T(52), T(46 + h % 2), c.v("gla_out_norm"), T(50 + h % 2), ALU.mult, ALU.mult), s["head_normed"])
        st.done(tt(H(h), T(52), T(22 + h), ALU.mult), s["mixed"])
    units = [(b, h) for b in range(NB) for h in range(4)]
    for n in range(len(units) + 1):
        if n < 16:
            b, h = units[n]
            width, z, o = P * (b + 1), T(n % 2), n % 2
            if n >= 2:
                dve.wait_ge(*mix.filled(("pT", *units[n - 2])))
            dve.wait_ge(*mix.filled(("qk", b, h)))
            sel = c.square("causal_neg") if b == 0 else T(16 + b)[:, 0:width]
            st.last(v.tensor_tensor_reduce(z[:, 0:width], mix.bank(("qk", b, h))[:, 0:width], sel, 1.0, -3e38, ALU.add, ALU.max,
                                           small[:, 60 + o:61 + o]), mix.emptied(("qk", b, h)))
            st.done(ts(small[:, 56 + o:57 + o], small[:, 60 + o:61 + o], -P ** -0.5, ALU.mult), s["max_ready"])
        if n >= 1:
            b, h = units[n - 1]
            o, width = (n - 1) % 2, P * (b + 1)
            dve.wait_ge(s["p_ready"], n)
            st.link(v.reciprocal(small[:, 62 + o:63 + o], small[:, 58 + o:59 + o]))
            st.done(ts(T(o)[:, 0:width], T(o)[:, 0:width], small[:, 62 + o:63 + o], ALU.mult), s["pn_ready"])
    ada_rows(31, 1)
    add_bias(0, 16, 32, "ada_b", 0)
    gains(1, 0, 4, "ffn_norm", 0)
    residual("abo", gate=lambda k: c.m(0, 2, k))

    def ada_in_loop(i, q, layer, ctx):
        row = 48 * layer + q - len(FIRST_ROWS)
        landed, n = c.ada_has_landed(row)
        dve.wait_ge(landed, i * 16 + n)
        w = c.ada_slot(row)
        if ctx:
            v.tensor_tensor_reduce(T(54, 2), w, c.cond[:, D:2 * D], 1.0, 0.0, ALU.mult, ALU.add, c.acc[:, 4 + q:5 + q]) \
                .then_inc(s["ada_first"], 1)
            dve.wait_ge(s["ada_first"], i * 4 + q + 1)
        v.tensor_tensor_reduce(w, w, c.cond[:, 0:D], 1.0, 0.0, ALU.mult, ALU.add, c.acc[:, q:q + 1]).then_inc(s["ada_used"], 1)
        dve.wait_ge(s["ada_used"], i * 4 + row + 1)

    def ada_columns(i, layer, ctx):
        done = 11 * (layer - 1)
        for n in range(2 if ctx else 1):
            to = 48 * layer if n == 0 else 3 * 48
            v.tensor_copy(c.mod[:, bass.ds(i * 4 + to, 4)], c.acc[:, 4 * n:4 * n + 4]).then_inc(s["ada_copied"], 1)
            dve.wait_ge(s["ada_copied"], i * (2 if ctx else 1) + done + n + 1)

    def swiglu(ffn, ctx):
        layer, up = ffn + 1, f"up{ffn}"
        u0 = proj.number[(up, 0)]
        with dve.Fori(0, 2 * FT // 4) as i:
            for j in range(4):
                u, p = u0 + j, j // 2
                ada_in_loop(i, j, layer, ctx)
                rest_ahead(up, i, j)
                if j % 2 == 1:
                    dve.wait_ge(proj.full_sem, i * 4 + u + 1)
                    dve.wait_ge(proj.empty_sem[(u - 1) % RING], i + (u - 1) // RING + 1)
                    raw = T(52 + p)
                    tt(raw, raw, proj.banks[:, u % RING, :], ALU.mult).then_inc(proj.empty_sem[u % RING], 1)
                    dve.wait_ge(proj.empty_sem[u % RING], i + u // RING + 1)
                    split_mid(i, ffn, p, raw)
            ada_columns(i, layer, ctx)
        for j in range(44, 48):
            row = 48 * layer + j - len(FIRST_ROWS)
            if ctx:
                dve.wait_ge(*c.ada_has_landed(row))
                st.link(v.tensor_tensor_reduce(T(54, 2), c.ada_slot(row), c.cond[:, D:2 * D], 1.0, 0.0, ALU.mult, ALU.add, c.mod[:, 3 * 48 + j:3 * 48 + j + 1]))
            ada_row(row, c.cond[:, 0:D], c.mod[:, 48 * layer + j:48 * layer + j + 1])

    norm(1)
    dve.sem_inc(s["mid_ready"], 2)
    swiglu(0, False)
    add_bias(1, 0, 48, "ada_b", 48)
    gains(2, 1, 1, "mix_norm", 8)
    gains(3, 1, 4, "ffn_norm", 8)
    residual("dn0", gate=lambda k: c.m(0, 5, k))
    norm(2)

    def rest_s(n):
        rest_chunk(("cu", "sq", "sk", "sv")[n // 4], n % 4)

    for g in range(4):
        rest_s(g + SPLIT_RING)
        dve.wait_ge(*proj.emptied(("cu", g)))
        src = T(g)
        for n in range(g + 1):
            sh, dst = 2 ** n, T(4 + n % 2)
            st.link(tt(dst[:, sh:S], src[:, sh:S], src[:, 0:S - sh], ALU.add))
            st.link(v.tensor_copy(dst[:, 0:sh], src[:, 0:sh]))
            src = dst
        st.link(tt(src[:, 0:16], src[:, 0:16], c.const("count")[:, 16 * g:16 * g + 16], ALU.mult))
        st.link(ts(src[:, 16:S], src[:, 16:S], 0.5 ** (g + 1), ALU.mult))
        st.done(tt(T(6 + g), src, T(g), ALU.subtract), s["pooled"])
    for t in range(8):
        rest_s(4 + t + SPLIT_RING)
        inverse(("stat_s", t), T(22 + t % 2))
        st.done(stt(T(10 + t), T(18 + t % 2), c.v("sb_q_norm" if t < 4 else "sb_k_norm"), T(22 + t % 2), ALU.mult, ALU.mult),
                s["head_normed"])
    for n in range(12 + SPLIT_RING, 16):
        rest_s(n)
    for h in range(5):
        if h < 4:
            z, sp = T(28 + 3 * (h % 2), 3)[:, 0:TRI[4]], T(34 + 3 * (h % 2), 3)[:, 0:TRI[4]]
            dve.wait_ge(s["z_ready"], h + 1)
            st.link(stt(sp, z, 0.0, sp, ALU.max, ALU.add))
            for j in range(NB - 1):
                w = slice(TRI[j], TRI[j] + P)
                st.link(tt(sp[:, w], sp[:, w], c.square("strict"), ALU.mult))
            w = slice(TRI[3], TRI[3] + P)
            st.done(tt(sp[:, w], sp[:, w], c.square("strict"), ALU.mult), s["sp_ready"])
            st.link(tt(z, z, sp, ALU.subtract))
            for j in range(NB):
                w = slice(TRI[j], TRI[j] + P)
                st.link(tt(z[:, w], z[:, w], c.square("strict_neg"), ALU.add))
        if h >= 1:
            z = T(28 + 3 * ((h - 1) % 2), 3)
            for j in range(NB):
                key = ("cum", h - 1, j)
                dve.wait_ge(*mix.filled(key))
                w = z[:, TRI[j]:TRI[j + 1]]
                st.last(tt(w, w, mix.bank(key)[:, 0:S - P * j], ALU.subtract), mix.emptied(key))
    residual("cdo", gate=lambda k: c.m(1, 2, k))
    norm(3)
    dve.wait_ge(s["cond_ready"], 2)
    swiglu(1, True)
    add_bias(2, 0, 48, "b_mod_3", 0)
    add_bias(3, 0, 48, "b_mod_3", 0)
    gains(6, 3, 1, "g_pre_mix_3", 0)
    gains(4, 2, 1, "g_pre_mix_3", 0)
    gains(5, 2, 4, "g_pre_mlp_3", 0)
    st.link(tt(c.g(7, 0, 8), c.m(2, 2, 0, 8), c.v("g_post_mix_3", 0, 8), ALU.mult))
    st.link(tt(c.g(8, 0, 8), c.m(2, 5, 0, 8), c.v("g_post_mlp_3", 0, 8), ALU.mult))
    residual("dn1", gate=lambda k: c.m(1, 5, k))
    norm(4)

    def rest_m(n):
        rest_chunk(("mqk", "mv", "mo")[n // 8], n % 8)

    for t in range(8):
        rest_m(t + SPLIT_RING)
        dve.wait_ge(s["conv_init"], t + 1)
        bank = proj.bank(("mqk", t))
        for back in (1, 2, 3):
            out = T(t)[:, back:S]
            ins = stt(out, bank[:, 0:S - back], c.v("m_conv_w_2", 8 * (3 - back) + t), out, ALU.mult, ALU.add)
            if back < 3:
                st.link(ins)
            else:
                st.last(ins, proj.emptied(("mqk", t)))
    r4 = lambda i: T(i)[0:4, :]
    for n in range(8 + SPLIT_RING, 24):
        rest_m(n)
    st.link(v.memset(r4(27), 1.0))
    dve.wait_ge(s["m_gate"], 1)
    st.link(stt(r4(25), r4(25), 0.0, r4(26), ALU.min, ALU.subtract))
    st.link(v.tensor_tensor_scan(r4(28), r4(27), r4(25), 0.0, ALU.mult, ALU.add))
    st.link(tt(r4(29), r4(24), r4(28), ALU.subtract))
    st.link(v.tensor_tensor_scan(r4(30), r4(29), r4(29), 0.0, ALU.max, ALU.max))
    st.link(ts(r4(31), r4(30), -1.0, ALU.mult))
    st.done(tt(r4(28), r4(28), r4(30), ALU.add), s["m_rows"])

    def decay_args(h):
        nm, e = T(32 + h % 2), T(EH[h % 2], 3)
        dve.wait_ge(*mix.emptied(("mbc", h, 1)))
        for j in range(NB):
            ins = ts(e[:, TRI[j]:TRI[j + 1]], nm[:, P * j:S], small[:, 64 + 4 * j + h:65 + 4 * j + h], ALU.add, 0.0, ALU.min)
            if j < NB - 1:
                st.link(ins)
            else:
                st.done(ins, s["e_arg"])

    decay_args(0)
    for h in range(4):
        e, p = T(EH[h % 2], 3), T(38 + 3 * (h % 2), 3)
        dve.wait_ge(s["e_ready"], h + 1)
        for j in range(NB):
            w = slice(TRI[j], TRI[j] + P)
            st.link(tt(e[:, w], e[:, w], c.square("before"), ALU.mult))
        for j in range(NB):
            key = ("ms", h, j)
            dve.wait_ge(*mix.filled(key))
            w = slice(TRI[j], TRI[j + 1])
            st.last(stt(p[:, w], mix.bank(key)[:, 0:S - P * j], P ** -0.5, e[:, w], ALU.mult, ALU.mult), mix.emptied(key))
        if h < 3:
            decay_args(h + 1)
        dve.wait_ge(*mix.emptied(("md", h)))
        st.link(tt(T(47), T(47), T(34 + h % 2), ALU.max))
        st.link(v.reciprocal(T(47), T(47)))
        for k in range(2):
            hm = T(48 + 2 * (h % 2) + k)
            st.done(tt(hm, mix.bank(("mn", h, k)), T(47), ALU.mult), s["hm_ready"])
            dve.sem_inc(*mix_release(mix, ("mn", h, k)))
        inverse(("stat_m", h), T(52))
        for k in range(2):
            hm = T(48 + 2 * (h % 2) + k)
            st.link(stt(hm, hm, c.v("m_head_norm_2", 2 * h + k), T(52), ALU.mult, ALU.mult))
            st.done(tt(H(2 * h + k), hm, T(16 + 2 * h + k), ALU.mult), s["mixed"])
    residual("mout")

    def conv_ffn(ffn):
        layer, up = ffn - 2, f"up{ffn}"
        u0 = proj.number[(up, 0)]
        w0 = VCOL["f_conv_w_2"] + 3 * 2 * FT * layer
        with dve.Fori(0, 2 * FT // 4) as i:
            for p in range(2):
                for g in range(2):
                    u, a = u0 + 2 * p + g, T(52 + 2 * p + g)
                    rest_ahead(up, i, 2 * p + g)
                    dve.wait_ge(s["conv_init"], i * 4 + (8 + 2 * FT * layer + 2 * p + g + 1))
                    for back in (1, 2):
                        col = w0 + 2 * FT * (2 - back) + FT * g + p
                        ins = stt(a[:, back:S], proj.banks[:, u % RING, 0:S - back], c.vec[:, bass.ds(i * 2 + col, 1)],
                                  a[:, back:S], ALU.mult, ALU.add)
                        if back == 1:
                            ins.then_inc(s["convolved"], 1)
                            dve.wait_ge(s["convolved"], i * 4 + (CONVOLVED[layer] + 2 * p + g + 1))
                        else:
                            ins.then_inc(proj.empty_sem[u % RING], 1)
                            dve.wait_ge(proj.empty_sem[u % RING], i + u // RING + 1)
                dve.wait_ge(s["conv_act"], i * 2 + (8 + FT * layer + p + 1))
                raw = T(52 + 2 * p)
                tt(raw, raw, T(53 + 2 * p), ALU.mult).then_inc(s["mid_raw"], 1)
                dve.wait_ge(s["mid_raw"], i * 2 + (FT * layer + p + 1))
                split_mid(i, ffn, p, raw)

    norm(5)
    conv_ffn(2)
    residual("dn2")
    norm(6)
    pad = S + CONV - 1
    u_all = T(0, 9)[:, 0:KD * pad]
    st.link(v.memset(u_all.rearrange("p (k t) -> p k t", k=KD)[:, :, 0:CONV - 1], 0.0))
    for t in range(KD):
        key = ("ca", 2 * t)
        u = u_all[:, t * pad:(t + 1) * pad]
        dve.wait_ge(*proj.emptied(("ca", 2 * t + 1)))
        st.last(stt(u[:, CONV - 1:pad], proj.bank(key), c.v("c_b_in_2", t), T(9 + t % 2), ALU.add, ALU.mult), proj.emptied(key))
        acc = T(11 + t)
        st.link(ts(acc, u[:, 0:S], c.v("c_dw_w_2", t), ALU.mult, c.v("c_dw_b_2", t), ALU.add))
        for k in range(1, CONV):
            ins = stt(acc, u[:, k:k + S], c.v("c_dw_w_2", 8 * k + t), acc, ALU.mult, ALU.add)
            if k < CONV - 1:
                st.link(ins)
            else:
                ins.then_inc(s["u_ready"], 1)
                dve.wait_ge(s["u_ready"], t + 1)
    dve.wait_ge(*mix.filled(("lnm", 0)))
    st.last(ts(T(RSTD), mix.bank(("lnm", 0)), 1 / D, ALU.mult), mix.emptied(("lnm", 0)))
    for k in range(KD):
        st.done(tt(T(11 + k), T(11 + k), T(RSTD), ALU.subtract), s["u_centred"])
    inverse(("lnv", 0), T(RSTD))
    for k in range(KD):
        st.done(tt(T(11 + k), T(11 + k), T(RSTD), ALU.mult), s["u_normed"])
    residual("cout", bias=lambda k: c.v("c_b_out_2", k))
    norm(7)
    conv_ffn(3)
    residual("dn3")
    norm(8)
    inverse(("ssc", 0), T(12)[:, 0:CTX])
    for k in range(KD):
        w = slice(k * CTX, (k + 1) * CTX)
        st.done(tt(T(28, 4)[:, w], T(24, 4)[:, w], T(12)[:, 0:CTX], ALU.mult), s["u_centred"])
    e, l, y, t8 = small[:, 80:88], small[:, 88:96], small[:, 128:136], small[:, 136:144]
    dve.wait_ge(s["lg_abs"], 1)
    st.link(ts(y, e, 1.0, ALU.add))
    st.link(ts(t8, y, -1.0, ALU.add))
    st.link(tt(t8, e, t8, ALU.subtract))
    st.link(v.reciprocal(y, y))
    st.link(tt(t8, t8, y, ALU.mult))
    st.link(tt(l, l, t8, ALU.add))
    st.link(stt(l, small[:, 0:8], 0.0, l, ALU.min, ALU.subtract))
    norm(9)

    def rest_r(n):
        rest_chunk(*R_CHUNKS[n])

    for n in range(SPLIT_RING):
        rest_r(n)
    for t in range(8):
        rest_r(t + SPLIT_RING)
        rotate(("rot_r", t), T(16 + t), T(24 + t % 2), T(41), T(42), T(26), s["head_roped"])
    for n in range(8 + SPLIT_RING, 16 + SPLIT_RING):
        rest_r(n)
    dve.wait_ge(*proj.emptied(("fv", 3)))
    vs = T(33, 2).rearrange("p (g c) -> p g c", c=64)
    st.link(tt(T(41, 2), T(33, 2), T(33, 2), ALU.mult))
    st.done(v.tensor_reduce(small[:, 96:112], T(41, 2).rearrange("p (g c) -> p g c", c=64), AX.X, ALU.add), s["vs_var"])
    for n in range(16 + SPLIT_RING, 22 + SPLIT_RING):
        rest_r(n)
    dve.wait_ge(s["vs_std"], 1)
    st.link(v.reciprocal(small[:, 96:112], small[:, 96:112]))
    st.link(tt(vs, vs, small[:, 96:112].unsqueeze(2).broadcast_to([P, 16, 64]), ALU.mult))
    dve.wait_ge(s["late"], 16 * 2)
    vb = T(33, 2).rearrange("p (n c) -> p n c", c=256)
    st.done(tt(vb, vb, c.sgu_norm[:, :].unsqueeze(1).broadcast_to([P, NB, 256]), ALU.mult), s["vs_ready"])
    dist = T(47, 6)
    for h in range(4):
        fwd, bwd = small[:, 88 + h:89 + h], small[:, 92 + h:93 + h]
        if h == 0:
            dve.wait_ge(*proj.emptied(("rg", 3)))
        own, before, after = (T(at, 2)[:, 0:width] for at, width in TABLES)
        st.link(ts(own, dist[:, 0:SELF_W], fwd, ALU.mult))
        st.done(stt(own, dist[:, SELF_W:2 * SELF_W], bwd, own, ALU.mult, ALU.add), s["table_arg"])
        st.done(ts(before, dist[:, 2 * SELF_W:2 * SELF_W + CTX_W], fwd, ALU.mult), s["table_arg"])
        st.done(ts(after, dist[:, 2 * SELF_W + CTX_W:6 * S], bwd, ALU.mult), s["table_arg"])
        dve.wait_ge(s["table_ready"], 3 * (h + 1))
        st.link(tt(before, before, after, ALU.add))
        for j in range(6):
            key = ("rs", h, j)
            dve.wait_ge(*mix.filled(key))
            w = own[:, 384 - P * j:896 - P * j] if j < 4 else before[:, P * (5 - j):P * (5 - j) + S]
            st.last(tt(T(RP[j]), mix.bank(key), w, ALU.mult), mix.emptied(key))
        inverse(("stat_r", h), c.late_tile(1))
        st.link(tt(T(57), T(57), c.late_tile(1), ALU.mult))
        st.done(tt(T(8 + h), T(57), T(37 + h), ALU.mult), s["mixed"])
    dve.wait_ge(s["dft_loaded"], 48)
    for t in range(2):
        key = ("sgu", t)
        dve.wait_ge(*mix.filled(key))
        for g in range(2):
            r = slice(64 * g, 64 * g + 64)
            bias = c.sgu_b[r, (2 * t + g) * P:(2 * t + g + 1) * P].unsqueeze(1).broadcast_to([64, NB, P])
            out = c.late_tile(4 + t)[r, :].rearrange("p (n c) -> p n c", c=P)
            ins = tt(out, mix.bank(key)[r, :].rearrange("p (n c) -> p n c", c=P), bias, ALU.add)
            if g == 0:
                st.link(ins)
            else:
                st.last(ins, mix.emptied(key))
        st.done(tt(c.late_tile(4 + t), c.late_tile(4 + t), T(35 + t), ALU.mult), s["sgu_ready"])
    u0 = proj.number[("br", 0)]

    def branch_tiles(i, last=False):
        for n in range(2):
            out = c.pool[:, bass.ds(i * (2 * S) + (16 + n) * S, S)]
            for g in range(3):
                ahead = 3 * n + g + SPLIT_RING
                if not (last and ahead >= 6):
                    split, chunk = c.first_split["br"] + ahead, c.first_chunk["br"] + 4 * (ahead // 3) + ahead % 3
                    dve.wait_ge(s["w_rounded"], i * 6 + (split + 1))
                    tt(c.lo(split), c.slot(chunk), c.hi(split).bitcast(F32), ALU.subtract).then_inc(s["w_split"], 1)
            for g in range(3):
                u = u0 + 6 * n + 3 + g
                dve.wait_ge(proj.full_sem, i * 12 + u + 1)
                dve.wait_ge(proj.empty_sem[(u - 3) % RING], i * 3 + ((u - 3) // RING + 1))
                dst = out if g == 0 else T(30)
                tt(dst, proj.banks[:, u % RING, :], T(24 + 3 * n + g), ALU.mult).then_inc(proj.empty_sem[u % RING], 1)
                dve.wait_ge(proj.empty_sem[u % RING], i * 3 + (u // RING + 1))
                if g > 0:
                    sem, m = (s["pr_ready"], 1) if g == 1 else (s["merged"], 1)
                    tt(out, out, T(30), ALU.add).then_inc(sem, 1)
                    dve.wait_ge(sem, i * 2 + (n + 1))

    with dve.Fori(0, 3) as i:
        branch_tiles(i)
    branch_tiles(3, last=True)

    def post_norm(stage, r, y, gain, sem):
        inverse(("ssy", r), T(RSTD))
        for k in range(KD):
            st.link(stt(T(y + k), T(y + k), c.g(gain, k), T(RSTD), ALU.mult, ALU.mult))
            st.done(tt(X(k), X(k), T(y + k), ALU.add), sem)

    post_norm("ro", 0, 27, 7, s["x_ready"])
    norm(10)
    dve.sem_inc(s["mlp_mid"], 4)
    u0 = proj.number[("upr", 0)]

    def square_tiles(i, last=False):
        for j in range(4):
            u = u0 + j
            if not (last and j >= 2):
                rest_ahead("upr", i, j)
            dve.wait_ge(proj.empty_sem[u % RING], i + (u // RING + 1))
            tt(c.pool[:, bass.ds(i * (4 * S) + j * S, S)], T(32 + j), T(32 + j), ALU.mult).then_inc(s["mlp_mid"], 1)

    with dve.Fori(0, F3T // 4 - 1) as i:
        square_tiles(i)
    square_tiles(F3T // 4 - 1, last=True)
    post_norm("dnr", 1, 32, 8, s["out_ready"])


def mix_release(mix, key):
    sem, _ = mix.emptied(key)
    return sem, 1


ROUND = 1.5 * 2 ** 23
TURN = (6.28125, 0.0019354820251464844, -1.7484555314695172e-07)
CONVOLVED = (0, 2 * FT)



def build(nc, dram):
    with ExitStack() as ctx:
        c = Chip(nc, ctx, dram)
        block = ctx.enter_context(nc.Block())

        @block.sync
        def _(sp):
            sync_program(nc, sp, c)

        @block.gpsimd
        def _(pool):
            gpsimd_program(nc, pool, c)

        @block.tensor
        def _(pe):
            tensor_program(nc, pe, c)

        @block.scalar
        def _(act):
            scalar_program(nc, act, c)

        @block.vector
        def _(dve):
            vector_program(nc, dve, c)


def columns(w, kt):
    parts = [kt] if kt == FT else pieces(kt)
    n = w.shape[1] // P
    a = w.reshape(len(parts), parts[0], P, n, P).transpose(3, 0, 2, 1, 4)
    return np.ascontiguousarray(a.reshape(n * len(parts), P, parts[0] * P))


def rows(w):
    m = w.shape[1] // S
    a = w.reshape(4, 2, P, m, S).transpose(3, 0, 2, 1, 4)
    return np.ascontiguousarray(a.reshape(4 * m, P, 2 * S))


def paired(w):
    k, n = w.shape
    return w.reshape(k, 2, n // (2 * P), P).transpose(0, 2, 1, 3).reshape(k, n)


def lay_out(a):
    f = {k: np.asarray(x) for k, x in a.items()}
    ab, cd, mw, w3 = f["ab_w_in"][0], f["cd_w_in"][0], f["m_w_in_2"][0], f["w_in_3"][0]
    col = lambda w, lo, hi, kt=8: columns(np.ascontiguousarray(w[:, lo:hi]), kt)
    row = lambda w, lo, hi: rows(np.ascontiguousarray(w[:, lo:hi]))
    w = {
        "iq": col(ab, 3088, 3600), "ik": columns(np.concatenate([ab[:, 3600:3664]] * 2, 1), 8), "gr": col(ab, 1040, 1552),
        "gq": col(ab, 0, 256), "gk": col(ab, 256, 512), "gv": row(ab, 512, 1024), "dv": row(ab, 2576, 3088),
        "dq": col(ab, 1552, 2064), "dk": col(ab, 2064, 2576), "abo": columns(f["ab_w_out"][0], 8),
        "cu": col(cd, 0, 512), "sq": col(cd, 512, 1024), "sk": col(cd, 1024, 1536), "sv": row(cd, 1536, 2048),
        "cdo": columns(f["cd_w_out"][0], 8),
        "mqk": col(mw, 0, 1024), "mv": row(mw, 1024, 2048), "mo": col(mw, 2048, 3072), "mout": columns(f["m_w_out_2"][0], 8),
        "ca": columns(paired(f["c_w_in_2"][0]), 8), "cout": columns(f["c_w_out_2"][0], 8),
        "ck": col(w3, 512, 1024), "cv": row(w3, 1024, 1536), "rk": col(w3, 512, 1024), "rq": col(w3, 0, 512),
        "rv": row(w3, 1024, 1536), "fv": rows(np.concatenate([w3[:, 2048:2304], w3[:, 2560:2816]], 1)),
        "ru": col(w3, 2304, 2560), "rg": col(w3, 1536, 2048), "ro": columns(f["w_out_3"][0], 8),
        "upr": columns(f["w_up_3"][0], 8), "dnr": columns(f["w_down_3"][0], 32),
    }
    for layer in range(2):
        w[f"up{layer}"] = columns(paired(f["ffn_w1"][layer]), 8)
        w[f"dn{layer}"] = columns(f["ffn_w2"][layer], FT)
        w[f"up{layer + 2}"] = columns(paired(f["f_w_up_2"][layer]), 8)
        w[f"dn{layer + 2}"] = columns(f["f_w_down_2"][layer], FT)
    gates = [w3[:, 2816 + D * g:2816 + D * (g + 1)] for g in range(3)]
    branch = np.concatenate([f["w_branch_a_3"][0], f["w_branch_b_3"][0], f["w_branch_c_3"][0]], 0)
    parts = [columns(np.ascontiguousarray(m), 8) for m in (*gates, branch)]
    w["br"] = np.stack(parts, 1).reshape(32, P, D)
    small = np.concatenate([ab[:, 1024:1040], ab[:, 3664:3672], mw[:, 3072:3080]], 1)
    out = {f"w_{k}": x for k, x in w.items()}
    out["w_small"] = np.ascontiguousarray(small.reshape(KD, P, 32).transpose(1, 0, 2).reshape(P, KD * 32))
    out["ada"] = np.concatenate([m.T for m in (f["ada_w"][0], f["ada_w"][1], f["w_mod_3"][0])], 0).reshape(144, P, D)
    out["x"] = np.ascontiguousarray(f["x"][0].T)
    out["ctx"] = np.ascontiguousarray(f["ctx_3"][0].T)
    out["vectors"] = np.ascontiguousarray(np.concatenate([f[n].reshape(-1, P).T for n, _ in VECTORS], 1))
    out["squares"] = np.concatenate(list(square_constants().values()), 1)
    out["others"] = np.concatenate([x.astype(np.float32) for x in other_constants().values()], 1)
    out.update({k: x.astype(np.float32) for k, x in late_constants().items()})
    out["c"], out["c_3"], out["c_ctx_3"] = f["c"][0], f["c_3"][0], f["c_ctx_3"]
    out["positions"] = f["positions"][0]
    out["gla_gate_up"] = f["gla_gate_up"][0]
    out["m_bias"] = np.ascontiguousarray(f["m_b_gates_2"][0].reshape(2, 4).T)
    out["pool_w"] = np.ascontiguousarray(f["pool_w"][0].transpose(1, 0, 2).reshape(P, 4 * P))
    out["sgu_w"] = np.ascontiguousarray(f["sgu_w_s_3"][0].transpose(2, 0, 1).reshape(P, 4 * P))
    out["sgu_norm"], out["sgu_b"] = f["sgu_norm_3"][0], f["sgu_b_s_3"][0].reshape(-1)
    out["decay"] = f["ret_decay_logit_3"][0].reshape(-1)
    return out


def kernel(**inputs):
    import concourse.bacc as bacc
    from concourse.bass_utils import run_bass_kernel_spmd

    nc = bacc.Bacc("TRN2", target_bir_lowering=False, num_devices=1, dynamic_dma_scratch_size=4096)
    arrays = lay_out(inputs)
    dram = {n: nc.dram_tensor(f"in_{n}", a.shape, mybir.dt.from_np(a.dtype), kind="ExternalInput").ap() for n, a in arrays.items()}
    dram["out"] = nc.dram_tensor("out", (D, S), F32, kind="ExternalOutput").ap()
    build(nc, dram)
    r = run_bass_kernel_spmd(nc, [{f"in_{n}": a for n, a in arrays.items()}], core_ids=[0])
    return np.ascontiguousarray(r.results[0]["out"].T)[None]
```
